# Optimizing a Trainium2 kernel written in Bass

```python
import jax, jax.numpy as jnp
from jax import lax
import numpy as np

D_MODEL = 1024
BATCH = 1
SEQ = 128
DEPTH = 2
DEC_BATCH = 1
DEC_SEQ = 256
PAST_LEN = 128

GRID_W = 64
CONV_DIM = 256
CONV_WIDTH = 3
NA_HEADS = 4
NA_HEAD_DIM = 64
NA_DIM = NA_HEADS * NA_HEAD_DIM
NA_WIN_ROWS = 8
NA_WIN_COLS = 16
ML_HEADS = 4
ML_HEAD_DIM = 128
ML_DIM = ML_HEADS * ML_HEAD_DIM
ML_CHUNK = 64
N_DIRS = 2
N_GROUPS = 4
EXPERTS_PER_GROUP = 4
N_EXPERTS = N_GROUPS * EXPERTS_PER_GROUP
TOP_K = 2
EXPERT_FF = 512
ROPE_BASE = 10000.0
ATTN_BLOCK = 128
EPS = 1e-6
N_MOD = 6
SPLIT_POINTS = (CONV_DIM, 2 * CONV_DIM, 3 * CONV_DIM,
                3 * CONV_DIM + NA_DIM, 3 * CONV_DIM + 2 * NA_DIM, 3 * CONV_DIM + 3 * NA_DIM,
                3 * CONV_DIM + 3 * NA_DIM + ML_DIM, 3 * CONV_DIM + 3 * NA_DIM + 2 * ML_DIM,
                3 * CONV_DIM + 3 * NA_DIM + 3 * ML_DIM, 3 * CONV_DIM + 3 * NA_DIM + 4 * ML_DIM)
IN_COLS = 3 * CONV_DIM + 3 * NA_DIM + 4 * ML_DIM + 2 * N_DIRS * ML_HEADS
MIX_DIM = CONV_DIM + NA_DIM + ML_DIM

kernel_name = 'hybrid_diffusion_prefix_step'

F32 = jnp.float32

def rmsnorm(x, g):
    xf = x.astype(F32)
    y = xf * lax.rsqrt(jnp.mean(xf * xf, axis=-1, keepdims=True) + EPS)
    return (y * g.astype(F32)).astype(x.dtype)

def adaln_params(cvec, w_mod, b_mod):
    m = jax.nn.silu(cvec) @ w_mod + b_mod
    m = jnp.moveaxis(m.reshape(*cvec.shape[:-1], N_MOD, D_MODEL), -2, 0)
    return m[..., None, :]

def project(h, w_in, ml_gate_b):
    B, T, _ = h.shape
    z = h @ w_in
    cb, cc, ch, nq, nk, nv, mq, mk, mv, mo, mg = jnp.split(z, SPLIT_POINTS, axis=-1)
    na = tuple(a.reshape(B, T, NA_HEADS, NA_HEAD_DIM) for a in (nq, nk, nv))
    ml = tuple(a.reshape(B, T, ML_HEADS, ML_HEAD_DIM) for a in (mq, mk, mv))
    gates = mg.astype(F32).reshape(B, T, 2, N_DIRS, ML_HEADS) + ml_gate_b.astype(F32)
    return (cb, cc, ch), na, ml, mo, gates[:, :, 0], gates[:, :, 1]

def short_conv(u, w):
    return lax.conv_general_dilated(u, w.astype(u.dtype)[:, None, :], window_strides=(1,),
                                    padding=((CONV_WIDTH // 2, CONV_WIDTH // 2),),
                                    dimension_numbers=('NWC', 'WIO', 'NWC'),
                                    feature_group_count=u.shape[-1])

def axial_rope(x):
    B, T, H, Dh = x.shape
    t = jnp.arange(T)
    pos = jnp.stack([t // GRID_W, t % GRID_W], axis=-1).astype(F32)
    nf = Dh // 4
    inv = ROPE_BASE ** (-jnp.arange(nf, dtype=F32) / nf)
    ang = pos[:, :, None] * inv
    cos = jnp.cos(ang)[None, :, None].astype(x.dtype)
    sin = jnp.sin(ang)[None, :, None].astype(x.dtype)
    xr = x.reshape(B, T, H, 2, 2, nf)
    x1, x2 = xr[..., 0, :], xr[..., 1, :]
    out = jnp.stack([x1 * cos - x2 * sin, x1 * sin + x2 * cos], axis=-2)
    return out.reshape(B, T, H, Dh)

def context_attention(q, k, v):
    B, L, H, Dh = q.shape
    nb = L // ATTN_BLOCK
    qb = q.reshape(B, nb, ATTN_BLOCK, H, Dh).transpose(1, 0, 2, 3, 4)
    scale = Dh ** -0.5

    def block(qi):
        s = jnp.einsum('bqhd,bkhd->bhqk', qi, k).astype(F32) * scale
        p = jax.nn.softmax(s, axis=-1).astype(v.dtype)
        return jnp.einsum('bhqk,bkhd->bqhd', p, v)

    o = lax.map(block, qb)
    return o.transpose(1, 0, 2, 3, 4).reshape(B, L, H, Dh)

def neighbourhood_attention(q, k, v, k_ctx, v_ctx, rpb):
    B, T, H, Dh = q.shape
    rows = T // GRID_W
    kr = min(NA_WIN_ROWS, rows)
    kc = NA_WIN_COLS
    scale = Dh ** -0.5
    kg = k.reshape(B, rows, GRID_W, H, Dh)
    vg = v.reshape(B, rows, GRID_W, H, Dh)
    qg = q.reshape(B, rows, GRID_W, H, Dh).transpose(1, 0, 2, 3, 4)
    cols = jnp.arange(GRID_W)
    col_start = jnp.clip(cols - kc // 2, 0, GRID_W - kc)
    col_mask = (cols[None, :] >= col_start[:, None]) & (cols[None, :] < col_start[:, None] + kc)
    col_idx = jnp.clip(cols[None, :] - cols[:, None] + NA_WIN_COLS - 1, 0, 2 * NA_WIN_COLS - 2)
    r_idx = jnp.arange(rows)
    row_start = jnp.clip(r_idx - kr // 2, 0, rows - kr)

    def row_block(args):
        r, start, q_r = args
        k_blk = lax.dynamic_slice_in_dim(kg, start, kr, axis=1)
        v_blk = lax.dynamic_slice_in_dim(vg, start, kr, axis=1)
        row_off = start + jnp.arange(kr) - r + NA_WIN_ROWS - 1
        bias = rpb[:, row_off[None, :, None], col_idx[:, None, :]].astype(F32)
        s_loc = jnp.einsum('bqhd,bkwhd->bhqkw', q_r, k_blk).astype(F32) * scale + bias[None]
        s_loc = jnp.where(col_mask[:, None, :], s_loc, -jnp.inf).reshape(B, H, GRID_W, kr * GRID_W)
        s_ctx = jnp.einsum('bqhd,bchd->bhqc', q_r, k_ctx).astype(F32) * scale
        p = jax.nn.softmax(jnp.concatenate([s_loc, s_ctx], axis=-1), axis=-1).astype(v.dtype)
        p_loc = p[..., :kr * GRID_W].reshape(B, H, GRID_W, kr, GRID_W)
        p_ctx = p[..., kr * GRID_W:]
        return (jnp.einsum('bhqkw,bkwhd->bqhd', p_loc, v_blk)
                + jnp.einsum('bhqc,bchd->bqhd', p_ctx, v_ctx))

    o = lax.map(row_block, (r_idx, row_start, qg))
    return o.transpose(1, 0, 2, 3, 4).reshape(B, T, H, Dh)

def mlstm_chunkwise(q, k, v, log_i, log_f, C0, n0, m0):
    B, H, T, Dh = q.shape
    L = ML_CHUNK
    nc = T // L

    def to_chunks(a):
        return jnp.moveaxis(a.reshape(B, H, nc, L, *a.shape[3:]), 2, 0)

    causal = jnp.tril(jnp.ones((L, L), dtype=bool))

    def step(carry, xs):
        C, n, m = carry
        qc, kc, vc, li, lf = xs
        b = jnp.cumsum(lf, axis=-1)
        d = jnp.where(causal, b[..., :, None] - b[..., None, :] + li[..., None, :], -jnp.inf)
        inter = b + m[..., None]
        m_t = jnp.maximum(inter, d.max(axis=-1))
        w = jnp.exp(d - m_t[..., None])
        a = jnp.exp(inter - m_t)
        s = jnp.einsum('bhtd,bhsd->bhts', qc, kc) * w
        num = a[..., None] * jnp.einsum('bhtd,bhde->bhte', qc, C) + jnp.einsum('bhts,bhse->bhte', s, vc)
        den = a * jnp.einsum('bhtd,bhd->bht', qc, n) + s.sum(axis=-1)
        h = num / jnp.maximum(jnp.abs(den), jnp.exp(-m_t))[..., None]
        b_last = b[..., -1]
        g = b_last[..., None] - b + li
        m_new = jnp.maximum(b_last + m, g.max(axis=-1))
        a_s = jnp.exp(b_last + m - m_new)
        w_s = jnp.exp(g - m_new[..., None])
        C_new = a_s[..., None, None] * C + jnp.einsum('bhs,bhsd,bhse->bhde', w_s, kc, vc)
        n_new = a_s[..., None] * n + jnp.einsum('bhs,bhsd->bhd', w_s, kc)
        return (C_new, n_new, m_new), h

    (C, n, m), hs = lax.scan(step, (C0, n0, m0),
                             (to_chunks(q), to_chunks(k), to_chunks(v), to_chunks(log_i), to_chunks(log_f)))
    return jnp.moveaxis(hs, 0, 2).reshape(B, H, T, Dh), C, n, m

def mlstm_bidir(q, k, v, i_pre, f_pre, C0, n0, m0):
    out_dtype = q.dtype
    qf = jnp.moveaxis(q, 2, 1).astype(F32)
    kf = jnp.moveaxis(k, 2, 1).astype(F32) * (ML_HEAD_DIM ** -0.5)
    vf = jnp.moveaxis(v, 2, 1).astype(F32)
    log_i = jnp.moveaxis(i_pre, 1, -1)
    log_f = jax.nn.log_sigmoid(jnp.moveaxis(f_pre, 1, -1))
    C0, n0, m0 = C0.astype(F32), n0.astype(F32), m0.astype(F32)
    flip = lambda a: jnp.flip(a, axis=2)
    h_f, C_f, n_f, m_f = mlstm_chunkwise(qf, kf, vf, log_i[:, 0], log_f[:, 0], C0[:, 0], n0[:, 0], m0[:, 0])
    h_b, C_b, n_b, m_b = mlstm_chunkwise(flip(qf), flip(kf), flip(vf), flip(log_i[:, 1]), flip(log_f[:, 1]),
                                         C0[:, 1], n0[:, 1], m0[:, 1])
    h = jnp.moveaxis(h_f + flip(h_b), 1, 2)
    C = jnp.stack([C_f, C_b], axis=1).astype(out_dtype)
    n = jnp.stack([n_f, n_b], axis=1).astype(out_dtype)
    m = jnp.stack([m_f, m_b], axis=1).astype(out_dtype)
    return h, C, n, m

def mlstm_readout(h, mo, g):
    B, T = h.shape[:2]
    hf = h.astype(F32)
    hn = hf * lax.rsqrt(jnp.mean(hf * hf, axis=-1, keepdims=True) + EPS)
    return (hn.reshape(B, T, ML_DIM) * g.astype(F32) * jax.nn.sigmoid(mo.astype(F32))).astype(mo.dtype)

def merge(conv_o, na_o, ml_o, w_out):
    B, T, _ = conv_o.shape
    return jnp.concatenate([conv_o, na_o.reshape(B, T, NA_DIM), ml_o], axis=-1) @ w_out

def hier_moe(h, w_rg, b_rg, w_re, b_re, w_gate, w_up, w_down):
    shp = h.shape
    x = h.reshape(-1, D_MODEL)
    N = x.shape[0]
    tok = jnp.arange(N)
    gl = (x @ w_rg).astype(F32) + b_rg.astype(F32)
    gp = jax.nn.softmax(gl, axis=-1)
    g_top = jnp.argmax(gl, axis=-1)
    el = ((x @ w_re).astype(F32) + b_re.astype(F32)).reshape(N, N_GROUPS, EXPERTS_PER_GROUP)
    top_v, top_i = lax.top_k(el[tok, g_top], TOP_K)
    w = jax.nn.softmax(top_v, axis=-1) * gp[tok, g_top][:, None]
    eid = g_top[:, None] * EXPERTS_PER_GROUP + top_i
    gates = jnp.sum(jax.nn.one_hot(eid, N_EXPERTS, dtype=F32) * w[..., None], axis=1)
    a = jax.nn.silu(jnp.einsum('nd,edf->nef', x, w_gate)) * jnp.einsum('nd,edf->nef', x, w_up)
    y = jnp.einsum('nef,efd->nd', a * gates[..., None].astype(a.dtype), w_down)
    return y.reshape(shp)

def context_layer(x, mods, ln1_g, w_in, conv_w, ml_gate_b, ml_norm_g, w_out, ln2_g,
                  w_rg, b_rg, w_re, b_re, w_gate, w_up, w_down):
    sh1, sc1, g1, sh2, sc2, g2 = mods
    B = x.shape[0]
    h = rmsnorm(x, ln1_g) * (1 + sc1) + sh1
    (cb, cc, ch), (nq, nk, nv), (mq, mk, mv), mo, ig, fg = project(h, w_in, ml_gate_b)
    conv_o = cb * short_conv(cc * ch, conv_w)
    na_o = context_attention(nq, nk, nv)
    C0 = jnp.zeros((B, N_DIRS, ML_HEADS, ML_HEAD_DIM, ML_HEAD_DIM), F32)
    n0 = jnp.zeros((B, N_DIRS, ML_HEADS, ML_HEAD_DIM), F32)
    m0 = jnp.zeros((B, N_DIRS, ML_HEADS), F32)
    ml_h, C, n, m = mlstm_bidir(mq, mk, mv, ig, fg, C0, n0, m0)
    ml_o = mlstm_readout(ml_h, mo, ml_norm_g)
    x = x + g1 * merge(conv_o, na_o, ml_o, w_out)
    h2 = rmsnorm(x, ln2_g) * (1 + sc2) + sh2
    x = x + g2 * hier_moe(h2, w_rg, b_rg, w_re, b_re, w_gate, w_up, w_down)
    return x, nk, nv, C, n, m

def latent_layer(x, mods, k_ctx, v_ctx, C0, n0, m0, ln1_g, w_in, conv_w, na_rpb, ml_gate_b, ml_norm_g,
                 w_out, ln2_g, w_rg, b_rg, w_re, b_re, w_gate, w_up, w_down):
    sh1, sc1, g1, sh2, sc2, g2 = mods
    h = rmsnorm(x, ln1_g) * (1 + sc1) + sh1
    (cb, cc, ch), (nq, nk, nv), (mq, mk, mv), mo, ig, fg = project(h, w_in, ml_gate_b)
    conv_o = cb * short_conv(cc * ch, conv_w)
    na_o = neighbourhood_attention(nq, nk, nv, k_ctx, v_ctx, na_rpb)
    ml_h, _, _, _ = mlstm_bidir(axial_rope(mq), axial_rope(mk), mv, ig, fg, C0, n0, m0)
    ml_o = mlstm_readout(ml_h, mo, ml_norm_g)
    x = x + g1 * merge(conv_o, na_o, ml_o, w_out)
    h2 = rmsnorm(x, ln2_g) * (1 + sc2) + sh2
    x = x + g2 * hier_moe(h2, w_rg, b_rg, w_re, b_re, w_gate, w_up, w_down)
    return x

def setup_inputs(seed: int = 0) -> dict:
    key = jax.random.key(seed)
    ks = jax.random.split(key, 32)
    nrm = lambda k, shape, s: jax.random.normal(k, shape, F32) * s
    x_prompt = nrm(ks[0], (BATCH, SEQ, D_MODEL), 1.0)
    x_sample = nrm(ks[1], (DEC_BATCH, DEC_SEQ, D_MODEL), 1.0)
    cache_k = nrm(ks[2], (DEC_BATCH, DEPTH, PAST_LEN, NA_HEADS, NA_HEAD_DIM), 1.0)
    cache_v = nrm(ks[3], (DEC_BATCH, DEPTH, PAST_LEN, NA_HEADS, NA_HEAD_DIM), 1.0)
    state_C = nrm(ks[4], (DEC_BATCH, DEPTH, N_DIRS, ML_HEADS, ML_HEAD_DIM, ML_HEAD_DIM), 0.1)
    state_n = nrm(ks[5], (DEC_BATCH, DEPTH, N_DIRS, ML_HEADS, ML_HEAD_DIM), 0.1)
    state_m = nrm(ks[6], (DEC_BATCH, DEPTH, N_DIRS, ML_HEADS), 0.5)
    c = nrm(ks[7], (DEC_BATCH, D_MODEL), 1.0)
    c_ctx = nrm(ks[8], (D_MODEL,), 1.0)
    w_mod = nrm(ks[9], (DEPTH, D_MODEL, N_MOD * D_MODEL), 0.5 * D_MODEL ** -0.5)
    b_mod = nrm(ks[10], (DEPTH, N_MOD * D_MODEL), 0.02)
    ln1_g = 1.0 + nrm(ks[11], (DEPTH, D_MODEL), 0.02)
    w_in = nrm(ks[12], (DEPTH, D_MODEL, IN_COLS), D_MODEL ** -0.5)
    conv_w = nrm(ks[13], (DEPTH, CONV_WIDTH, CONV_DIM), CONV_WIDTH ** -0.5)
    na_rpb = nrm(ks[14], (DEPTH, NA_HEADS, 2 * NA_WIN_ROWS - 1, 2 * NA_WIN_COLS - 1), 0.02)
    ml_gate_b = jnp.concatenate([nrm(ks[15], (DEPTH, 1, N_DIRS, ML_HEADS), 0.1),
                                 3.0 + nrm(ks[16], (DEPTH, 1, N_DIRS, ML_HEADS), 0.1)], axis=1)
    ml_norm_g = 1.0 + nrm(ks[17], (DEPTH, ML_DIM), 0.02)
    w_out = nrm(ks[18], (DEPTH, MIX_DIM, D_MODEL), MIX_DIM ** -0.5)
    ln2_g = 1.0 + nrm(ks[19], (DEPTH, D_MODEL), 0.02)
    w_rg = nrm(ks[20], (DEPTH, D_MODEL, N_GROUPS), D_MODEL ** -0.5)
    b_rg = nrm(ks[21], (DEPTH, N_GROUPS), 0.01)
    w_re = nrm(ks[22], (DEPTH, D_MODEL, N_EXPERTS), D_MODEL ** -0.5)
    b_re = nrm(ks[23], (DEPTH, N_EXPERTS), 0.01)
    w_gate = nrm(ks[24], (DEPTH, N_EXPERTS, D_MODEL, EXPERT_FF), D_MODEL ** -0.5)
    w_up = nrm(ks[25], (DEPTH, N_EXPERTS, D_MODEL, EXPERT_FF), D_MODEL ** -0.5)
    w_down = nrm(ks[26], (DEPTH, N_EXPERTS, EXPERT_FF, D_MODEL), EXPERT_FF ** -0.5)
    final_g = 1.0 + nrm(ks[27], (D_MODEL,), 0.02)
    return {'x_prompt': x_prompt, 'x_sample': x_sample, 'cache_k': cache_k, 'cache_v': cache_v,
            'state_C': state_C, 'state_n': state_n, 'state_m': state_m, 'c': c, 'c_ctx': c_ctx,
            'w_mod': w_mod, 'b_mod': b_mod, 'ln1_g': ln1_g, 'w_in': w_in, 'conv_w': conv_w,
            'na_rpb': na_rpb, 'ml_gate_b': ml_gate_b, 'ml_norm_g': ml_norm_g, 'w_out': w_out,
            'ln2_g': ln2_g, 'w_rg': w_rg, 'b_rg': b_rg, 'w_re': w_re, 'b_re': b_re,
            'w_gate': w_gate, 'w_up': w_up, 'w_down': w_down, 'final_g': final_g}

def reference(x_prompt, x_sample, cache_k, cache_v, state_C, state_n, state_m, c, c_ctx,
              w_mod, b_mod, ln1_g, w_in, conv_w, na_rpb, ml_gate_b, ml_norm_g, w_out,
              ln2_g, w_rg, b_rg, w_re, b_re, w_gate, w_up, w_down, final_g):
    xp = x_prompt
    ks, vs, Cs, ns, ms = [], [], [], [], []
    for l in range(DEPTH):
        mods = adaln_params(c_ctx, w_mod[l], b_mod[l])
        xp, k_l, v_l, C_l, n_l, m_l = context_layer(
            xp, mods, ln1_g[l], w_in[l], conv_w[l], ml_gate_b[l], ml_norm_g[l], w_out[l], ln2_g[l],
            w_rg[l], b_rg[l], w_re[l], b_re[l], w_gate[l], w_up[l], w_down[l])
        ks.append(k_l)
        vs.append(v_l)
        Cs.append(C_l)
        ns.append(n_l)
        ms.append(m_l)
    xs = x_sample
    for l in range(DEPTH):
        mods = adaln_params(c, w_mod[l], b_mod[l])
        xs = latent_layer(
            xs, mods, cache_k[:, l], cache_v[:, l], state_C[:, l], state_n[:, l], state_m[:, l],
            ln1_g[l], w_in[l], conv_w[l], na_rpb[l], ml_gate_b[l], ml_norm_g[l], w_out[l], ln2_g[l],
            w_rg[l], b_rg[l], w_re[l], b_re[l], w_gate[l], w_up[l], w_down[l])
    y_prompt = rmsnorm(xp, final_g)
    y_sample = rmsnorm(xs, final_g)
    new_cache_k = jnp.stack(ks, axis=1)
    new_cache_v = jnp.stack(vs, axis=1)
    new_state_C = jnp.stack(Cs, axis=1)
    new_state_n = jnp.stack(ns, axis=1)
    new_state_m = jnp.stack(ms, axis=1)
    return (y_prompt, y_sample, new_cache_k, new_cache_v, new_state_C, new_state_n, new_state_m)


_drawn_inputs = setup_inputs


def setup_inputs(seed=0):
    import zlib

    import numpy as np

    out = dict(_drawn_inputs(seed))
    spreads = {}
    factors = {'cache_k': 2.802,
     'state_C': 3.858,
     'state_n': 8.0,
     'state_m': 7.598,
     'na_rpb': 64.0,
     'ml_norm_g': 5.857,
     'b_rg': 23.585,
     'b_re': 27.166,
     'final_g': 9.784,
     'ln2_g': 3.117}
    for name, (base, spread) in spreads.items():
        noise = np.random.default_rng([zlib.crc32(name.encode()), seed]).standard_normal(out[name].shape)
        drawn = base * np.exp(spread * noise) if base else spread * noise
        out[name] = __import__('jax').numpy.asarray(drawn.astype(out[name].dtype))
    for name, factor in factors.items():
        out[name] = (out[name] * factor).astype(out[name].dtype)
    return out
```

```python
from contextlib import ExitStack

import numpy as np
import concourse.bass as bass
from concourse import mybir

ALU = mybir.AluOpType
ACT = mybir.ActivationFunctionType
F32 = mybir.dt.float32
I32 = mybir.dt.int32
AX = mybir.AxisListType

P = 128
BIG = 1.0e30
GRID_W = 64
WIN_ROWS, WIN_COLS = 8, 16
EPS = 1e-6
SMALLS = 13
RING = 4
BANKS = 8
RELBIAS_DIFFS = 7

C_IDENT, C_MASKF, C_MASKB, C_TRI, C_IOTA, C_ONES, C_MEAN = (P * i for i in range(7))
C_SEL = 7 * P
C_ROPE = C_SEL + 8 * P
C_NAMASK = C_ROPE + 2 * P
C_PRIO4 = C_NAMASK + GRID_W
C_PRIO16 = C_PRIO4 + 4
C_BASE = C_PRIO16 + 16
C_EPS = C_BASE + 4
C_ONE = C_EPS + 1
C_STEP = C_ONE + 1
C_WIDTH = C_STEP + 2

V_LN1, V_LN2, V_BMOD, V_CONV, V_N0, V_C, V_FINAL, V_ROWS = 0, 8, 16, 64, 70, 78, 94, 102


def constant_table():
    t = np.zeros((P, C_WIDTH), np.float32)
    i = np.arange(P)
    t[:, C_IDENT:C_IDENT + P] = np.eye(P)
    t[:, C_MASKF:C_MASKF + P] = np.where(i[:, None] > i[None, :], BIG, 0.0)
    t[:, C_MASKB:C_MASKB + P] = np.where(i[:, None] < i[None, :], BIG, 0.0)
    t[:, C_TRI:C_TRI + P] = i[:, None] < i[None, :]
    t[:, C_IOTA:C_IOTA + P] = i[None, :]
    t[:, C_ONES:C_ONES + P] = 1.0
    t[:, C_MEAN:C_MEAN + P] = 1.0 / 1024
    for dh in range(8):
        t[(dh // 4) * 32 + dh % 4, C_SEL + dh * P:C_SEL + (dh + 1) * P] = 1.0
    nf = 32
    inv = (np.float32(10000.0) ** (-np.arange(nf, dtype=np.float32) / nf)).astype(np.float32)
    for half in range(2):
        tok = half * P + i
        pos = np.stack([tok // GRID_W, tok % GRID_W], -1).astype(np.float32)
        ang = (pos[:, :, None] * inv).astype(np.float32).reshape(P, 2 * nf)
        t[:, C_ROPE + half * P:C_ROPE + half * P + 64] = np.cos(ang)
        t[:, C_ROPE + half * P + 64:C_ROPE + (half + 1) * P] = np.sin(ang)
    col = i % GRID_W
    start = np.clip(col - WIN_COLS // 2, 0, GRID_W - WIN_COLS)
    key = np.arange(GRID_W)
    inside = (key[None, :] >= start[:, None]) & (key[None, :] < start[:, None] + WIN_COLS)
    t[:, C_NAMASK:C_NAMASK + GRID_W] = np.where(inside, 0.0, -BIG)
    t[:, C_PRIO4:C_PRIO4 + 4] = np.arange(4, 0, -1)
    t[:, C_PRIO16:C_PRIO16 + 16] = np.arange(16, 0, -1)
    t[:, C_BASE:C_BASE + 4] = P * np.arange(4)
    t[:, C_EPS] = EPS
    t[:, C_ONE] = 1.0
    t[:, C_STEP:C_STEP + 2] = np.arange(2)
    return t


class Banks:

    def __init__(self, full, drained):
        self.full, self.drained = full, drained
        self.at, self.used, self.per_job = {}, [0] * BANKS, [0] * BANKS
        self.in_job = False

    def place(self, name, bank):
        self.at[name] = (bank, self.used[bank], self.in_job)
        self.used[bank] += 1
        if self.in_job:
            self.per_job[bank] += 1

    def number(self, name, job):
        bank, n, in_job = self.at[name]
        return bank, (job * self.per_job[bank] + n if in_job and job is not None else n)

    def wait_free(self, pe, name, job=None):
        bank, n = self.number(name, job)
        if self.at[name][1] > 0:
            pe.wait_ge(self.drained[bank], n)

    def wait_full(self, eng, name, job=None):
        bank, n = self.number(name, job)
        eng.wait_ge(self.full[bank], n + 1)

    def wait_drained(self, eng, name, job=None):
        bank, n = self.number(name, job)
        eng.wait_ge(self.drained[bank], n + 1)

    def bank(self, name):
        return self.at[name][0]


def build(nc, a, o):
    D, FF, NT, TILES, DEPTH = 1024, 512, 384, 3, 2
    KT = D // P
    IN_COLS = a["w_in"].shape[2]
    STREAMS = ((0, slice(0, P)), (1, slice(P, NT)))
    ISQ = 1.0 / float(np.sqrt(128.0))

    with ExitStack() as ctx:
        def sb(name, shape, dt=F32):
            return ctx.enter_context(nc.sbuf_tensor(name, shape, dt))

        layer_sems = []

        def sem(name, kept=False):
            s = ctx.enter_context(nc.semaphore(name))
            if not kept:
                layer_sems.append(s)
            return s

        xT = sb("xT", [P, KT, NT])
        hT = sb("hT", [P, KT, NT])
        mixT = sb("mixT", [P, KT, NT])
        ring = sb("ring", [P, RING, 4096])
        zqk = sb("zqk", [P, 3, 1024])
        vaug = sb("vaug", [P, 3, 4, 129])
        arena = sb("arena", [P, 6668])
        kvp = sb("kvp", [P, 512])
        nv = sb("nv", [P, 2, 256])
        cb = sb("cb", [P, 2, NT])
        upad = sb("upad", [P, 2, 388])
        nqT = sb("nqT", [P, 2, NT])
        nkT = sb("nkT", [P, 2, NT])
        cst = sb("cst", [P, C_WIDTH])
        caug = sb("caug", [P, 8, 129])
        cnew = sb("cnew", [P, 8, 129])
        relb = sb("relb", [P, 4, RELBIAS_DIFFS, GRID_W])
        gbc = sb("gbc", [P, 512])
        vrow = sb("vrow", [V_ROWS, P])
        vT = sb("vT", [P, V_ROWS])
        csil = sb("csil", [P, 8, 2])
        modT = sb("modT", [P, 48, 2])
        gain1 = sb("gain1", [P, 8, 2])
        gain2 = sb("gain2", [P, 8, 2])
        std = sb("std", [P, NT])
        wgate = sb("wgate", [P, KT, 16])
        wroute = sb("wroute", [P, KT, 20])
        gbias = sb("gbias", [P, 16])
        rbias = sb("rbias", [P, 20])
        m0 = sb("m0", [64, 1])
        gpad = sb("gpad", [P, 2, 3, 64])
        rows = mixT[0:64, 2:8, :]
        mend = sb("mend", [64, 4])
        tokg = sb("tokg", [P, 9, 64])
        kct = sb("kct", [P, 2, P])
        cachek = sb("cachek", [P, 256])
        cachev = sb("cachev", [P, 256])
        small = sb("small", [P, 64])
        head = sb("head", [P, 3, 12])
        route = sb("route", [P, 320])
        jobs = sb("jobs", [P, 4], I32)
        gslot = sb("gslot", [P, 4])

        ident = cst[:, C_IDENT:C_IDENT + P]
        ones = cst[:, C_ONES:C_ONES + P]
        mean = cst[:, C_MEAN:C_MEAN + P]
        eps = cst[:, C_EPS:C_EPS + 1]
        one = cst[:, C_ONE:C_ONE + 1]

        W = arena[:, 0:1024].rearrange("p (b n) -> p b n", b=2)
        S = arena[:, 1024:2048].rearrange("p (b n) -> p b n", b=2)
        inter = arena[:, 2048:2048 + 774].rearrange("p (b t n) -> p b t n", b=2, t=3)
        total = arena[:, 2822:2822 + 774].rearrange("p (b t n) -> p b t n", b=2, t=3)
        sigo = arena[:, 3596:5132].rearrange("p (t n) -> p t n", t=3)
        hsum = arena[:, 5132:6668].rearrange("p (t n) -> p t n", t=3)
        pctx = arena[:, 0:512]
        ploc = arena[:, 512:1280].rearrange("p (b n) -> p b n", b=2)
        pT = arena[:, 1280:2048].rearrange("p (b n) -> p b n", b=2)
        xg = arena[:, 0:1024].rearrange("p (k n) -> p k n", k=KT)
        sg = arena[:, 1024:2048].rearrange("p (b n) -> p b n", b=2)
        act_in = arena[:, 2048:3072].rearrange("p (b n) -> p b n", b=2)
        aT = arena[:, 3072:4096].rearrange("p (b n) -> p b n", b=2)
        ysb = arena[:, 4096:5120]
        selT = arena[:, 5120:5504]
        sel = arena[:, 5504:5888].rearrange("p (t n) -> p t n", t=3)
        h2tok = zqk
        kw = sb("kw", [P, 2, P])
        cuts = [0]

        def piece(n, pattern=None, **sizes):
            cuts[0] += n
            v = route[:, cuts[0] - n:cuts[0]]
            return v.rearrange(pattern, **sizes) if pattern else v
        logits = piece(60, "p (t n) -> p t n", t=3)
        oh_group = piece(12, "p (t n) -> p t n", t=3)
        gates4 = piece(12, "p (t n) -> p t n", t=3)
        picked = piece(48, "p (t n) -> p t n", t=3)
        one1 = piece(48, "p (t n) -> p t n", t=3)
        one2 = piece(48, "p (t n) -> p t n", t=3)
        r_exp = piece(15, "p (t n) -> p t n", t=3)
        g_best, e_best1, e_best2, r_tmp, r_tmp2, slot_of = (piece(3) for _ in range(6))
        rank_s = piece(16)
        extra, upto, before, jobs_f = (piece(4) for _ in range(4))
        squares = mixT

        ps = [ctx.enter_context(nc.psum_tensor(f"ps{b}", [P, 512], F32)) for b in range(BANKS)]

        full = [sem(f"full{b}") for b in range(BANKS)]
        drained = [sem(f"drained{b}") for b in range(BANKS)]
        ring_loaded = [sem(f"ring_loaded{s}") for s in range(RING)]
        vecs_loaded = sem("vecs_loaded", kept=True)
        smalls_loaded = sem("smalls_loaded", kept=True)
        stored = sem("stored", kept=True)
        vT_ready = sem("vT_ready")
        csil_ready = sem("csil_ready")
        squares_ready = sem("squares_ready")
        std_ready = sem("std_ready")
        scaled_ready = sem("scaled_ready")
        h_ready = sem("h_ready")
        gpad_ready = sem("gpad_ready")
        fexp_ready = sem("fexp_ready")
        fabs_ready = sem("fabs_ready")
        rowsin_ready = sem("rowsin_ready")
        rowsout_ready = sem("rowsout_ready")
        rope_ready = sem("rope_ready")
        conv_ready = sem("conv_ready")
        pmax_ready = sem("pmax_ready")
        pexp_ready = sem("pexp_ready")
        prob_ready = sem("prob_ready")
        caug_ready = sem("caug_ready")
        decay_ready = sem("decay_ready")
        score_ready = sem("score_ready")
        inter_ready = sem("inter_ready")
        total_done = sem("total_done")
        kw_ready = sem("kw_ready")
        msq_ready = sem("msq_ready")
        hstd_ready = sem("hstd_ready")
        hnorm_ready = sem("hnorm_ready")
        onehot_ready = sem("onehot_ready")
        rexp_in = sem("rexp_in")
        rexp_ready = sem("rexp_ready")
        jobs_ready = sem("jobs_ready")
        sel_ready = sem("sel_ready")
        silu_ready = sem("silu_ready")
        gated_ready = sem("gated_ready")
        mnew_ready = sem("mnew_ready")
        dve_chain = sem("dve_chain")
        act_chain = sem("act_chain")
        job_chain = sem("job_chain")
        const_loaded = sem("const_loaded", kept=True)
        x_loaded = sem("x_loaded", kept=True)
        x_turned = sem("x_turned", kept=True)
        x_copied = sem("x_copied", kept=True)
        set_once = sem("set_once", kept=True)
        windows_written = sem("windows_written", kept=True)
        bias_windows = nc.dram_tensor("bias_windows", (DEPTH, P, 4, RELBIAS_DIFFS, GRID_W), F32).ap()

        bk = Banks(full, drained)
        turn = [0]

        def spread(names, over=range(BANKS)):
            over = list(over)
            for name in names:
                bk.place(name, over[turn[0] % len(over)])
                turn[0] += 1

        ML_CHUNKS = ("mq", "mk", "mv", "mo")
        spread(["vec", "mod", "ss1", "gate"])
        spread([("mq", t) for t in range(3)] + ["gT_f", "gT_i"])
        spread([(c, t) for c in ML_CHUNKS[1:] for t in range(3)])
        spread([("fm", i) for i in range(10)] + ["kvp", ("nv", 0), ("nv", 1)])
        spread(["rowsA", "rowsB", "kc"] + [("qkT", i) for i in range(8)])
        NA = [(h, q) for h in range(4) for q in range(2)]
        spread([("sp", 0), ("sp", 1)], range(6))
        spread([("ss", *NA[0]), ("ss", *NA[1])], range(6))
        spread([("pTp", h) for h in range(4)], range(6))
        for n, u in enumerate(NA):
            spread([("pT", *u)], range(6))
            if n + 2 < len(NA):
                spread([("ss", *NA[n + 2])], range(6))
        for i in range(2):
            bk.place(("o", i), 6 + i)
        for dh in range(8):
            spread([("mu", dh), ("kq", dh), ("int", dh), ("num", dh), ("C", dh)])
        spread([("hT", h) for h in range(4)] + [("wo", m) for m in range(8)])
        spread(["ss2", "lg"] + [("h2", i) for i in range(6)] + ["rank"])
        bk.in_job = True
        bk.place("selT", 7)
        bk.place("gs", 6)
        bk.place(("xg", 0), 2)
        bk.place(("xg", 1), 3)
        GU_BANKS = [(4, 5), (2, 3), (4, 5), (2, 3)]
        for e in range(4):
            bk.place(("G", e), GU_BANKS[e][0])
            bk.place(("U", e), GU_BANKS[e][1])
            if e:
                bk.place(("aT", e - 1), 6 + (e - 1) % 2)
        bk.place(("aT", 3), 7)
        bk.place(("y", 0), 0)
        bk.place(("y", 1), 1)
        for m in range(KT):
            bk.place(("back", m), (2, 3, 4, 5, 6, 7)[m % 6])
        bk.in_job = False

        loads = [(("mod", c), None) for c in range(12)]
        loads += [((c, 0), (c, 2)) for c in ML_CHUNKS]
        loads += [(("conv", 0), ("fm", 3)), (("conv", 1), ("fm", 7)), (("kv", 0), ("nv", 1))]
        loads += [(("wo", 0), ("wo", 3)), (("wo", 1), ("wo", 7))]
        MOE0 = len(loads)
        PER_JOB = 12
        JOB_READS = [r for e in range(4) for r in (("G", e), ("U", e), ("aT+", e))]
        index = {name: i for i, (name, _) in enumerate(loads)}
        mod_read = sem("mod_read")
        down_read = sem("down_read")

        def slot(i):
            return ring[:, i % RING, :]

        def wait_loaded(eng, i, job=None):
            if job is None:
                eng.wait_ge(ring_loaded[i % RING], 16 * (i // RING + 1))
            else:
                n = MOE0 + i
                eng.wait_ge(ring_loaded[n % RING],
                            job * (16 * PER_JOB // RING) + 16 * (n // RING + 1))

        def job_slot(i):
            return slot(MOE0 + i)

        def layer(ap, l):
            return ap[bass.ds(l, 1)]

        xrow = ring[:, 0:1, 0:3072].rearrange("p a (t d) -> p (a t) d", t=3)
        with nc.Block() as block:
            @block.sync
            def _(sp):
                sp.dma_start(xrow[:, 0, :], a["x_prompt"][0]).then_inc(x_loaded, 16)
                sp.dma_start(xrow[:, 1:3, :], a["x_sample"][0].rearrange("(t p) d -> p t d", p=P)
                             ).then_inc(x_loaded, 16)
                sp.dma_start(cst[:], a["constants"]).then_inc(const_loaded, 16)

            @block.gpsimd
            def _(pool):
                for d in range(DEPTH):
                    for parity in range(2):
                        for h in range(4):
                            base = ((d * 4 + h) * 15 + 4 - parity) * 31 + 15
                            pool.dma_start(bias_windows[d, 64 * parity:64 * parity + 64, h].rearrange("p j w -> j p w"),
                                           bass.AP(a["na_rpb"].tensor, base,
                                                   [[31, RELBIAS_DIFFS], [-1, GRID_W], [1, GRID_W]])
                                           ).then_inc(windows_written, 16)
                pool.wait_ge(windows_written, 16 * 8 * DEPTH)

            @block.vector
            def _(dve):
                dve.memset(upad[:], 0.0).then_inc(set_once, 1)
                dve.memset(gpad[:], 0.0).then_inc(set_once, 1)
                dve.memset(vaug[:, :, :, 128:129], 1.0).then_inc(set_once, 1)
                dve.memset(m0[:], 0.0).then_inc(set_once, 1)
                for k in range(KT):
                    dve.wait_ge(x_turned, k + 1)
                    dve.tensor_copy(xT[:, k, :], ps[k][:, 0:NT]).then_inc(x_copied, 1)

            @block.tensor
            def _(pe):
                pe.wait_ge(x_loaded, 32)
                pe.wait_ge(const_loaded, 16)
                for k in range(KT):
                    for t in range(TILES):
                        mm = pe.transpose(ps[k][:, t * P:(t + 1) * P], xrow[:, t, k * P:(k + 1) * P], ident)
                    mm.then_inc(x_turned, 1)

        with nc.Fori(0, DEPTH) as l:
            with nc.Block() as block:

                @block.sync
                def _(sp):
                    w_mod = layer(a["w_mod"], l).rearrange("a (k p) n -> p (a k) n", p=P)
                    w_in = layer(a["w_in"], l).rearrange("a (k p) n -> p (a k) n", p=P)
                    w_out = layer(a["w_out"], l).rearrange("a (k p) n -> p (a k) n", p=P)
                    first = {"mq": 1536, "mk": 2048, "mv": 2560, "mo": 3072}
                    for i, (name, _) in enumerate(loads):
                        if i >= RING:
                            before, last = loads[i - RING]
                            if before[0] == "mod" and before[1] < 11:
                                sp.wait_ge(mod_read, before[1] + 1)
                            elif before[0] == "mod":
                                bk.wait_full(sp, "mod")
                            else:
                                bk.wait_full(sp, last)
                        kind, n = name
                        if kind == "mod":
                            src = w_mod[:, :, n * 512:(n + 1) * 512]
                        elif kind == "wo":
                            src = w_out[:, :, n * 512:(n + 1) * 512]
                        else:
                            c0 = {"conv": 512 * n, "kv": 1024}.get(kind, first.get(kind))
                            src = w_in[:, :, c0:c0 + 512]
                        sp.dma_start(slot(i).rearrange("p (k n) -> p k n", k=KT), src
                                     ).then_inc(ring_loaded[i % RING], 16)

                    def down_is_read(e, job):
                        if e < 3:
                            sp.wait_ge(down_read, job * 3 + e + 1)
                        else:
                            bk.wait_full(sp, ("y", 1), job)

                    def job_loads(job, group, first_job):
                        for i in range(PER_JOB):
                            e, which = i // 3, i % 3
                            if i >= RING:
                                pe_, pw = (i - RING) // 3, (i - RING) % 3
                                if pw < 2:
                                    bk.wait_full(sp, ("GU"[pw], pe_), job)
                                else:
                                    down_is_read(pe_, job)
                            elif first_job:
                                before, last = loads[MOE0 + i - RING]
                                bk.wait_full(sp, last)
                            else:
                                pe_, pw = (i + PER_JOB - RING) // 3, (i + PER_JOB - RING) % 3
                                if pw < 2:
                                    bk.wait_full(sp, ("GU"[pw], pe_), job - 1)
                                else:
                                    down_is_read(pe_, job - 1)
                            w = a[("w_gate", "w_up", "w_down")[which]]
                            rows_of = w[bass.ds(l, 1), bass.ds(group * 4 + e, 1)]
                            kt = KT if which < 2 else FF // P
                            sp.dma_start(job_slot(i).rearrange("p (k n) -> p k n", k=kt),
                                         rows_of.rearrange("a e (k p) n -> p (a e k) n", p=P)
                                         ).then_inc(ring_loaded[(MOE0 + i) % RING], 16)

                    job_loads(0, 0, True)
                    with sp.Fori(1, 4) as job:
                        job_loads(job, job, False)
                    sp.wait_ge(jobs_ready, 1)
                    count = sp.value_load(jobs[0:1, 0:1], min_val=4, max_val=6)
                    with sp.If(count > 4):
                        with sp.Fori(4, count) as job:
                            group = sp.value_load(jobs[0:1, bass.ds(job - 3, 1)], min_val=0, max_val=3)
                            job_loads(job, group, False)

                @block.gpsimd
                def _(pool):
                    def row(first, n, src):
                        pool.dma_start(vrow[first:first + n, :], src).then_inc(vecs_loaded, 16)
                    row(V_LN1, 8, layer(a["ln1_g"], l).rearrange("a (r n) -> (a r) n", n=P))
                    row(V_LN2, 8, layer(a["ln2_g"], l).rearrange("a (r n) -> (a r) n", n=P))
                    row(V_BMOD, 48, layer(a["b_mod"], l).rearrange("a (r n) -> (a r) n", n=P))
                    row(V_CONV, 6, layer(a["conv_w"], l).rearrange("a w (r n) -> (a w r) n", n=P))
                    row(V_N0, 8, a["state_n"][0][bass.ds(l, 1)].rearrange("a r h d -> (a r h) d"))
                    row(V_C, 8, a["c_ctx"].rearrange("(r n) -> r n", n=P))
                    row(V_C + 8, 8, a["c"].rearrange("a (r n) -> (a r) n", n=P))
                    row(V_FINAL, 8, a["final_g"].rearrange("(r n) -> r n", n=P))

                    def load(dst, src):
                        pool.dma_start(dst, src, allow_slow_non_contiguous=True).then_inc(smalls_loaded, 16)
                    load(wgate[:], layer(a["w_in"], l).rearrange("a (k p) n -> p (a k) n", p=P)[:, :, IN_COLS - 16:IN_COLS])
                    load(wroute[:, :, 0:4], layer(a["w_rg"], l).rearrange("a (k p) n -> p (a k) n", p=P))
                    load(wroute[:, :, 4:20], layer(a["w_re"], l).rearrange("a (k p) n -> p (a k) n", p=P))
                    load(gbias[:], layer(a["ml_gate_b"], l).rearrange("a r n h -> a (r n h)").broadcast_to((P, 16)))
                    load(rbias[:, 0:4], layer(a["b_rg"], l).broadcast_to((P, 4)))
                    load(rbias[:, 4:20], layer(a["b_re"], l).broadcast_to((P, 16)))
                    load(gbc[:], layer(a["ml_norm_g"], l).broadcast_to((P, 512)))
                    for d in range(2):
                        load(m0[32 * d:32 * d + 4, :], a["state_m"][0][bass.ds(l, 1), d].rearrange("a h -> h a"))
                    load(cachek[:], a["cache_k"][0][bass.ds(l, 1)].rearrange("a t h d -> (a t) (h d)"))
                    load(cachev[:], a["cache_v"][0][bass.ds(l, 1)].rearrange("a t h d -> (a t) (h d)"))
                    load(caug[:, :, 0:P], a["state_C"][0][bass.ds(l, 1)].rearrange("a r h d e -> d (a r h) e"))
                    load(relb[:], bias_windows[bass.ds(l, 1)].rearrange("a p h j w -> (a p) h j w"))

                    def store(dst, src):
                        pool.dma_start(dst, src, allow_slow_non_contiguous=True).then_inc(stored, 16)
                    bk.wait_drained(pool, "kvp")
                    store(o["new_cache_k"][0][bass.ds(l, 1)].rearrange("a t h d -> (a t) (h d)"), kvp[:, 0:256])
                    store(o["new_cache_v"][0][bass.ds(l, 1)].rearrange("a t h d -> (a t) (h d)"), kvp[:, 256:512])
                    pool.wait_ge(mnew_ready, 1)
                    for d in range(2):
                        store(o["new_state_m"][0][bass.ds(l, 1), d].rearrange("a h -> h a"),
                              mend[32 * d:32 * d + 4, 2:3])
                    for dh in range(8):
                        bk.wait_drained(pool, ("C", dh))
                    store(o["new_state_C"][0][bass.ds(l, 1)].rearrange("a r h d e -> d (a r h) e"), cnew[:, :, 0:P])
                    store(o["new_state_n"][0][bass.ds(l, 1)].rearrange("a r h d -> d (a r h)"), cnew[:, :, P])
                    pool.wait_ge(stored, (l + 1) * (16 * 6))

                @block.tensor
                def _(pe):
                    def begin(name, job=None):
                        bk.wait_free(pe, name, job)
                        return ps[bk.bank(name)]

                    def done(mm, name):
                        mm.then_inc(full[bk.bank(name)], 1)

                    def sum_squares(name, n):
                        p = begin(name)
                        for k in range(KT):
                            pe.wait_ge(squares_ready, n * KT + k + 1)
                            mm = pe.matmul(p[:, 0:NT], mean, squares[:, k, :], start=(k == 0), stop=(k == KT - 1))
                        done(mm, name)

                    pe.wait_ge(vecs_loaded, (l + 1) * (16 * 8))
                    p = begin("vec")
                    done(pe.transpose(p[:, 0:V_ROWS], vrow[:], ident[0:V_ROWS, 0:V_ROWS]), "vec")
                    pe.wait_ge(csil_ready, 1)
                    p = begin("mod")
                    for m in range(48):
                        wait_loaded(pe, m // 4)
                        w = slot(m // 4).rearrange("p (k n) -> p k n", k=KT)
                        for k in range(KT):
                            mm = pe.matmul(p[:, 2 * m:2 * m + 2], w[:, k, (m % 4) * P:(m % 4 + 1) * P],
                                           csil[:, k, :], start=(k == 0), stop=(k == KT - 1))
                        if m == 47:
                            done(mm, "mod")
                        elif m % 4 == 3:
                            mm.then_inc(mod_read, 1)
                    sum_squares("ss1", 0)

                    pe.wait_ge(h_ready, KT)
                    pe.wait_ge(smalls_loaded, (l + 1) * (16 * SMALLS))
                    p = begin("gate")
                    for t in range(TILES):
                        for k in range(KT):
                            mm = pe.matmul(p[:, t * 16:(t + 1) * 16], hT[:, k, t * P:(t + 1) * P], wgate[:, k, :],
                                           start=(k == 0), stop=(k == KT - 1))
                    done(mm, "gate")

                    def token_major(name, load, t, c0, n):
                        wait_loaded(pe, index[load])
                        w = slot(index[load]).rearrange("p (k n) -> p k n", k=KT)
                        p = begin(name)
                        for k in range(KT):
                            mm = pe.matmul(p[:, 0:n], hT[:, k, t * P:(t + 1) * P], w[:, k, c0:c0 + n],
                                           start=(k == 0), stop=(k == KT - 1))
                        done(mm, name)

                    for t in range(TILES):
                        token_major(("mq", t), ("mq", 0), t, 0, 512)
                    pe.wait_ge(gpad_ready, 2)
                    for n, name in enumerate(("gT_f", "gT_i")):
                        p = begin(name)
                        for t in range(TILES):
                            mm = pe.transpose(p[0:64, t * P:(t + 1) * P], gpad[:, n, t, :], ident)
                        done(mm, name)
                    for c in ML_CHUNKS[1:]:
                        for t in range(TILES):
                            token_major((c, t), (c, 0), t, 0, 512)
                    for i in range(10):
                        load = ("conv", i // 4) if i < 8 else ("kv", 0)
                        wait_loaded(pe, index[load])
                        w = slot(index[load]).rearrange("p (k n) -> p k n", k=KT)
                        p = begin(("fm", i))
                        for k in range(KT):
                            mm = pe.matmul(p[:, 0:NT], w[:, k, (i % 4) * P:(i % 4 + 1) * P], hT[:, k, :],
                                           start=(k == 0), stop=(k == KT - 1))
                        done(mm, ("fm", i))
                    token_major("kvp", ("kv", 0), 0, 0, 512)
                    token_major(("nv", 0), ("kv", 0), 1, 256, 256)
                    token_major(("nv", 1), ("kv", 0), 2, 256, 256)

                    pe.wait_ge(rowsout_ready, 4)
                    p = begin("rowsA")
                    for n, r in enumerate((1, 5)):
                        for t in range(TILES):
                            mm = pe.transpose(p[:, (3 * n + t) * 64:(3 * n + t + 1) * 64],
                                              rows[:, r, t * P:(t + 1) * P], ident[0:64, 0:64])
                    done(mm, "rowsA")
                    p = begin("rowsB")
                    for n, (r, t) in enumerate(((4, 1), (4, 2), (4, 0))):
                        mm = pe.transpose(p[:, n * 64:(n + 1) * 64], rows[:, r, t * P:(t + 1) * P],
                                          ident[0:64, 0:64])
                    done(mm, "rowsB")
                    p = begin("kc")
                    for i in range(2):
                        mm = pe.transpose(p[:, i * P:(i + 1) * P], cachek[:, i * P:(i + 1) * P], ident)
                    done(mm, "kc")
                    pe.wait_ge(rope_ready, 1)
                    for i in range(8):
                        p = begin(("qkT", i))
                        for t in range(TILES):
                            mm = pe.transpose(p[:, t * P:(t + 1) * P], zqk[:, t, i * P:(i + 1) * P], ident)
                        done(mm, ("qkT", i))

                    def half(h):
                        return slice(64 * (h % 2), 64 * (h % 2) + 64)

                    bk.wait_drained(pe, ("fm", 9))
                    bk.wait_drained(pe, ("fm", 8))
                    bk.wait_drained(pe, "kc")
                    for odd in range(2):
                        p = begin(("sp", odd))
                        for i in range(2):
                            mm = pe.matmul(p[:, i * P:(i + 1) * P], nqT[half(odd), i, 0:P],
                                           nkT[half(odd), i, 0:P], start=True, stop=True)
                        done(mm, ("sp", odd))

                    def latent_scores(h, q):
                        p = begin(("ss", h, q))
                        qs = nqT[half(h), h // 2, (1 + q) * P:(2 + q) * P]
                        pe.matmul(p[:, 0:256], qs, nkT[half(h), h // 2, P:NT], start=True, stop=True)
                        done(pe.matmul(p[:, 256:384], qs, kct[half(h), h // 2, :], start=True, stop=True),
                             ("ss", h, q))

                    latent_scores(*NA[0])
                    latent_scores(*NA[1])
                    pe.wait_ge(prob_ready, 1)
                    for h in range(4):
                        p = begin(("pTp", h))
                        done(pe.transpose(p[:, 0:P], pctx[:, h * P:(h + 1) * P], ident), ("pTp", h))
                        bk.wait_drained(pe, ("pTp", h))
                        o_ps = ps[bk.bank(("o", h // 2))]
                        if h % 2 == 0:
                            begin(("o", h // 2))
                        pe.matmul(o_ps[half(h), 0:P], kvp[:, 256 + h * 64:256 + (h + 1) * 64],
                                  pT[:, h % 2, 0:P], start=True, stop=True)
                    for n, (h, q) in enumerate(NA):
                        pe.wait_ge(prob_ready, n + 2)
                        p = begin(("pT", h, q))
                        for i in range(3):
                            mm = pe.transpose(p[:, i * P:(i + 1) * P], ploc[:, n % 2, i * P:(i + 1) * P], ident)
                        done(mm, ("pT", h, q))
                        if n + 2 < len(NA):
                            latent_scores(*NA[n + 2])
                        bk.wait_drained(pe, ("pT", h, q))
                        for i in range(3):
                            values = nv[:, i] if i < 2 else cachev[:]
                            mm = pe.matmul(ps[bk.bank(("o", h // 2))][half(h), (1 + q) * P:(2 + q) * P],
                                           values[:, h * 64:(h + 1) * 64],
                                           pT[:, n % 2, i * P:(i + 1) * P], start=(i == 0), stop=(i == 2))
                        if h % 2 == 1 and q == 1:
                            done(mm, ("o", h // 2))

                    for i in range(8):
                        bk.wait_drained(pe, ("qkT", i))
                    pe.wait_ge(caug_ready, 1)
                    TRI_BLOCKS = [(0, 0), (1, 1), (2, 2)]

                    def blocks(dh):
                        return TRI_BLOCKS + [(1, 2) if dh < 4 else (2, 1)]

                    def weights_and_scores(dh):
                        h = dh % 4
                        p = begin(("mu", dh))
                        sel_row = cst[0:64, C_SEL + dh * P:C_SEL + (dh + 1) * P]
                        mask = C_MASKF if dh < 4 else C_MASKB
                        off = blocks(dh)[3][1]
                        pe.matmul(p[:, 0:NT], sel_row, rows[:, 3, :], start=True, stop=False, skip_group_check=True)
                        for b in range(3):
                            pe.matmul(p[:, b * P:(b + 1) * P], ident, cst[:, mask:mask + P], start=False,
                                      stop=True, skip_group_check=True)
                        done(pe.matmul(p[:, NT:512], sel_row, rows[:, 3, off * P:(off + 1) * P], start=True,
                                       stop=True, skip_group_check=True), ("mu", dh))
                        p = begin(("kq", dh))
                        for b, (s, t) in enumerate(blocks(dh)):
                            mm = pe.matmul(p[:, b * P:(b + 1) * P], hT[:, 4 + h, s * P:(s + 1) * P],
                                           hT[:, h, t * P:(t + 1) * P], start=True, stop=True)
                        done(mm, ("kq", dh))
                        p = begin(("int", dh))
                        for t in (1, 2):
                            mm = pe.matmul(p[:, (t - 1) * 129:t * 129], hT[:, h, t * P:(t + 1) * P],
                                           caug[:, dh, :], start=True, stop=True)
                        done(mm, ("int", dh))

                    def read_memory(dh):
                        h = dh % 4
                        pe.wait_ge(score_ready, dh + 1)
                        p = begin(("num", dh))
                        for t in range(TILES):
                            own = [b for b, (_, to) in enumerate(blocks(dh)) if to == t]
                            for n, b in enumerate(own):
                                mm = pe.matmul(p[:, t * 129:(t + 1) * 129], S[:, dh % 2, b * P:(b + 1) * P],
                                               vaug[:, blocks(dh)[b][0], h, :], start=(n == 0),
                                               stop=(n == len(own) - 1))
                        done(mm, ("num", dh))
                        pe.wait_ge(kw_ready, dh + 1)
                        p = begin(("C", dh))
                        done(pe.matmul(p[:, 0:129], kw[:, dh % 2, :], vaug[:, 0, h, :], start=True, stop=True),
                             ("C", dh))

                    weights_and_scores(0)
                    for dh in range(8):
                        if dh < 7:
                            weights_and_scores(dh + 1)
                        read_memory(dh)

                    pe.wait_ge(hnorm_ready, 1)
                    for h in range(4):
                        p = begin(("hT", h))
                        for t in range(TILES):
                            mm = pe.transpose(p[:, t * P:(t + 1) * P], hsum[:, t, h * P:(h + 1) * P], ident)
                        done(mm, ("hT", h))

                    pe.wait_ge(conv_ready, 1)
                    for i in range(2):
                        bk.wait_drained(pe, ("o", i))
                    for h in range(4):
                        bk.wait_drained(pe, ("hT", h))
                    for m in range(KT):
                        i = index[("wo", m // 4)]
                        wait_loaded(pe, i)
                        w = slot(i).rearrange("p (k n) -> p k n", k=KT)
                        p = begin(("wo", m))
                        for k in range(KT):
                            mm = pe.matmul(p[:, 0:NT], w[:, k, (m % 4) * P:(m % 4 + 1) * P], mixT[:, k, :],
                                           start=(k == 0), stop=(k == KT - 1))
                        done(mm, ("wo", m))

                    sum_squares("ss2", 1)

                    pe.wait_ge(h_ready, 2 * KT)
                    p = begin("lg")
                    for t in range(TILES):
                        for k in range(KT):
                            mm = pe.matmul(p[:, t * 20:(t + 1) * 20], hT[:, k, t * P:(t + 1) * P], wroute[:, k, :],
                                           start=(k == 0), stop=(k == KT - 1))
                    done(mm, "lg")
                    for i in range(6):
                        t, half_of = i // 2, i % 2
                        p = begin(("h2", i))
                        for n in range(4):
                            mm = pe.transpose(p[:, n * P:(n + 1) * P],
                                              hT[:, half_of * 4 + n, t * P:(t + 1) * P], ident)
                        done(mm, ("h2", i))
                    pe.wait_ge(onehot_ready, 1)
                    p = begin("rank")
                    tri = cst[:, C_TRI:C_TRI + P]
                    for t in range(TILES):
                        for s in range(t):
                            pe.matmul(p[:, t * 4:(t + 1) * 4], ones, oh_group[:, s, :], start=(s == 0), stop=False)
                        pe.matmul(p[:, t * 4:(t + 1) * 4], tri, oh_group[:, t, :], start=(t == 0), stop=True)
                    for s in range(TILES):
                        mm = pe.matmul(p[:, 12:16], ones, oh_group[:, s, :], start=(s == 0), stop=(s == 2))
                    done(mm, "rank")

                    pe.wait_ge(jobs_ready, 1)
                    for i in range(6):
                        bk.wait_drained(pe, ("h2", i))
                    count = pe.value_load(jobs[0:1, 0:1], min_val=4, max_val=6)
                    with pe.Fori(0, count) as job:
                        pe.wait_ge(sel_ready, job + 1)
                        p = begin("selT", job)
                        for t in range(TILES):
                            mm = pe.transpose(p[:, t * P:(t + 1) * P], sel[:, t, :], ident)
                        done(mm, "selT")
                        p = begin("gs", job)
                        for t in range(TILES):
                            mm = pe.matmul(p[:, 0:4], sel[:, t, :], gates4[:, t, :], start=(t == 0), stop=(t == 2))
                        done(mm, "gs")
                        for x in range(2):
                            p = begin(("xg", x), job)
                            for n in range(4):
                                k = 4 * x + n
                                for t in range(TILES):
                                    mm = pe.matmul(p[:, n * P:(n + 1) * P], h2tok[:, t, k * P:(k + 1) * P],
                                                   sel[:, t, :], start=(t == 0), stop=(t == 2))
                            done(mm, ("xg", x))
                        for x in range(2):
                            bk.wait_drained(pe, ("xg", x), job)

                        def gate_up(e):
                            for which, name in enumerate("GU"):
                                i = 3 * e + which
                                wait_loaded(pe, i, job)
                                w = job_slot(i).rearrange("p (k n) -> p k n", k=KT)
                                p = begin((name, e), job)
                                for k in range(KT):
                                    mm = pe.matmul(p[:, :], xg[:, k, :], w[:, k, :], start=(k == 0),
                                                   stop=(k == KT - 1))
                                done(mm, (name, e))

                        def down(e):
                            pe.wait_ge(gated_ready, job * 4 + e + 1)
                            p = begin(("aT", e), job)
                            for f in range(4):
                                mm = pe.transpose(p[:, f * P:(f + 1) * P], act_in[:, e % 2, f * P:(f + 1) * P], ident)
                            done(mm, ("aT", e))
                            bk.wait_drained(pe, ("aT", e), job)
                            wait_loaded(pe, 3 * e + 2, job)
                            w = job_slot(3 * e + 2).rearrange("p (k n) -> p k n", k=4)
                            for f in range(4):
                                for y in range(2):
                                    if e == 0 and f == 0:
                                        begin(("y", y), job)
                                    mm = pe.matmul(ps[bk.bank(("y", y))][:, :], aT[:, e % 2, f * P:(f + 1) * P],
                                                   w[:, f, y * 512:(y + 1) * 512], start=(e == 0 and f == 0),
                                                   stop=(e == 3 and f == 3))
                                    if e == 3 and f == 3 and y == 0:
                                        done(mm, ("y", 0))
                            if e == 3:
                                done(mm, ("y", 1))
                            else:
                                mm.then_inc(down_read, 1)

                        gate_up(0)
                        for e in range(4):
                            if e < 3:
                                gate_up(e + 1)
                            down(e)
                        for y in range(2):
                            bk.wait_drained(pe, ("y", y), job)
                        for m in range(KT):
                            p = begin(("back", m), job)
                            done(pe.matmul(p[:, 0:NT], ysb[:, m * P:(m + 1) * P], selT, start=True, stop=True),
                                 ("back", m))

                @block.scalar
                def _(act):
                    chain = [0]

                    def link(ins):
                        chain[0] += 1
                        ins.then_inc(act_chain, 1)
                        act.wait_ge(act_chain, chain[0])

                    def drain(name, ins):
                        ins.then_inc(drained[bk.bank(name)], 1)

                    def norm(n):
                        for k in range(KT):
                            act.activation(squares[:, k, :], xT[:, k, :], ACT.Square).then_inc(squares_ready, 1)
                        name = ("ss1", "ss2")[n]
                        bk.wait_full(act, name)
                        act.activation(std[:], ps[bk.bank(name)][:, 0:NT], ACT.Sqrt, bias=eps
                                       ).then_inc(drained[bk.bank(name)], 1)
                        for k in range(KT):
                            for j, cols in STREAMS:
                                act.wait_ge(scaled_ready, 2 * (n * KT + k) + j + 1)
                                ins = act.activation(hT[:, k, cols], hT[:, k, cols], ACT.Identity,
                                                     bias=modT[:, 24 * n + k, j:j + 1])
                                if j == 0:
                                    chain[0] += 1
                                    ins.then_inc(act_chain, 1)
                                    act.wait_ge(act_chain, chain[0])
                                else:
                                    ins.then_inc(h_ready, 1)

                    act.wait_ge(vT_ready, 1)
                    act.activation(csil[:].rearrange("p k s -> p s k"),
                                   vT[:, V_C:V_C + 16].rearrange("p (s k) -> p s k", s=2), ACT.Silu
                                   ).then_inc(csil_ready, 1)
                    norm(0)
                    for t in range(TILES):
                        bk.wait_full(act, ("mq", t))
                        drain(("mq", t), act.copy(zqk[:, t, 0:512], ps[bk.bank(("mq", t))][:, :]))
                    act.wait_ge(fabs_ready, 1)
                    link(act.activation(rows[:, 4, :], rows[:, 2, :], ACT.Exp))
                    act.activation(rows[:, 5, :], rows[:, 4, :], ACT.Ln, bias=one[0:64, :]).then_inc(fexp_ready, 1)
                    for t in range(TILES):
                        bk.wait_full(act, ("mk", t))
                        drain(("mk", t), act.copy(zqk[:, t, 512:1024], ps[bk.bank(("mk", t))][:, :]))
                    for t in range(TILES):
                        bk.wait_full(act, ("mv", t))
                        drain(("mv", t), act.copy(vaug[:, t, :, 0:P],
                                                  ps[bk.bank(("mv", t))][:, :].rearrange("p (h d) -> p h d", h=4)))
                    act.wait_ge(rowsin_ready, 1)
                    act.activation(rows[:, 4, P:NT], rows[:, 3, P:NT], ACT.Exp, bias=m0[:, :], scale=-1.0
                                   ).then_inc(rowsout_ready, 1)
                    act.activation(rows[:, 4, 0:P], rows[:, 1, 0:P], ACT.Exp, bias=mend[:, 1:2]
                                   ).then_inc(rowsout_ready, 1)
                    act.activation(rows[:, 5, :], rows[:, 2, :], ACT.Exp, scale=-1.0).then_inc(rowsout_ready, 1)
                    for t in range(TILES):
                        bk.wait_full(act, ("mo", t))
                        drain(("mo", t), act.activation(sigo[:, t, :], ps[bk.bank(("mo", t))][:, :], ACT.Sigmoid))
                    for i in range(10):
                        src = ps[bk.bank(("fm", i))][:, 0:NT]
                        name = ("fm", i)
                        if i in (4, 5):
                            continue
                        bk.wait_full(act, name)
                        if i < 2:
                            drain(name, act.copy(cb[:, i, :], src))
                        elif i < 4:
                            link(act.copy(upad[:, i - 2, 1:129], src[:, 0:P]))
                            drain(name, act.copy(upad[:, i - 2, 130:386], src[:, P:NT]))
                        elif i < 8:
                            drain(name, act.mul(nqT[:, i - 6, :], src, 0.125))
                        else:
                            drain(name, act.copy(nkT[:, i - 8, :], src))
                    bk.wait_full(act, "kvp")
                    drain("kvp", act.copy(kvp[:], ps[bk.bank("kvp")][:, :]))
                    for i in range(2):
                        bk.wait_full(act, ("nv", i))
                        drain(("nv", i), act.copy(nv[:, i], ps[bk.bank(("nv", i))][:, 0:256]))
                    bk.wait_full(act, "rowsA")
                    drain("rowsA", act.copy(tokg[:, 0:6, :], ps[bk.bank("rowsA")][:, 0:384].rearrange("p (n r) -> p n r", n=6)))
                    bk.wait_full(act, "rowsB")
                    drain("rowsB", act.copy(tokg[:, 6:9, :], ps[bk.bank("rowsB")][:, 0:192].rearrange("p (n r) -> p n r", n=3)))
                    bk.wait_full(act, "kc")
                    drain("kc", act.copy(kct[:], ps[bk.bank("kc")][:, 0:256].rearrange("p (n r) -> p n r", n=2)))
                    for i in range(8):
                        bk.wait_full(act, ("qkT", i))
                        drain(("qkT", i), act.copy(hT[:, i, :], ps[bk.bank(("qkT", i))][:, 0:NT]))

                    act.wait_ge(pmax_ready, 1)
                    act.activation(pctx[:], pctx[:], ACT.Exp).then_inc(pexp_ready, 1)

                    def latent_exp(n):
                        act.wait_ge(pmax_ready, n + 2)
                        act.activation(ploc[:, n % 2, :], ploc[:, n % 2, :], ACT.Exp,
                                       bias=small[:, 8 + n:9 + n], accum_out=small[:, 16 + n:17 + n]
                                       ).then_inc(pexp_ready, 1)

                    latent_exp(0)
                    for h in range(4):
                        bk.wait_full(act, ("pTp", h))
                        drain(("pTp", h), act.copy(pT[:, h % 2, 0:P], ps[bk.bank(("pTp", h))][:, 0:P]))
                    for n, (h, q) in enumerate(NA):
                        if n + 1 < len(NA):
                            latent_exp(n + 1)
                        bk.wait_full(act, ("pT", h, q))
                        drain(("pT", h, q), act.copy(pT[:, n % 2, :], ps[bk.bank(("pT", h, q))][:, 0:NT]))
                    for i in range(2):
                        bk.wait_full(act, ("o", i))
                        drain(("o", i), act.copy(mixT[:, 2 + i, :], ps[bk.bank(("o", i))][:, 0:NT]))

                    for dh in range(8):
                        lane = (dh // 4) * 32 + dh % 4
                        tiles_of_s = (0, 1, 2, 1 if dh < 4 else 2)
                        bk.wait_full(act, ("mu", dh))
                        for b in range(4):
                            if b == 0 and dh >= 2:
                                act.wait_ge(score_ready, dh - 1)
                            ins = act.activation(W[:, dh % 2, b * P:(b + 1) * P],
                                                 ps[bk.bank(("mu", dh))][:, b * P:(b + 1) * P], ACT.Exp,
                                                 bias=tokg[:, tiles_of_s[b], lane:lane + 1], scale=-1.0)
                        drain(("mu", dh), ins)
                        bk.wait_full(act, ("int", dh))
                        if dh >= 2:
                            act.wait_ge(total_done, dh - 1)
                        for t in (1, 2):
                            ins = act.activation(inter[:, dh % 2, t, :],
                                                 ps[bk.bank(("int", dh))][:, (t - 1) * 129:t * 129],
                                                 ACT.Copy, scale=tokg[:, 5 + t, lane:lane + 1])
                        drain(("int", dh), ins)
                        if dh >= 1:
                            bk.wait_full(act, ("C", dh - 1))
                            drain(("C", dh - 1), act.copy(cnew[:, dh - 1, :], ps[bk.bank(("C", dh - 1))][:, 0:129]))
                    bk.wait_full(act, ("C", 7))
                    drain(("C", 7), act.copy(cnew[:, 7, :], ps[bk.bank(("C", 7))][:, 0:129]))
                    act.wait_ge(msq_ready, 1)
                    act.activation(head[:, 1, :], head[:, 0, :], ACT.Sqrt, bias=eps, scale=1.0 / P
                                   ).then_inc(hstd_ready, 1)
                    for h in range(4):
                        bk.wait_full(act, ("hT", h))
                        drain(("hT", h), act.copy(mixT[:, 4 + h, :], ps[bk.bank(("hT", h))][:, 0:NT]))

                    for m in range(KT):
                        bk.wait_drained(act, ("wo", m))
                    norm(1)
                    for i in range(6):
                        bk.wait_full(act, ("h2", i))
                        drain(("h2", i), act.copy(h2tok[:, i // 2, (i % 2) * 512:(i % 2 + 1) * 512],
                                                  ps[bk.bank(("h2", i))][:, :]))
                    act.wait_ge(rexp_in, 1)
                    act.activation(r_exp, r_exp, ACT.Exp).then_inc(rexp_ready, 1)

                    act.wait_ge(jobs_ready, 1)
                    count = act.value_load(jobs[0:1, 0:1], min_val=4, max_val=6)
                    with act.Fori(0, count) as job:
                        bk.wait_full(act, "selT", job)
                        drain("selT", act.copy(selT, ps[bk.bank("selT")][:, 0:NT]))
                        bk.wait_full(act, ("xg", 0), job)
                        drain(("xg", 0), act.copy(xg[:, 0:4, :], ps[bk.bank(("xg", 0))][:, :].rearrange("p (k n) -> p k n", k=4)))
                        for e in range(4):
                            bk.wait_full(act, ("G", e), job)
                            if e >= 2:
                                act.wait_ge(gated_ready, job * 4 + e - 1)
                            else:
                                act.wait_ge(gated_ready, job * 4)
                            drain(("G", e), act.activation(sg[:, e % 2, :], ps[bk.bank(("G", e))][:, :], ACT.Silu))
                            bk.wait_full(act, ("aT", e), job)
                            drain(("aT", e), act.copy(aT[:, e % 2, :], ps[bk.bank(("aT", e))][:, :]))
                        bk.wait_full(act, ("y", 0), job)
                        drain(("y", 0), act.copy(ysb[:, 0:512], ps[bk.bank(("y", 0))][:, :]))

                @block.vector
                def _(dve):
                    chain = [0]

                    def link(ins):
                        chain[0] += 1
                        ins.then_inc(dve_chain, 1)
                        dve.wait_ge(dve_chain, chain[0])

                    def drain(name, ins):
                        ins.then_inc(drained[bk.bank(name)], 1)

                    def full_of(name, job=None):
                        bk.wait_full(dve, name, job)
                        return ps[bk.bank(name)]

                    def norm(n):
                        bk.wait_drained(dve, ("ss1", "ss2")[n])
                        link(dve.reciprocal(std[:], std[:]))
                        gain = (gain1, gain2)[n]
                        for k in range(KT):
                            for j, cols in STREAMS:
                                dve.scalar_tensor_tensor(hT[:, k, cols], xT[:, k, cols], gain[:, k, j:j + 1],
                                                         std[:, cols], ALU.mult, ALU.mult
                                                         ).then_inc(scaled_ready, 1)

                    p = full_of("vec")
                    dve.tensor_copy(vT[:], p[:, 0:V_ROWS]).then_inc(drained[bk.bank("vec")], 1)
                    bk.wait_drained(dve, "vec")
                    dve.sem_inc(vT_ready, 1)
                    dve.wait_ge(smalls_loaded, (l + 1) * (16 * SMALLS))
                    dve.tensor_copy(caug[:, :, P], vT[:, V_N0:V_N0 + 8]).then_inc(caug_ready, 1)
                    na_mask = cst[:, C_NAMASK:C_NAMASK + GRID_W]
                    link(dve.tensor_tensor(relb[:].rearrange("p h j w -> p (h j) w"),
                                           relb[:].rearrange("p h j w -> p (h j) w"),
                                           na_mask[:, None, :].broadcast_to((P, 4 * RELBIAS_DIFFS, GRID_W)), ALU.add))
                    p = full_of("mod")
                    drain("mod", dve.tensor_tensor(modT[:], p[:, 0:96].rearrange("p (m s) -> p m s", s=2),
                                                   vT[:, V_BMOD:V_BMOD + 48][:, :, None].broadcast_to((P, 48, 2)), ALU.add))
                    bk.wait_drained(dve, "mod")
                    for g, m0_, v0 in ((gain1, 8, V_LN1), (gain2, 32, V_LN2)):
                        link(dve.scalar_tensor_tensor(g[:], modT[:, m0_:m0_ + 8, :], 1.0,
                                                      vT[:, v0:v0 + 8][:, :, None].broadcast_to((P, 8, 2)),
                                                      ALU.add, ALU.mult))
                    norm(0)

                    p = full_of("gate")
                    for n, c0 in ((1, 0), (0, 8)):
                        for t in range(TILES):
                            ins = dve.tensor_tensor(
                                gpad[:, n, t, :].rearrange("p (d r) -> p d r", d=2)[:, :, 0:4],
                                p[:, t * 16 + c0:t * 16 + c0 + 8].rearrange("p (d h) -> p d h", d=2),
                                gbias[:, c0:c0 + 8].rearrange("p (d h) -> p d h", d=2), ALU.add)
                            if t == 2:
                                ins.then_inc(gpad_ready, 1)
                    dve.wait_ge(gpad_ready, 2)
                    dve.sem_inc(drained[bk.bank("gate")], 1)
                    p = full_of("gT_f")
                    drain("gT_f", dve.tensor_copy(rows[:, 0, :], p[0:64, 0:NT]))
                    p = full_of("gT_i")
                    drain("gT_i", dve.tensor_copy(rows[:, 1, :], p[0:64, 0:NT]))
                    bk.wait_drained(dve, "gT_f")
                    bk.wait_drained(dve, "gT_i")
                    dve.scalar_tensor_tensor(rows[:, 2, :], rows[:, 0, :], -1.0, rows[:, 0, :], ALU.mult, ALU.min
                                             ).then_inc(fabs_ready, 1)
                    dve.wait_ge(fexp_ready, 1)
                    link(dve.scalar_tensor_tensor(rows[:, 0, :], rows[:, 0, :], 0.0, rows[:, 5, :], ALU.min, ALU.subtract))
                    F, B = slice(0, 32), slice(32, 64)
                    segments = ((F, slice(0, P)), (F, slice(P, NT)), (B, slice(P - 1, None, -1)), (B, slice(NT - 1, P - 1, -1)))
                    for n, (r, c) in enumerate(segments):
                        ins = dve.tensor_tensor_scan(rows[r, 2, c], rows[r, 0, c], rows[r, 0, c], 0.0, ALU.add, ALU.bypass)
                        link(ins)
                    link(dve.tensor_tensor(rows[:, 1, :], rows[:, 1, :], rows[:, 2, :], ALU.subtract))
                    for n, (r, c) in enumerate(segments):
                        init = m0[r, 0:1] if n % 2 else 0.0
                        ins = dve.tensor_tensor_scan(rows[r, 3, c], rows[r, 1, c], rows[r, 1, c], init, ALU.max, ALU.bypass)
                        link(ins)
                    for r, last in ((F, P - 1), (B, 0)):
                        dve.tensor_scalar(mend[r, 1:2], rows[r, 3, last:last + 1], -1.0, None, ALU.mult)
                        link(dve.tensor_tensor(mend[r, 2:3], rows[r, 3, last:last + 1], rows[r, 2, last:last + 1], ALU.add))
                    link(dve.tensor_tensor(rows[:, 2, :], rows[:, 2, :], rows[:, 3, :], ALU.add))
                    dve.sem_inc(rowsin_ready, 1)
                    dve.sem_inc(mnew_ready, 1)
                    dve.sem_inc(rowsout_ready, 1)

                    for t in range(TILES):
                        bk.wait_drained(dve, ("mk", t))
                        bk.wait_drained(dve, ("mq", t))
                    for t in (1, 2):
                        z = zqk[:, t, :].rearrange("p (h x y f) -> p h x y f", h=8, x=2, y=2)
                        for h0 in (0, 4):
                            x1, x2 = (z[:, h0:h0 + 4, :, y, :] for y in (0, 1))
                            table = cst[:, C_ROPE + (t - 1) * P:C_ROPE + t * P].rearrange("p (s x f) -> p s x f", s=2, x=2)
                            cos, sin = (table[:, None, s].broadcast_to((P, 4, 2, 32)) for s in (0, 1))
                            tmp = [total[:].rearrange("p b t n -> p (b t n)")[:, n * 256:(n + 1) * 256]
                                   .rearrange("p (h x f) -> p h x f", h=4, x=2) for n in range(3)]
                            dve.tensor_tensor(tmp[0], x1, sin, ALU.mult)
                            dve.tensor_tensor(tmp[1], x2, sin, ALU.mult)
                            link(dve.tensor_tensor(tmp[2], x1, cos, ALU.mult))
                            link(dve.tensor_tensor(x1, tmp[2], tmp[1], ALU.subtract))
                            link(dve.tensor_tensor(tmp[2], x2, cos, ALU.mult))
                            link(dve.tensor_tensor(x2, tmp[2], tmp[0], ALU.add))
                    dve.sem_inc(rope_ready, 1)

                    for i in range(2):
                        bk.wait_drained(dve, ("fm", 2 + i))
                        bk.wait_drained(dve, ("fm", i))
                        p = full_of(("fm", 4 + i))
                        dve.tensor_tensor(upad[:, i, 1:129], upad[:, i, 1:129], p[:, 0:P], ALU.mult)
                        drain(("fm", 4 + i), dve.tensor_tensor(upad[:, i, 130:386], upad[:, i, 130:386], p[:, P:NT], ALU.mult))
                        bk.wait_drained(dve, ("fm", 4 + i))
                        taps = [vT[:, V_CONV + 2 * w + i:V_CONV + 2 * w + i + 1] for w in range(3)]
                        out = ((mixT[:, i, 0:P], 1, P), (mixT[:, i, P:NT], 130, 256))
                        for dst, c0, n in out:
                            link(dve.tensor_scalar(dst, upad[:, i, c0:c0 + n], taps[1], None, ALU.mult))
                        for w, shift in ((0, -1), (2, 1)):
                            for dst, c0, n in out:
                                link(dve.scalar_tensor_tensor(dst, upad[:, i, c0 + shift:c0 + shift + n], taps[w],
                                                              dst, ALU.mult, ALU.add))
                        link(dve.tensor_tensor(mixT[:, i, :], mixT[:, i, :], cb[:, i, :], ALU.mult))
                    dve.sem_inc(conv_ready, 1)

                    pc4 = pctx.rearrange("p (h k) -> p h k", h=4)
                    for odd in range(2):
                        p = full_of(("sp", odd))
                        pair = p[:, 0:256].rearrange("p (h k) -> p h k", h=2)
                        most = small[:, 2 + 2 * odd:4 + 2 * odd]
                        link(dve.tensor_reduce(most, pair, AX.X, ALU.max))
                        drain(("sp", odd), dve.tensor_tensor(pc4[:, odd::2], pair, most[:, :, None].broadcast_to((P, 2, P)),
                                                             ALU.subtract))
                    bk.wait_drained(dve, ("sp", 0))
                    bk.wait_drained(dve, ("sp", 1))
                    dve.sem_inc(pmax_ready, 1)

                    def latent_max(n):
                        h, q = NA[n]
                        p = full_of(("ss", h, q))
                        if n >= 2:
                            bk.wait_full(dve, ("pT", *NA[n - 2]))
                        dve.tensor_tensor(ploc[:, n % 2, 0:256].rearrange("p (j w) -> p j w", j=4),
                                          p[:, 0:256].rearrange("p (j w) -> p j w", j=4),
                                          relb[:, h, 3 - 2 * q:7 - 2 * q, :], ALU.add)
                        drain(("ss", h, q), dve.tensor_copy(ploc[:, n % 2, 256:384], p[:, 256:384]))
                        bk.wait_drained(dve, ("ss", h, q))
                        dve.tensor_reduce(small[:, 8 + n:9 + n], ploc[:, n % 2, :], AX.X, ALU.max, negate=True
                                          ).then_inc(pmax_ready, 1)

                    latent_max(0)
                    dve.wait_ge(pexp_ready, 1)
                    link(dve.tensor_reduce(small[:, 2:6], pc4, AX.X, ALU.add))
                    link(dve.reciprocal(small[:, 2:6], small[:, 2:6]))
                    dve.tensor_tensor(pc4, pc4, small[:, 2:6][:, :, None].broadcast_to((P, 4, P)), ALU.mult
                                      ).then_inc(prob_ready, 1)
                    for n in range(len(NA)):
                        if n + 1 < len(NA):
                            latent_max(n + 1)
                        dve.wait_ge(pexp_ready, n + 2)
                        link(dve.reciprocal(small[:, 24 + n:25 + n], small[:, 16 + n:17 + n]))
                        dve.tensor_scalar(ploc[:, n % 2, :], ploc[:, n % 2, :], small[:, 24 + n:25 + n], None, ALU.mult
                                          ).then_inc(prob_ready, 1)

                    bk.wait_drained(dve, "rowsA")
                    bk.wait_drained(dve, "rowsB")

                    def scores(dh):
                        h, lane = dh % 4, (dh // 4) * 32 + dh % 4
                        bk.wait_drained(dve, ("mu", dh))
                        p = full_of(("kq", dh))
                        if dh >= 2:
                            bk.wait_full(dve, ("C", dh - 2))
                        dve.scalar_tensor_tensor(S[:, dh % 2, :], p[:, :], ISQ, W[:, dh % 2, :], ALU.mult, ALU.mult
                                                 ).then_inc(score_ready, 1)
                        dve.tensor_scalar(kw[:, dh % 2, :], zqk[:, 0, 512 + h * P:512 + (h + 1) * P],
                                          tokg[:, 8, lane:lane + 1], ISQ, ALU.mult, ALU.mult).then_inc(kw_ready, 1)
                        dve.wait_ge(score_ready, dh + 1)
                        dve.sem_inc(drained[bk.bank(("kq", dh))], 1)

                    scores(0)
                    for dh in range(8):
                        h, lane, b = dh % 4, (dh // 4) * 32 + dh % 4, dh % 2
                        if dh < 7:
                            scores(dh + 1)
                        p = full_of(("num", dh))
                        bk.wait_drained(dve, ("int", dh))
                        dve.tensor_copy(total[:, b, 0, :], p[:, 0:129])
                        drain(("num", dh), dve.tensor_tensor(total[:, b, 1:3, :], inter[:, b, 1:3, :],
                                                             p[:, 129:387].rearrange("p (t n) -> p t n", t=2), ALU.add))
                        bk.wait_drained(dve, ("num", dh))
                        dve.sem_inc(total_done, 1)
                        den = total[:, b, :, 128]
                        link(dve.scalar_tensor_tensor(small[:, 32:35], den, -1.0, den, ALU.mult, ALU.max))
                        link(dve.tensor_tensor(small[:, 32:35], small[:, 32:35], tokg[:, 3:6, lane], ALU.max))
                        link(dve.reciprocal(small[:, 32:35], small[:, 32:35]))
                        for t in range(TILES):
                            dst = hsum[:, t, h * P:(h + 1) * P]
                            if dh < 4:
                                ins = dve.tensor_scalar(dst, total[:, b, t, 0:P], small[:, 32 + t:33 + t], None, ALU.mult)
                            else:
                                ins = dve.scalar_tensor_tensor(dst, total[:, b, t, 0:P], small[:, 32 + t:33 + t], dst,
                                                               ALU.mult, ALU.add)
                        link(ins)

                    hs3 = hsum.rearrange("p t (h d) -> p (t h) d", h=4)
                    sq3 = zqk[:, 0:2, :].rearrange("p t n -> p (t n)")[:, 0:1536].rearrange("p (t d) -> p t d", t=12)
                    bk.wait_full(dve, ("C", 7))
                    link(dve.tensor_tensor(sq3, hs3, hs3, ALU.mult))
                    dve.tensor_reduce(head[:, 0, :], sq3, AX.X, ALU.add).then_inc(msq_ready, 1)
                    for t in range(TILES):
                        bk.wait_drained(dve, ("mo", t))
                    link(dve.tensor_tensor(sigo, sigo, gbc[:, None, :].broadcast_to((P, 3, 512)), ALU.mult))
                    dve.wait_ge(hstd_ready, 1)
                    link(dve.reciprocal(head[:, 2, :], head[:, 1, :]))
                    link(dve.tensor_tensor(hs3, hs3, head[:, 2, :][:, :, None].broadcast_to((P, 12, P)), ALU.mult))
                    dve.tensor_tensor(hsum, hsum, sigo, ALU.mult).then_inc(hnorm_ready, 1)

                    def residual(name, gate0, m, p):
                        for j, cols in STREAMS:
                            ins = dve.scalar_tensor_tensor(xT[:, m, cols], p[:, cols], modT[:, gate0 + m, j:j + 1],
                                                           xT[:, m, cols], ALU.mult, ALU.add)
                            if j == 0:
                                yield ins
                        drain(name, ins)

                    for m in range(KT):
                        p = full_of(("wo", m))
                        for ins in residual(("wo", m), 16, m, p):
                            link(ins)
                    for m in range(KT):
                        bk.wait_drained(dve, ("wo", m))
                    norm(1)

                    p = full_of("lg")
                    drain("lg", dve.tensor_tensor(logits, p[:, 0:60].rearrange("p (t n) -> p t n", t=3),
                                                  rbias[:, None, :].broadcast_to((P, 3, 20)), ALU.add))
                    bk.wait_drained(dve, "lg")
                    gl, el = logits[:, :, 0:4], logits[:, :, 4:20]

                    def bc(x, n):
                        return x[:, :, None].broadcast_to((P, 3, n))

                    def first_max(values, best, onehot, prio, n):
                        link(dve.tensor_reduce(best, values, AX.X, ALU.max))
                        link(dve.tensor_tensor(onehot, values, bc(best, n), ALU.is_equal))
                        link(dve.tensor_tensor(onehot, onehot, cst[:, None, prio:prio + n].broadcast_to((P, 3, n)), ALU.mult))
                        link(dve.tensor_reduce(r_tmp, onehot, AX.X, ALU.max))
                        return dve.tensor_tensor(onehot, onehot, bc(r_tmp, n), ALU.is_equal)

                    first_max(gl, g_best, oh_group, C_PRIO4, 4).then_inc(onehot_ready, 1)
                    dve.wait_ge(onehot_ready, 1)
                    el4 = el.rearrange("p t (g e) -> p t g e", g=4)
                    picked4 = picked.rearrange("p t (g e) -> p t g e", g=4)
                    off4 = one1.rearrange("p t (g e) -> p t g e", g=4)
                    ohb = oh_group[:, :, :, None].broadcast_to((P, 3, 4, 4))
                    for t in range(TILES):
                        dve.tensor_tensor(picked4[:, t], el4[:, t], ohb[:, t], ALU.mult)
                        link(dve.tensor_scalar(off4[:, t], ohb[:, t], -1.0, BIG, ALU.add, ALU.mult))
                    link(dve.tensor_tensor(picked, picked, one1, ALU.add))
                    link(first_max(picked, e_best1, one1, C_PRIO16, 16))
                    link(dve.scalar_tensor_tensor(picked, one1, -3.0 * BIG, picked, ALU.mult, ALU.add))
                    link(first_max(picked, e_best2, one2, C_PRIO16, 16))
                    link(dve.tensor_tensor(r_exp[:, :, 0:4], gl, bc(g_best, 4), ALU.subtract))
                    dve.tensor_tensor(r_exp[:, :, 4], e_best2, e_best1, ALU.subtract).then_inc(rexp_in, 1)
                    dve.wait_ge(rexp_ready, 1)
                    link(dve.tensor_reduce(r_tmp, r_exp[:, :, 0:4], AX.X, ALU.add))
                    link(dve.tensor_scalar(r_tmp2, r_exp[:, :, 4], 1.0, None, ALU.add))
                    link(dve.tensor_tensor(r_tmp, r_tmp, r_tmp2, ALU.mult))
                    link(dve.reciprocal(r_tmp, r_tmp))
                    link(dve.tensor_tensor(r_tmp2, r_tmp, r_exp[:, :, 4], ALU.mult))
                    link(dve.tensor_tensor(one1, one1, bc(r_tmp, 16), ALU.mult))
                    link(dve.tensor_tensor(one2, one2, bc(r_tmp2, 16), ALU.mult))
                    link(dve.tensor_tensor(one1, one1, one2, ALU.add))
                    link(dve.tensor_reduce(gates4, one1.rearrange("p t (g e) -> p t e g", g=4), AX.X, ALU.add))
                    p = full_of("rank")
                    link(dve.tensor_copy(rank_s, p[:, 0:16]))
                    dve.sem_inc(drained[bk.bank("rank")], 1)
                    ranks = rank_s[:, 0:12].rearrange("p (t g) -> p t g", t=3)
                    sizes = rank_s[:, 12:16]
                    link(dve.tensor_scalar(extra, sizes, 128.5, None, ALU.is_gt))
                    link(dve.scalar_tensor_tensor(extra, sizes, 256.5, extra, ALU.is_gt, ALU.add))
                    link(dve.tensor_tensor_scan(upto, extra, extra, 0.0, ALU.add, ALU.bypass))
                    link(dve.tensor_tensor(before, upto, extra, ALU.subtract))
                    base = cst[:, C_BASE:C_BASE + 4]
                    link(dve.tensor_scalar(before, before, 128.0, 384.0, ALU.mult, ALU.add))
                    link(dve.tensor_tensor(before, before, base, ALU.subtract))
                    link(dve.tensor_tensor(ranks, ranks, oh_group, ALU.mult))
                    link(dve.tensor_reduce(r_tmp, ranks, AX.X, ALU.add))
                    link(dve.tensor_tensor(ranks, oh_group, before[:, None, :].broadcast_to((P, 3, 4)), ALU.mult))
                    link(dve.tensor_reduce(r_tmp2, ranks, AX.X, ALU.add))
                    link(dve.tensor_scalar(g_best, r_tmp, 127.5, None, ALU.is_gt))
                    link(dve.tensor_tensor(r_tmp2, r_tmp2, g_best, ALU.mult))
                    link(dve.tensor_tensor(r_tmp, r_tmp, r_tmp2, ALU.add))
                    link(dve.tensor_tensor(ranks, oh_group, base[:, None, :].broadcast_to((P, 3, 4)), ALU.mult))
                    link(dve.tensor_reduce(r_tmp2, ranks, AX.X, ALU.add))
                    link(dve.tensor_tensor(slot_of, r_tmp, r_tmp2, ALU.add))
                    link(dve.tensor_scalar(jobs_f[:, 0:1], upto[:, 3:4], 4.0, None, ALU.add))
                    for n in range(2):
                        link(dve.tensor_scalar(rank_s[:, 0:4], upto, n + 0.5, None, ALU.is_lt))
                        link(dve.tensor_reduce(jobs_f[:, 1 + n:2 + n], rank_s[:, 0:4], AX.X, ALU.add))
                    link(dve.tensor_scalar(jobs_f[:, 1:3], jobs_f[:, 1:3], 3.0, None, ALU.min))
                    dve.tensor_copy(jobs[:, 0:3], jobs_f[:, 0:3]).then_inc(jobs_ready, 1)
                    dve.wait_ge(jobs_ready, 1)

                    count = dve.value_load(jobs[0:1, 0:1], min_val=4, max_val=6)
                    with dve.Fori(0, count) as job:
                        dve.sem_clear(job_chain)
                        steps = [0]

                        def step(ins):
                            steps[0] += 1
                            ins.then_inc(job_chain, 1)
                            dve.wait_ge(job_chain, steps[0])

                        for t in range(TILES):
                            step(dve.tensor_scalar(sel[:, t, :], cst[:, C_IOTA:C_IOTA + P], slot_of[:, t:t + 1], None,
                                                   ALU.is_equal))
                        dve.tensor_scalar(slot_of, slot_of, -128.0, None, ALU.add).then_inc(sel_ready, 1)
                        dve.wait_ge(sel_ready, job + 1)
                        p = full_of("gs", job)
                        drain("gs", dve.tensor_copy(gslot[:], p[:, 0:4]))
                        bk.wait_drained(dve, "gs", job)
                        p = full_of(("xg", 1), job)
                        drain(("xg", 1), dve.tensor_copy(xg[:, 4:8, :], p[:, :].rearrange("p (k n) -> p k n", k=4)))
                        for e in range(4):
                            p = full_of(("U", e), job)
                            bk.wait_drained(dve, ("G", e), job)
                            step(dve.scalar_tensor_tensor(act_in[:, e % 2, :], p[:, :], gslot[:, e:e + 1], sg[:, e % 2, :],
                                                          ALU.mult, ALU.mult))
                            dve.sem_inc(drained[bk.bank(("U", e))], 1)
                            dve.sem_inc(gated_ready, 1)
                        p = full_of(("y", 1), job)
                        drain(("y", 1), dve.tensor_copy(ysb[:, 512:1024], p[:, :]))
                        for m in range(KT):
                            p = full_of(("back", m), job)
                            for ins in residual(("back", m), 40, m, p):
                                step(ins)

            nc.all_engine_barrier()
            nums = sorted(s.num for s in layer_sems)
            starts = [n for n in nums if n - 1 not in nums]
            ends = [n + 1 for n in nums if n + 1 not in nums]
            for start, end in zip(starts, ends):
                nc.sync.sem_clear(range(start, end))
            nc.all_engine_barrier()

        fin = hT
        outrow = ring[:, 0:1, 0:3072].rearrange("p a (t d) -> p (a t) d", t=3)
        fin_sq, fin_sum, fin_root, fin_scaled = (sem(n, kept=True) for n in ("fin_sq", "fin_sum", "fin_root", "fin_scaled"))
        fin_turned, fin_copied, fin_stored = (sem(n, kept=True) for n in ("fin_turned", "fin_copied", "fin_stored"))
        with nc.Block() as block:
            @block.scalar
            def _(act):
                act.activation(mixT[:], xT[:], ACT.Square).then_inc(fin_sq, 1)
                act.wait_ge(fin_sum, 1)
                act.activation(std[:], ps[0][:, 0:NT], ACT.Sqrt, bias=eps).then_inc(fin_root, 1)

            @block.tensor
            def _(pe):
                pe.wait_ge(fin_sq, 1)
                for k in range(KT):
                    mm = pe.matmul(ps[0][:, 0:NT], mean, mixT[:, k, :], start=(k == 0), stop=(k == KT - 1))
                mm.then_inc(fin_sum, 1)
                for i in range(6):
                    pe.wait_ge(fin_scaled, 4 * (i % 2) + 4)
                    for n in range(4):
                        mm = pe.transpose(ps[1 + i][:, n * P:(n + 1) * P],
                                          fin[:, (i % 2) * 4 + n, (i // 2) * P:(i // 2 + 1) * P], ident)
                    mm.then_inc(fin_turned, 1)

            @block.vector
            def _(dve):
                dve.wait_ge(fin_root, 1)
                dve.reciprocal(std[:], std[:]).then_inc(fin_root, 1)
                dve.wait_ge(fin_root, 2)
                for k in range(KT):
                    dve.scalar_tensor_tensor(fin[:, k, :], xT[:, k, :], vT[:, V_FINAL + k:V_FINAL + k + 1], std[:],
                                             ALU.mult, ALU.mult).then_inc(fin_scaled, 1)
                for i in range(6):
                    dve.wait_ge(fin_turned, i + 1)
                    dve.tensor_copy(outrow[:, i // 2, (i % 2) * 512:(i % 2 + 1) * 512], ps[1 + i][:, :]
                                    ).then_inc(fin_copied, 1)

            @block.sync
            def _(sp):
                sp.wait_ge(fin_copied, 2)
                sp.dma_start(o["y_prompt"][0], outrow[:, 0, :]).then_inc(fin_stored, 16)
                sp.wait_ge(fin_copied, 6)
                sp.dma_start(o["y_sample"][0].rearrange("(t p) d -> p t d", p=P), outrow[:, 1:3, :]
                             ).then_inc(fin_stored, 16)
                sp.wait_ge(fin_stored, 32)


_OUTS = {
    "y_prompt": (1, 128, 1024), "y_sample": (1, 256, 1024),
    "new_cache_k": (1, 2, 128, 4, 64), "new_cache_v": (1, 2, 128, 4, 64),
    "new_state_C": (1, 2, 2, 4, 128, 128), "new_state_n": (1, 2, 2, 4, 128), "new_state_m": (1, 2, 2, 4),
}


def kernel(**inputs):
    import concourse.bacc as bacc
    from concourse.bass_utils import run_bass_kernel_spmd as run

    nc = bacc.Bacc("TRN2", target_bir_lowering=False, num_devices=1)
    arrays, a, o = {}, {}, {}
    for name, value in {**inputs, "constants": constant_table()}.items():
        value = np.ascontiguousarray(value)
        arrays[f"in_{name}"] = value
        a[name] = nc.dram_tensor(f"in_{name}", value.shape, mybir.dt.from_np(value.dtype), kind="ExternalInput").ap()
    for name, shape in _OUTS.items():
        o[name] = nc.dram_tensor(f"out_{name}", shape, F32, kind="ExternalOutput").ap()
    build(nc, a, o)
    r = run(nc, [arrays], core_ids=[0])
    return tuple(r.results[0][f"out_{name}"] for name in _OUTS)
```

```python
from contextlib import ExitStack

import numpy as np
import concourse.bass as bass
from concourse import mybir

ALU = mybir.AluOpType
ACT = mybir.ActivationFunctionType
F32 = mybir.dt.float32
I32 = mybir.dt.int32
AX = mybir.AxisListType

P = 128
BIG = 1.0e30
GRID_W = 64
WIN_ROWS, WIN_COLS = 8, 16
EPS = 1e-6
SMALLS = 16
RING = 4
BANKS = 8
RELBIAS_DIFFS = 7

C_IDENT, C_MASKF, C_MASKB, C_TRI, C_IOTA, C_ONES, C_MEAN = (P * i for i in range(7))
C_SEL = 7 * P
C_ROPE = C_SEL + 8 * P
C_NAMASK = C_ROPE + 2 * P
C_PRIO4 = C_NAMASK + GRID_W
C_PRIO16 = C_PRIO4 + 4
C_BASE = C_PRIO16 + 16
C_EPS = C_BASE + 4
C_ONE = C_EPS + 1
C_STEP = C_ONE + 1
C_WIDTH = C_STEP + 2

V_LN1, V_LN2, V_BMOD, V_CONV, V_N0, V_C, V_FINAL, V_ROWS = 0, 8, 16, 64, 70, 78, 94, 102

NA = [(h, q) for h in range(4) for q in range(2)]


def mixing_steps(first_layer):
    mods = [("mod", 1, c) for c in range(12)] if first_layer else []
    fill = [("by_token", "mo", t) for t in range(3)] + [("by_feature", i) for i in range(4)]
    steps = [("gates",)]
    steps += [("by_token", "mq", t) for t in range(3)] + [("by_token", "mk", t) for t in range(3)]
    steps += mods[0:1] + [("rope",)] + [("by_feature", i) for i in (6, 7, 4, 5)] + mods[1:2]
    steps += [("by_feature", 8), ("by_feature", 9), ("by_token", "kvp", 0), ("by_token", "nv", 1), ("by_token", "nv", 2)]
    steps += mods[2:3] + [("gate_columns",), ("old_keys",)] + [("by_token", "mv", t) for t in range(3)] + mods[3:4]
    steps += [("context_scores",), ("turn", 0), ("turn", 1), ("turn", 2), ("turn", 3), ("scores", 0), ("turn", 4),
              ("turn", 5), ("turn", 6), ("turn", 7), ("scores", 1), ("context_turn",)]
    del mods[:4]
    for n in range(8):
        steps += [("turn_probs", n)] + ([("scores", n + 2)] if n < 6 else [])
        steps += fill[n:n + 1]
        steps += [("context_values",)] if n == 0 else []
        steps += [("values", n)] + (mods[:1] if n % 2 else [])
        if n % 2:
            del mods[:1]
    steps += [("decay", 0)]
    for dh in range(8):
        steps += ([("decay", dh + 1)] if dh < 7 else []) + mods[:1] + [("read", dh)]
        del mods[:1]
    assert not mods
    return steps


def constant_table():
    t = np.zeros((P, C_WIDTH), np.float32)
    i = np.arange(P)
    t[:, C_IDENT:C_IDENT + P] = np.eye(P)
    t[:, C_MASKF:C_MASKF + P] = np.where(i[:, None] > i[None, :], BIG, 0.0)
    t[:, C_MASKB:C_MASKB + P] = np.where(i[:, None] < i[None, :], BIG, 0.0)
    t[:, C_TRI:C_TRI + P] = i[:, None] < i[None, :]
    t[:, C_IOTA:C_IOTA + P] = i[None, :]
    t[:, C_ONES:C_ONES + P] = 1.0
    t[:, C_MEAN:C_MEAN + P] = 1.0 / 1024
    for dh in range(8):
        t[(dh // 4) * 32 + dh % 4, C_SEL + dh * P:C_SEL + (dh + 1) * P] = 1.0
    nf = 32
    inv = (np.float32(10000.0) ** (-np.arange(nf, dtype=np.float32) / nf)).astype(np.float32)
    for half in range(2):
        tok = half * P + i
        pos = np.stack([tok // GRID_W, tok % GRID_W], -1).astype(np.float32)
        ang = (pos[:, :, None] * inv).astype(np.float32).reshape(P, 2 * nf)
        t[:, C_ROPE + half * P:C_ROPE + half * P + 64] = np.cos(ang)
        t[:, C_ROPE + half * P + 64:C_ROPE + (half + 1) * P] = np.sin(ang)
    col = i % GRID_W
    start = np.clip(col - WIN_COLS // 2, 0, GRID_W - WIN_COLS)
    key = np.arange(GRID_W)
    inside = (key[None, :] >= start[:, None]) & (key[None, :] < start[:, None] + WIN_COLS)
    t[:, C_NAMASK:C_NAMASK + GRID_W] = np.where(inside, 0.0, -BIG)
    t[:, C_PRIO4:C_PRIO4 + 4] = np.arange(4, 0, -1)
    t[:, C_PRIO16:C_PRIO16 + 16] = np.arange(16, 0, -1)
    t[:, C_BASE:C_BASE + 4] = P * np.arange(4)
    t[:, C_EPS] = EPS
    t[:, C_ONE] = 1.0
    t[:, C_STEP:C_STEP + 2] = np.arange(2)
    return t


class Banks:

    def __init__(self, full, drained):
        self.full, self.drained = full, drained
        self.at, self.used, self.per_job = {}, [0] * BANKS, [0] * BANKS
        self.in_job = False

    def place(self, name, bank):
        assert name not in self.at
        self.at[name] = (bank, self.used[bank], self.in_job)
        self.used[bank] += 1
        if self.in_job:
            self.per_job[bank] += 1

    def number(self, name, job):
        bank, n, in_job = self.at[name]
        return bank, (job * self.per_job[bank] + n if in_job else n)

    def wait_free(self, pe, name, job=None):
        bank, n = self.number(name, job)
        if self.at[name][1] > 0 or self.at[name][2]:
            pe.wait_ge(self.drained[bank], n)

    def wait_full(self, eng, name, job=None):
        bank, n = self.number(name, job)
        eng.wait_ge(self.full[bank], n + 1)

    def wait_drained(self, eng, name, job=None):
        bank, n = self.number(name, job)
        eng.wait_ge(self.drained[bank], n + 1)

    def bank(self, name):
        return self.at[name][0]


def place_products(bk, first_layer):
    turn = [0]

    def spread(*names, over=(0, 1, 2, 3, 4, 6, 7)):
        for name in names:
            bk.place(name, over[turn[0] % len(over)])
            turn[0] += 1

    def mod(which, c):
        if c % 4 == 0:
            bk.place(("mod", which, c // 4), 5)
        if c % 4 == 3:
            bk.place(("modT", which, c // 4), 5)

    if first_layer:
        spread(("vec", 0), ("vec", 1))
        for c in range(12):
            mod(0, c)
    spread(("ss", 0))
    before_heads = (0, 1, 2, 3, 4)
    for kind, *args in mixing_steps(first_layer):
        if kind == "gates":
            spread("gates")
        elif kind == "by_token":
            spread(tuple(args), over=before_heads)
        elif kind == "by_feature":
            spread(("fm", *args), over=before_heads)
        elif kind == "mod":
            mod(*args)
        elif kind == "gate_columns":
            spread("rowsA", "rowsB", over=before_heads)
        elif kind == "old_keys":
            spread("old_keys", over=before_heads)
        elif kind == "turn":
            spread(("turn", *args), over=before_heads)
        elif kind == "context_scores":
            spread(("sp", 0), ("sp", 1), over=before_heads)
        elif kind == "scores":
            spread(("scores", *args), over=before_heads)
        elif kind == "context_turn":
            spread("pTc", over=before_heads)
        elif kind == "turn_probs":
            spread(("pT", *args), over=before_heads)
        elif kind == "context_values":
            bk.place(("o", 0), 6)
            bk.place(("o", 1), 7)
        elif kind == "decay":
            spread(("mu", *args), ("kq", *args), ("int", *args))
        elif kind == "read":
            spread(("num", *args), ("C", *args))
    spread(*[("hT", h) for h in range(4)], *[("wo", m) for m in range(8)], ("ss", 1))
    spread("lgT", "lg", *[("h2", i) for i in range(6)], "rank")
    bk.place("gs0", 6)
    bk.place(("xg0", 0), 2)
    bk.place(("xg0", 1), 3)
    bk.in_job = True
    for name, bank in ((("G", 0), 2), (("U", 0), 3), ("selT", 7), (("G", 1), 4), (("U", 1), 5), (("aT", 0), 6),
                       (("y", 0), 0), (("y", 1), 1), (("G", 2), 2), (("U", 2), 3), (("aT", 1), 7),
                       (("G", 3), 4), (("U", 3), 5), (("aT", 2), 6), ("gs", 7), (("xg", 0), 2), (("xg", 1), 3),
                       (("aT", 3), 6)):
        bk.place(name, bank)
    for m in range(8):
        bk.place(("back", m), (4, 5, 7, 6, 0, 1)[m % 6])
    bk.in_job = False


JOB_ORDER = (("G", 0), ("U", 0), ("G", 1), ("U", 1), ("G", 2), ("U", 2), ("D", 0),
             ("G", 3), ("U", 3), ("D", 1), ("D", 2), ("D", 3))


def stream_loads(first_layer):
    loads, mods_read = [], [0]

    def mod(which, c):
        if c % 4 == 3:
            loads.append((("mod", which, c), ("mod", which, c // 4)))
        else:
            mods_read[0] += 1
            loads.append((("mod", which, c), mods_read[0]))

    if first_layer:
        for c in range(12):
            mod(0, c)
    for kind, *args in mixing_steps(first_layer):
        if kind == "mod":
            mod(*args)
        elif kind == "by_token" and args[1] == 0 and args[0] in ("mq", "mk", "mv", "mo"):
            loads.append((("in", args[0]), (args[0], 2)))
        elif kind == "by_feature" and args[0] in (6, 8, 0):
            loads.append((("in", {6: "hq", 8: "kv", 0: "bc"}[args[0]]),
                          {6: ("fm", 5), 8: ("nv", 2), 0: ("fm", 3)}[args[0]]))
    loads += [(("out", 0), ("wo", 3)), (("out", 1), ("wo", 7))]
    return loads


IN_COLUMN = {"bc": 0, "hq": 512, "kv": 1024, "mq": 1536, "mk": 2048, "mv": 2560, "mo": 3072}


class Layer:

    def __init__(self, sem, number):
        self.number = number
        self.first = number == 0

        def s(name):
            return sem(f"{name}_{number}")
        self.bk = Banks([s(f"full{b}") for b in range(BANKS)], [s(f"drained{b}") for b in range(BANKS)])
        place_products(self.bk, self.first)
        self.ring_loaded = [s(f"ring_loaded{r}") for r in range(RING)]
        self.loads = stream_loads(self.first)
        self.index = {name: i for i, (name, _) in enumerate(self.loads)}
        self.mod_read = s("mod_read")
        self.down_read = s("down_read")
        self.smalls_loaded = s("smalls_loaded")
        self.stored = s("stored")
        self.squares_ready = s("squares_ready")
        self.scaled_ready = s("scaled_ready")
        self.h_context = s("h_context")
        self.h_latent = s("h_latent")
        self.wgp_ready = s("wgp_ready")
        self.fabs_ready = s("fabs_ready")
        self.fexp_ready = s("fexp_ready")
        self.rowsin_ready = s("rowsin_ready")
        self.rowsout_ready = s("rowsout_ready")
        self.rope_ready = s("rope_ready")
        self.conv_ready = s("conv_ready")
        self.pmax_ready = s("pmax_ready")
        self.pexp_ready = s("pexp_ready")
        self.prob_ready = s("prob_ready")
        self.caug_ready = s("caug_ready")
        self.score_ready = s("score_ready")
        self.kw_ready = s("kw_ready")
        self.msq_ready = s("msq_ready")
        self.sigo_ready = s("sigo_ready")
        self.hstd_ready = s("hstd_ready")
        self.hnorm_ready = s("hnorm_ready")
        self.onehot_ready = s("onehot_ready")
        self.rexp_in = s("rexp_in")
        self.rexp_ready = s("rexp_ready")
        self.jobs_ready = s("jobs_ready")
        self.sel_ready = s("sel_ready")
        self.gated_ready = s("gated_ready")
        self.x_done = s("x_done")

    def wait_loaded(self, eng, name):
        i = self.index[name]
        eng.wait_ge(self.ring_loaded[i % RING], 16 * (i // RING + 1))

    def buffer(self, name):
        return self.index[name] % RING

    def wait_job_loaded(self, eng, name, job):
        n = len(self.loads) + JOB_ORDER.index(name)
        eng.wait_ge(self.ring_loaded[n % RING], job * (16 * len(JOB_ORDER) // RING) + 16 * (n // RING + 1))

    def job_buffer(self, name):
        return (len(self.loads) + JOB_ORDER.index(name)) % RING


def build(nc, a, o):
    D, FF, NT, TILES, DEPTH = 1024, 512, 384, 3, 2
    KT = D // P
    IN_COLS = a["w_in"].shape[2]
    STREAMS = ((0, slice(0, P)), (1, slice(P, NT)))
    ISQ = 1.0 / float(np.sqrt(128.0))

    with ExitStack() as ctx:
        def sb(name, shape, dt=F32):
            return ctx.enter_context(nc.sbuf_tensor(name, shape, dt))

        def sem(name):
            return ctx.enter_context(nc.semaphore(name))

        xT = sb("xT", [P, KT, NT])
        hT = sb("hT", [P, KT, NT])
        mixT = sb("mixT", [P, KT, NT])
        ring = sb("ring", [P, RING, 4096])
        zqk = sb("zqk", [P, 3, 1024])
        kctx = sb("kctx", [P, 512])
        vaug = sb("vaug", [P, 3, 4, 129])
        arena = sb("arena", [P, 6668])
        kvp = sb("kvp", [P, 512])
        nv = sb("nv", [P, 2, 256])
        cb = sb("cb", [P, 2, NT])
        upad = sb("upad", [P, 2, 388])
        nqT = sb("nqT", [P, 2, NT])
        nkT = sb("nkT", [P, 2, NT])
        cst = sb("cst", [P, C_WIDTH])
        caug = sb("caug", [P, 8, 129])
        cnew = sb("cnew", [P, 8, 129])
        relb = sb("relb", [P, 4, RELBIAS_DIFFS, GRID_W])
        gbc = sb("gbc", [P, 512])
        vT = sb("vT", [P, DEPTH, V_ROWS])
        csil = sb("csil", [P, 8, 32])
        modT = sb("modT", [P, DEPTH, 48, 2])
        gains = sb("gains", [P, DEPTH, 2, 8, 2])
        std = sb("std", [P, NT])
        wgate = sb("wgate", [P, KT, 16])
        wgp = sb("wgp", [P, KT, P])
        wroute = sb("wroute", [P, KT, 20])
        gbias = sb("gbias", [P, 1])
        rbias = sb("rbias", [P, 20])
        m0 = sb("m0", [64, 1])
        rows = mixT[0:64, 2:8, :]
        mend = sb("mend", [64, 4])
        tokg = sb("tokg", [P, 9, 64])
        kct = sb("kct", [P, 2, P])
        cachek = sb("cachek", [P, 256])
        cachev = sb("cachev", [P, 256])
        small = sb("small", [P, 64])
        head = sb("head", [P, 3, 12])
        route = sb("route", [P, 320])
        jobs = sb("jobs", [P, 4], I32)
        gslot = sb("gslot", [P, 4])
        kw = sb("kw", [P, 2, P])

        ident = cst[:, C_IDENT:C_IDENT + P]
        ones = cst[:, C_ONES:C_ONES + P]
        mean = cst[:, C_MEAN:C_MEAN + P]
        eps = cst[:, C_EPS:C_EPS + 1]
        one = cst[:, C_ONE:C_ONE + 1]

        W = arena[:, 0:1024].rearrange("p (b n) -> p b n", b=2)
        S = arena[:, 1024:2048].rearrange("p (b n) -> p b n", b=2)
        inter = arena[:, 2048:2048 + 774].rearrange("p (b t n) -> p b t n", b=2, t=3)
        total = arena[:, 2822:2822 + 774].rearrange("p (b t n) -> p b t n", b=2, t=3)
        sigo = arena[:, 3596:5132].rearrange("p (t n) -> p t n", t=3)
        hsum = arena[:, 5132:6668].rearrange("p (t n) -> p t n", t=3)
        pctx = arena[:, 0:512]
        ploc = arena[:, 512:1280].rearrange("p (b n) -> p b n", b=2)
        pT = arena[:, 1280:2048].rearrange("p (b n) -> p b n", b=2)
        rope_tmp = [arena[:, 5132 + n * 256:5388 + n * 256].rearrange("p (h x f) -> p h x f", h=4, x=2) for n in range(3)]
        modrow = sb("modrow", [P, 512])
        xg = arena[:, 0:1024].rearrange("p (k n) -> p k n", k=KT)
        sg = arena[:, 1024:2048].rearrange("p (b n) -> p b n", b=2)
        act_in = arena[:, 2048:3072].rearrange("p (b n) -> p b n", b=2)
        aT = arena[:, 3072:4096].rearrange("p (b n) -> p b n", b=2)
        ysb = arena[:, 4096:5120]
        selT = arena[:, 5120:5504]
        sel = arena[:, 5504:5888].rearrange("p (t n) -> p t n", t=3)
        lgT = arena[0:20, 5888:5888 + NT]
        h2tok = zqk
        squares = hT
        xrow = ring[:, RING - 1, 0:3072].rearrange("p (t d) -> p t d", t=3)
        vrow = hT[0:V_ROWS, 0:2, 0:P]
        fin_rows = zqk
        cuts = [0]

        def piece(n, pattern=None, **sizes):
            cuts[0] += n
            v = route[:, cuts[0] - n:cuts[0]]
            return v.rearrange(pattern, **sizes) if pattern else v
        logits = piece(60, "p (t n) -> p t n", t=3)
        oh_group = piece(12, "p (t n) -> p t n", t=3)
        gates4 = piece(12, "p (t n) -> p t n", t=3)
        picked = piece(48, "p (t n) -> p t n", t=3)
        one1 = piece(48, "p (t n) -> p t n", t=3)
        one2 = piece(48, "p (t n) -> p t n", t=3)
        r_exp = piece(15, "p (t n) -> p t n", t=3)
        g_best, e_best1, e_best2, r_tmp, r_tmp2, slot_of = (piece(3) for _ in range(6))
        rank_s = piece(16)
        extra, upto, before, jobs_f = (piece(4) for _ in range(4))

        ps = [ctx.enter_context(nc.psum_tensor(f"ps{b}", [P, 512], F32)) for b in range(BANKS)]

        layers = [Layer(sem, n) for n in range(DEPTH)]
        const_loaded, x_loaded, x_turned, x_copied, vecs_loaded = (
            sem(n) for n in ("const_loaded", "x_loaded", "x_turned", "x_copied", "vecs_loaded"))
        set_once, windows_written, csil_ready, vT_ready, mod_ready = (
            sem(n) for n in ("set_once", "windows_written", "csil_ready", "vT_ready", "mod_ready"))
        dve_chain, act_chain, job_chain = (sem(n) for n in ("dve_chain", "act_chain", "job_chain"))
        fin_sq, fin_sum, fin_root, fin_scaled = (sem(n) for n in ("fin_sq", "fin_sum", "fin_root", "fin_scaled"))
        fin_turned, fin_copied, fin_stored = (sem(n) for n in ("fin_turned", "fin_copied", "fin_stored"))
        bias_windows = nc.dram_tensor("bias_windows", (DEPTH, P, 4, RELBIAS_DIFFS, GRID_W), F32).ap()

        TRI_BLOCKS = [(0, 0), (1, 1), (2, 2)]

        def blocks(dh):
            return TRI_BLOCKS + [(1, 2) if dh < 4 else (2, 1)]

        def half(h):
            return slice(64 * (h % 2), 64 * (h % 2) + 64)

        block = ctx.enter_context(nc.Block())

        @block.sync
        def _(sp):
            sp.dma_start(cst[:], a["constants"]).then_inc(const_loaded, 16)
            sp.dma_start(xrow[:, 0, :], a["x_prompt"][0]).then_inc(x_loaded, 16)
            sp.dma_start(xrow[:, 1:3, :], a["x_sample"][0].rearrange("(t p) d -> p t d", p=P)).then_inc(x_loaded, 16)
            jobs_before = None
            for ly in layers:
                bk, n_loads = ly.bk, len(ly.loads)
                w_mod = a["w_mod"].rearrange("l (k p) n -> l p k n", p=P)
                w_in = a["w_in"][ly.number].rearrange("(k p) n -> p k n", p=P)
                w_out = a["w_out"][ly.number].rearrange("(k p) n -> p k n", p=P)

                def job_buffer_free(of, name, job):
                    which, e = name
                    if which != "D":
                        of.bk.wait_full(sp, name, job)
                    elif e < 3:
                        sp.wait_ge(of.down_read, job * 3 + e + 1)
                    else:
                        of.bk.wait_full(sp, ("y", 1), job)

                def load_read(i):
                    last = ly.loads[i][1]
                    if isinstance(last, int):
                        sp.wait_ge(ly.mod_read, last)
                    else:
                        bk.wait_full(sp, last)

                def buffer_free(i):
                    if i >= RING:
                        load_read(i - RING)
                    elif ly.first:
                        if i % RING == RING - 1:
                            sp.wait_ge(x_turned, KT)
                    else:
                        old = layers[ly.number - 1]
                        for name in JOB_ORDER[-RING:]:
                            if old.job_buffer(name) == i % RING:
                                if name in (("D", 1), ("D", 2)):
                                    sp.wait_ge(old.down_read, jobs_before * 3)
                                else:
                                    job_buffer_free(old, name, jobs_before - 1)

                for i, (name, _) in enumerate(ly.loads):
                    buffer_free(i)
                    kind, *which = name
                    if kind == "mod":
                        src = w_mod[which[0], :, :, which[1] * 512:(which[1] + 1) * 512]
                    elif kind == "out":
                        src = w_out[:, :, which[0] * 512:(which[0] + 1) * 512]
                    else:
                        c0 = IN_COLUMN[which[0]]
                        src = w_in[:, :, c0:c0 + 512]
                    sp.dma_start(ring[:, i % RING, :].rearrange("p (k n) -> p k n", k=KT), src
                                 ).then_inc(ly.ring_loaded[i % RING], 16)

                def job_loads(job, group, before=None):
                    for i, (which, e) in enumerate(JOB_ORDER):
                        if i >= RING:
                            job_buffer_free(ly, JOB_ORDER[i - RING], job)
                        elif before is None:
                            load_read(n_loads + i - RING)
                        else:
                            job_buffer_free(ly, JOB_ORDER[i - RING], before)
                        w = a[{"G": "w_gate", "U": "w_up", "D": "w_down"}[which]][ly.number]
                        kt = FF // P if which == "D" else KT
                        b = ly.job_buffer((which, e))
                        sp.dma_start(ring[:, b, :].rearrange("p (k n) -> p k n", k=kt),
                                     w[bass.ds(group * 4 + e, 1)].rearrange("e (k p) n -> p (e k) n", p=P)
                                     ).then_inc(ly.ring_loaded[b], 16)

                job_loads(0, 0)
                with sp.Fori(0, 3) as before:
                    job_loads(before + 1, before + 1, before)
                sp.wait_ge(ly.jobs_ready, 1)
                jobs_before = sp.value_load(jobs[0:1, 0:1], min_val=4, max_val=6)
                with sp.If(jobs_before > 4):
                    with sp.Fori(3, jobs_before - 1) as before:
                        group = sp.value_load(jobs[0:1, bass.ds(before - 2, 1)], min_val=0, max_val=3)
                        job_loads(before + 1, group, before)

            sp.wait_ge(fin_copied, 2)
            sp.dma_start(o["y_prompt"][0], fin_rows[:, 0, :]).then_inc(fin_stored, 16)
            sp.wait_ge(fin_copied, 6)
            sp.dma_start(o["y_sample"][0].rearrange("(t p) d -> p t d", p=P), fin_rows[:, 1:3, :]
                         ).then_inc(fin_stored, 16)
            sp.wait_ge(fin_stored, 32)

        @block.gpsimd
        def _(pool):
            for d in range(DEPTH):
                for first, n, src in (
                        (V_LN1, 8, a["ln1_g"][d].rearrange("(r n) -> r n", n=P)),
                        (V_LN2, 8, a["ln2_g"][d].rearrange("(r n) -> r n", n=P)),
                        (V_BMOD, 48, a["b_mod"][d].rearrange("(r n) -> r n", n=P)),
                        (V_CONV, 6, a["conv_w"][d].rearrange("w (r n) -> (w r) n", n=P)),
                        (V_N0, 8, a["state_n"][0, d].rearrange("r h d -> (r h) d")),
                        (V_C, 8, a["c_ctx"].rearrange("(r n) -> r n", n=P)),
                        (V_C + 8, 8, a["c"][0].rearrange("(r n) -> r n", n=P)),
                        (V_FINAL, 8, a["final_g"].rearrange("(r n) -> r n", n=P))):
                    pool.dma_start(vrow[first:first + n, d, :], src).then_inc(vecs_loaded, 16)

            def small_loads(ly):
                d = ly.number

                def load(dst, src):
                    pool.dma_start(dst, src, allow_slow_non_contiguous=True).then_inc(ly.smalls_loaded, 16)
                load(wgate[:], a["w_in"][d].rearrange("(k p) n -> p k n", p=P)[:, :, IN_COLS - 16:IN_COLS])
                for r in range(2):
                    for way in range(2):
                        row = 64 * r + 32 * way
                        load(gbias[row:row + 4, :], a["ml_gate_b"][d, r, way:way + 1].rearrange("a h -> h a"))
                for way in range(2):
                    load(m0[32 * way:32 * way + 4, :], a["state_m"][0, d, way:way + 1].rearrange("a h -> h a"))
                load(cachek[:], a["cache_k"][0, d].rearrange("t h d -> t (h d)"))
                load(cachev[:], a["cache_v"][0, d].rearrange("t h d -> t (h d)"))
                load(caug[:, :, 0:P], a["state_C"][0, d].rearrange("r h d e -> d (r h) e"))
                load(relb[:], bias_windows[d])
                load(gbc[:], a["ml_norm_g"][d:d + 1].broadcast_to((P, 512)))
                load(wroute[:, :, 0:4], a["w_rg"][d].rearrange("(k p) n -> p k n", p=P))
                load(wroute[:, :, 4:20], a["w_re"][d].rearrange("(k p) n -> p k n", p=P))
                load(rbias[:, 0:4], a["b_rg"][d:d + 1].broadcast_to((P, 4)))
                load(rbias[:, 4:20], a["b_re"][d:d + 1].broadcast_to((P, 16)))

            for d in range(DEPTH):
                for parity in range(2):
                    for h in range(4):
                        base = ((d * 4 + h) * 15 + 4 - parity) * 31 + 15
                        pool.dma_start(bias_windows[d, 64 * parity:64 * parity + 64, h].rearrange("p j w -> j p w"),
                                       bass.AP(a["na_rpb"].tensor, base,
                                               [[31, RELBIAS_DIFFS], [-1, GRID_W], [1, GRID_W]])
                                       ).then_inc(windows_written, 16)
            pool.wait_ge(windows_written, 16 * 8 * DEPTH)
            pool.wait_ge(set_once, 6)
            small_loads(layers[0])
            for ly in layers:
                bk, d = ly.bk, ly.number

                def store(dst, src):
                    pool.dma_start(dst, src, allow_slow_non_contiguous=True).then_inc(ly.stored, 16)
                bk.wait_drained(pool, ("kvp", 0))
                store(o["new_cache_k"][0, d].rearrange("t h d -> t (h d)"), kvp[:, 0:256])
                store(o["new_cache_v"][0, d].rearrange("t h d -> t (h d)"), kvp[:, 256:512])
                pool.wait_ge(ly.rowsin_ready, 1)
                for way in range(2):
                    store(o["new_state_m"][0, d, way:way + 1].rearrange("a h -> h a"), mend[32 * way:32 * way + 4, 2:3])
                for dh in range(8):
                    bk.wait_drained(pool, ("C", dh))
                store(o["new_state_C"][0, d].rearrange("r h d e -> d (r h) e"), cnew[:, :, 0:P])
                store(o["new_state_n"][0, d].rearrange("r h d -> d (r h)"), cnew[:, :, P])
                pool.wait_ge(ly.stored, 16 * 6)
                if d + 1 < DEPTH:
                    pool.wait_ge(ly.jobs_ready, 1)
                    small_loads(layers[d + 1])

        @block.tensor
        def _(pe):
            pe.wait_ge(const_loaded, 16)
            pe.wait_ge(x_loaded, 32)
            for k in range(KT):
                for t in range(TILES):
                    mm = pe.transpose(ps[k][:, t * P:(t + 1) * P], xrow[:, t, k * P:(k + 1) * P], ident)
                mm.then_inc(x_turned, 1)

            for ly in layers:
                bk = ly.bk

                def begin(name, job=None):
                    bk.wait_free(pe, name, job)
                    return ps[bk.bank(name)]

                def done(mm, name):
                    mm.then_inc(bk.full[bk.bank(name)], 1)

                def mod(which, c):
                    ly.wait_loaded(pe, ("mod", which, c))
                    w = ring[:, ly.buffer(("mod", which, c)), :].rearrange("p (k n) -> p k n", k=KT)
                    name = ("mod", which, c // 4)
                    p = begin(name) if c % 4 == 0 else ps[bk.bank(name)]
                    for k in range(KT):
                        for g in range(4):
                            mm = pe.matmul(p[32 * g:32 * g + 32, (c % 4) * P:(c % 4 + 1) * P], csil[:, k, :],
                                           w[:, k, g * P:(g + 1) * P], start=(k == 0), stop=(k == KT - 1))
                    if c % 4 == 3:
                        done(mm, name)
                        bk.wait_drained(pe, name)
                        turned = ("modT", which, c // 4)
                        p = begin(turned)
                        for i in range(4):
                            mm = pe.transpose(p[:, i * P:(i + 1) * P], modrow[:, i * P:(i + 1) * P], ident)
                        done(mm, turned)
                    else:
                        mm.then_inc(ly.mod_read, 1)

                def sum_squares(n):
                    p = begin(("ss", n))
                    for k in range(KT):
                        pe.wait_ge(ly.squares_ready, n * KT + k + 1)
                        mm = pe.matmul(p[:, 0:NT], mean, squares[:, k, :], start=(k == 0), stop=(k == KT - 1))
                    done(mm, ("ss", n))

                def wait_normed(n, k):
                    pe.wait_ge(ly.h_context, n * KT + k + 1)
                    pe.wait_ge(ly.h_latent, n * KT + k + 1)

                def gates():
                    pe.wait_ge(ly.wgp_ready, 1)
                    p = begin("gates")
                    for k in range(KT):
                        wait_normed(0, k)
                        mm = pe.matmul(p[:, 0:NT], wgp[:, k, :], hT[:, k, :], start=(k == 0), stop=(k == KT - 1))
                    done(mm, "gates")

                def by_token(what, t):
                    load = ("in", "kv" if what in ("kvp", "nv") else what)
                    c0, n = (256, 256) if what == "nv" else (0, 512)
                    ly.wait_loaded(pe, load)
                    w = ring[:, ly.buffer(load), :].rearrange("p (k n) -> p k n", k=KT)
                    p = begin((what, t))
                    for k in range(KT):
                        mm = pe.matmul(p[:, 0:n], hT[:, k, t * P:(t + 1) * P], w[:, k, c0:c0 + n],
                                       start=(k == 0), stop=(k == KT - 1))
                    done(mm, (what, t))

                def by_feature(i):
                    load = ("in", ("bc", "hq", "kv")[i // 4])
                    ly.wait_loaded(pe, load)
                    w = ring[:, ly.buffer(load), :].rearrange("p (k n) -> p k n", k=KT)
                    p = begin(("fm", i))
                    for k in range(KT):
                        mm = pe.matmul(p[:, 0:NT], w[:, k, (i % 4) * P:(i % 4 + 1) * P], hT[:, k, :],
                                       start=(k == 0), stop=(k == KT - 1))
                    done(mm, ("fm", i))

                def gate_columns():
                    pe.wait_ge(ly.rowsout_ready, 3)
                    p = begin("rowsA")
                    for n, r in enumerate((1, 5)):
                        for t in range(TILES):
                            mm = pe.transpose(p[:, (3 * n + t) * 64:(3 * n + t + 1) * 64],
                                              rows[:, r, t * P:(t + 1) * P], ident[0:64, 0:64])
                    done(mm, "rowsA")
                    p = begin("rowsB")
                    for n, t in enumerate((1, 2, 0)):
                        mm = pe.transpose(p[:, n * 64:(n + 1) * 64], rows[:, 4, t * P:(t + 1) * P],
                                          ident[0:64, 0:64])
                    done(mm, "rowsB")

                def old_keys():
                    pe.wait_ge(ly.smalls_loaded, 16 * SMALLS)
                    p = begin("old_keys")
                    for i in range(2):
                        mm = pe.transpose(p[:, i * P:(i + 1) * P], cachek[:, i * P:(i + 1) * P], ident)
                    done(mm, "old_keys")

                def turn(i):
                    pe.wait_ge(ly.rope_ready, 1)
                    p = begin(("turn", i))
                    for t in range(TILES):
                        mm = pe.transpose(p[:, t * P:(t + 1) * P], zqk[:, t, i * P:(i + 1) * P], ident)
                    done(mm, ("turn", i))

                def context_scores():
                    bk.wait_drained(pe, ("fm", 7))
                    bk.wait_drained(pe, ("fm", 8))
                    bk.wait_drained(pe, ("fm", 9))
                    bk.wait_drained(pe, "old_keys")
                    for odd in range(2):
                        p = begin(("sp", odd))
                        for i in range(2):
                            mm = pe.matmul(p[:, i * P:(i + 1) * P], nqT[half(odd), i, 0:P],
                                           nkT[half(odd), i, 0:P], start=True, stop=True)
                        done(mm, ("sp", odd))

                def scores(n):
                    h, q = NA[n]
                    p = begin(("scores", n))
                    qs = nqT[half(h), h // 2, (1 + q) * P:(2 + q) * P]
                    pe.matmul(p[:, 0:256], qs, nkT[half(h), h // 2, P:NT], start=True, stop=True)
                    done(pe.matmul(p[:, 256:384], qs, kct[half(h), h // 2, :], start=True, stop=True), ("scores", n))

                def context_turn():
                    pe.wait_ge(ly.prob_ready, 1)
                    p = begin("pTc")
                    for h in range(4):
                        mm = pe.transpose(p[:, h * P:(h + 1) * P], pctx[:, h * P:(h + 1) * P], ident)
                    done(mm, "pTc")

                def turn_probs(n):
                    pe.wait_ge(ly.prob_ready, n + 2)
                    p = begin(("pT", n))
                    for i in range(3):
                        mm = pe.transpose(p[:, i * P:(i + 1) * P], ploc[:, n % 2, i * P:(i + 1) * P], ident)
                    done(mm, ("pT", n))

                def context_values():
                    bk.wait_drained(pe, "pTc")
                    for i in range(2):
                        begin(("o", i))
                    for h in range(4):
                        pe.matmul(ps[bk.bank(("o", h // 2))][half(h), 0:P], kvp[:, 256 + h * 64:256 + (h + 1) * 64],
                                  pctx[:, h * P:(h + 1) * P], start=True, stop=True)

                def values(n):
                    h, q = NA[n]
                    bk.wait_drained(pe, ("pT", n))
                    for i in range(3):
                        v = nv[:, i] if i < 2 else cachev[:]
                        mm = pe.matmul(ps[bk.bank(("o", h // 2))][half(h), (1 + q) * P:(2 + q) * P],
                                       v[:, h * 64:(h + 1) * 64], pT[:, n % 2, i * P:(i + 1) * P],
                                       start=(i == 0), stop=(i == 2))
                    if n % 4 == 3:
                        done(mm, ("o", n // 4))

                def decay(dh):
                    h = dh % 4
                    if dh == 0:
                        bk.wait_drained(pe, ("turn", 7))
                        bk.wait_drained(pe, ("turn", 6))
                        pe.wait_ge(ly.caug_ready, 1)
                    p = begin(("mu", dh))
                    sel_row = cst[0:64, C_SEL + dh * P:C_SEL + (dh + 1) * P]
                    mask = C_MASKF if dh < 4 else C_MASKB
                    off = blocks(dh)[3][1]
                    pe.matmul(p[:, 0:NT], sel_row, rows[:, 3, :], start=True, stop=False, skip_group_check=True)
                    for b in range(3):
                        pe.matmul(p[:, b * P:(b + 1) * P], ident, cst[:, mask:mask + P], start=False,
                                  stop=True, skip_group_check=True)
                    done(pe.matmul(p[:, NT:512], sel_row, rows[:, 3, off * P:(off + 1) * P], start=True,
                                   stop=True, skip_group_check=True), ("mu", dh))
                    p = begin(("kq", dh))
                    for b, (s, t) in enumerate(blocks(dh)):
                        mm = pe.matmul(p[:, b * P:(b + 1) * P], zqk[:, s, (4 + h) * P:(5 + h) * P],
                                       zqk[:, t, h * P:(h + 1) * P], start=True, stop=True)
                    done(mm, ("kq", dh))
                    p = begin(("int", dh))
                    for t in (1, 2):
                        mm = pe.matmul(p[:, (t - 1) * 129:t * 129], zqk[:, t, h * P:(h + 1) * P],
                                       caug[:, dh, :], start=True, stop=True)
                    done(mm, ("int", dh))

                def read(dh):
                    h = dh % 4
                    pe.wait_ge(ly.score_ready, dh + 1)
                    p = begin(("num", dh))
                    for t in range(TILES):
                        own = [b for b, (_, to) in enumerate(blocks(dh)) if to == t]
                        for n, b in enumerate(own):
                            mm = pe.matmul(p[:, t * 129:(t + 1) * 129], S[:, dh % 2, b * P:(b + 1) * P],
                                           vaug[:, blocks(dh)[b][0], h, :], start=(n == 0), stop=(n == len(own) - 1))
                    done(mm, ("num", dh))
                    pe.wait_ge(ly.kw_ready, dh + 1)
                    p = begin(("C", dh))
                    done(pe.matmul(p[:, 0:129], kw[:, dh % 2, :], vaug[:, 0, h, :], start=True, stop=True), ("C", dh))

                if ly.first:
                    pe.wait_ge(vecs_loaded, 16 * 8 * DEPTH)
                    pe.wait_ge(x_copied, KT)
                    for d in range(DEPTH):
                        p = begin(("vec", d))
                        done(pe.transpose(p[:, 0:V_ROWS], vrow[:, d, :], ident[0:V_ROWS, 0:V_ROWS]), ("vec", d))
                    pe.wait_ge(csil_ready, 1)
                    for c in range(12):
                        mod(0, c)
                sum_squares(0)
                steps = {"gates": gates, "by_token": by_token, "by_feature": by_feature, "mod": mod,
                         "gate_columns": gate_columns, "old_keys": old_keys, "turn": turn,
                         "context_scores": context_scores, "scores": scores, "context_turn": context_turn,
                         "turn_probs": turn_probs, "context_values": context_values, "values": values,
                         "decay": decay, "read": read}
                for kind, *args in mixing_steps(ly.first):
                    if kind in steps:
                        steps[kind](*args)

                pe.wait_ge(ly.hnorm_ready, 1)
                for h in range(4):
                    p = begin(("hT", h))
                    for t in range(TILES):
                        mm = pe.transpose(p[:, t * P:(t + 1) * P], hsum[:, t, h * P:(h + 1) * P], ident)
                    done(mm, ("hT", h))

                pe.wait_ge(ly.conv_ready, 1)
                for i in range(2):
                    bk.wait_drained(pe, ("o", i))
                for h in range(4):
                    bk.wait_drained(pe, ("hT", h))
                for m in range(KT):
                    ly.wait_loaded(pe, ("out", m // 4))
                    w = ring[:, ly.buffer(("out", m // 4)), :].rearrange("p (k n) -> p k n", k=KT)
                    p = begin(("wo", m))
                    for k in range(KT):
                        mm = pe.matmul(p[:, 0:NT], w[:, k, (m % 4) * P:(m % 4 + 1) * P], mixT[:, k, :],
                                       start=(k == 0), stop=(k == KT - 1))
                    done(mm, ("wo", m))

                sum_squares(1)

                p = begin("lgT")
                for k in range(KT):
                    wait_normed(1, k)
                    mm = pe.matmul(p[0:20, 0:NT], wroute[:, k, :], hT[:, k, :], start=(k == 0), stop=(k == KT - 1))
                done(mm, "lgT")
                bk.wait_drained(pe, "lgT")
                p = begin("lg")
                for t in range(TILES):
                    mm = pe.transpose(p[:, t * 20:(t + 1) * 20], lgT[:, t * P:(t + 1) * P], ident[0:20, 0:20])
                done(mm, "lg")
                for i in range(6):
                    t, upper = i // 2, i % 2
                    p = begin(("h2", i))
                    for n in range(4):
                        mm = pe.transpose(p[:, n * P:(n + 1) * P], hT[:, upper * 4 + n, t * P:(t + 1) * P], ident)
                    done(mm, ("h2", i))
                pe.wait_ge(ly.onehot_ready, 1)
                p = begin("rank")
                tri = cst[:, C_TRI:C_TRI + P]
                for t in range(TILES):
                    for s in range(t):
                        pe.matmul(p[:, t * 4:(t + 1) * 4], ones, oh_group[:, s, :], start=(s == 0), stop=False)
                    pe.matmul(p[:, t * 4:(t + 1) * 4], tri, oh_group[:, t, :], start=(t == 0), stop=True)
                for s in range(TILES):
                    mm = pe.matmul(p[:, 12:16], ones, oh_group[:, s, :], start=(s == 0), stop=(s == 2))
                done(mm, "rank")

                def gather(names, job=None):
                    p = begin(names[0], job)
                    for t in range(TILES):
                        mm = pe.matmul(p[:, 0:4], sel[:, t, :], gates4[:, t, :], start=(t == 0), stop=(t == 2))
                    done(mm, names[0])
                    for x in range(2):
                        p = begin(names[1 + x], job)
                        for n in range(4):
                            k = 4 * x + n
                            for t in range(TILES):
                                mm = pe.matmul(p[:, n * P:(n + 1) * P], h2tok[:, t, k * P:(k + 1) * P],
                                               sel[:, t, :], start=(t == 0), stop=(t == 2))
                        done(mm, names[1 + x])

                for i in range(6):
                    bk.wait_drained(pe, ("h2", i))
                pe.wait_ge(ly.sel_ready, 1)
                gather(("gs0", ("xg0", 0), ("xg0", 1)))
                for x in range(2):
                    bk.wait_drained(pe, ("xg0", x))
                pe.wait_ge(ly.jobs_ready, 1)
                count = pe.value_load(jobs[0:1, 0:1], min_val=4, max_val=6)
                with pe.Fori(0, count) as job:
                    def gate_up(e):
                        for which in "GU":
                            name = (which, e)
                            ly.wait_job_loaded(pe, name, job)
                            w = ring[:, ly.job_buffer(name), :].rearrange("p (k n) -> p k n", k=KT)
                            p = begin(name, job)
                            for k in range(KT):
                                mm = pe.matmul(p[:, :], xg[:, k, :], w[:, k, :], start=(k == 0), stop=(k == KT - 1))
                            done(mm, name)

                    def turn_hidden(e):
                        pe.wait_ge(ly.gated_ready, job * 4 + e + 1)
                        p = begin(("aT", e), job)
                        for f in range(4):
                            mm = pe.transpose(p[:, f * P:(f + 1) * P], act_in[:, e % 2, f * P:(f + 1) * P], ident)
                        done(mm, ("aT", e))

                    def down(e):
                        bk.wait_drained(pe, ("aT", e), job)
                        ly.wait_job_loaded(pe, ("D", e), job)
                        w = ring[:, ly.job_buffer(("D", e)), :].rearrange("p (k n) -> p k n", k=4)
                        for y in range(2):
                            if e == 0:
                                begin(("y", y), job)
                            for f in range(4):
                                mm = pe.matmul(ps[bk.bank(("y", y))][:, :], aT[:, e % 2, f * P:(f + 1) * P],
                                               w[:, f, y * 512:(y + 1) * 512], start=(e == 0 and f == 0),
                                               stop=(e == 3 and f == 3))
                            if e == 3:
                                done(mm, ("y", y))
                        if e < 3:
                            mm.then_inc(ly.down_read, 1)

                    bk.wait_free(pe, ("G", 0), job)
                    bk.wait_free(pe, ("U", 0), job)
                    gate_up(0)
                    p = begin("selT", job)
                    for t in range(TILES):
                        mm = pe.transpose(p[:, t * P:(t + 1) * P], sel[:, t, :], ident)
                    done(mm, "selT")
                    gate_up(1)
                    turn_hidden(0)
                    gate_up(2)
                    down(0)
                    turn_hidden(1)
                    gate_up(3)
                    down(1)
                    turn_hidden(2)
                    pe.wait_ge(ly.sel_ready, job + 2)
                    gather(("gs", ("xg", 0), ("xg", 1)), job)
                    turn_hidden(3)
                    down(2)
                    down(3)
                    bk.wait_drained(pe, "selT", job)
                    for y in range(2):
                        bk.wait_drained(pe, ("y", y), job)
                    for m in range(KT):
                        p = begin(("back", m), job)
                        done(pe.matmul(p[:, 0:NT], ysb[:, m * P:(m + 1) * P], selT, start=True, stop=True), ("back", m))

            pe.wait_ge(fin_sq, 1)
            for k in range(KT):
                mm = pe.matmul(ps[0][:, 0:NT], mean, mixT[:, k, :], start=(k == 0), stop=(k == KT - 1))
            mm.then_inc(fin_sum, 1)
            for i in range(6):
                pe.wait_ge(fin_scaled, 4 * (i % 2) + 4)
                for n in range(4):
                    mm = pe.transpose(ps[1 + i][:, n * P:(n + 1) * P],
                                      hT[:, (i % 2) * 4 + n, (i // 2) * P:(i // 2 + 1) * P], ident)
                mm.then_inc(fin_turned, 1)

        @block.scalar
        def _(act):
            chain = [0]

            def link(ins):
                chain[0] += 1
                ins.then_inc(act_chain, 1)
                act.wait_ge(act_chain, chain[0])

            act.wait_ge(set_once, 6)
            act.wait_ge(vT_ready, 1)
            act.activation(csil[:, :, 0:2].rearrange("p k s -> p s k"),
                           vT[:, 0, V_C:V_C + 16].rearrange("p (s k) -> p s k", s=2), ACT.Silu
                           ).then_inc(csil_ready, 1)
            act.wait_ge(x_copied, KT)
            for ly in layers:
                bk, L = ly.bk, ly.number

                def drain(name, ins):
                    ins.then_inc(bk.drained[bk.bank(name)], 1)

                def full_of(name, job=None):
                    bk.wait_full(act, name, job)
                    return ps[bk.bank(name)]

                def norm(n):
                    for k in range(KT):
                        if n == 1:
                            bk.wait_drained(act, ("wo", k))
                        act.activation(squares[:, k, :], xT[:, k, :], ACT.Square).then_inc(ly.squares_ready, 1)
                    p = full_of(("ss", n))
                    drain(("ss", n), act.activation(std[:], p[:, 0:NT], ACT.Sqrt, bias=eps))
                    cols = STREAMS[0][1]
                    for k in range(KT):
                        act.wait_ge(ly.scaled_ready, n * KT + k + 1)
                        act.activation(hT[:, k, cols], hT[:, k, cols], ACT.Identity,
                                       scale=gains[:, L, n, k, 0:1], bias=modT[:, L, 24 * n + k, 0:1]
                                       ).then_inc(ly.h_context, 1)

                def gates():
                    act.wait_ge(ly.fabs_ready, 1)
                    link(act.activation(rows[:, 4, :], rows[:, 2, :], ACT.Exp))
                    act.activation(rows[:, 5, :], rows[:, 4, :], ACT.Ln, bias=one[0:64, :]).then_inc(ly.fexp_ready, 1)

                def gates_end():
                    act.wait_ge(ly.rowsin_ready, 1)
                    act.activation(rows[:, 4, P:NT], rows[:, 3, P:NT], ACT.Exp, bias=m0[:, :], scale=-1.0
                                   ).then_inc(ly.rowsout_ready, 1)
                    act.activation(rows[:, 4, 0:P], rows[:, 1, 0:P], ACT.Exp, bias=mend[:, 1:2]
                                   ).then_inc(ly.rowsout_ready, 1)
                    act.activation(rows[:, 5, :], rows[:, 2, :], ACT.Exp, scale=-1.0).then_inc(ly.rowsout_ready, 1)

                def by_token(what, t):
                    p = full_of((what, t))
                    if what == "kvp" and not ly.first:
                        act.wait_ge(layers[L - 1].stored, 16 * 6)
                    if what == "mq":
                        ins = act.copy(zqk[:, t, 0:512], p[:, :])
                    elif what == "mk":
                        if t == 0:
                            act.copy(kctx[:], p[:, :])
                        ins = act.copy(zqk[:, t, 512:1024], p[:, :])
                    elif what == "mv":
                        ins = act.copy(vaug[:, t, :, 0:P], p[:, :].rearrange("p (h d) -> p h d", h=4))
                    elif what == "mo":
                        ins = act.copy(sigo[:, t, :], p[:, :])
                    elif what == "kvp":
                        ins = act.copy(kvp[:], p[:, :])
                    else:
                        ins = act.copy(nv[:, t - 1], p[:, 0:256])
                    drain((what, t), ins)
                    if (what, t) == ("mk", 0):
                        gates_end()

                def by_feature(i):
                    if i in (2, 3):
                        return
                    p = full_of(("fm", i))
                    if i < 2:
                        ins = act.copy(cb[:, i, :], p[:, 0:NT])
                    elif i < 6:
                        act.copy(upad[:, i - 4, 1:129], p[:, 0:P])
                        ins = act.copy(upad[:, i - 4, 130:386], p[:, P:NT])
                    elif i < 8:
                        ins = act.mul(nqT[:, i - 6, :], p[:, 0:NT], 0.125)
                    else:
                        ins = act.copy(nkT[:, i - 8, :], p[:, 0:NT])
                    drain(("fm", i), ins)

                def gate_columns():
                    p = full_of("rowsA")
                    drain("rowsA", act.copy(tokg[:, 0:6, :], p[:, 0:384].rearrange("p (n r) -> p n r", n=6)))
                    p = full_of("rowsB")
                    drain("rowsB", act.copy(tokg[:, 6:9, :], p[:, 0:192].rearrange("p (n r) -> p n r", n=3)))

                def old_keys():
                    p = full_of("old_keys")
                    drain("old_keys", act.copy(kct[:], p[:, 0:256].rearrange("p (n r) -> p n r", n=2)))

                def turn(i):
                    p = full_of(("turn", i))
                    drain(("turn", i), act.copy(zqk[:, :, i * P:(i + 1) * P], p[:, 0:NT].rearrange("p (t n) -> p t n", t=3)))

                def context_scores():
                    act.wait_ge(ly.pmax_ready, 1)
                    act.activation(pctx, pctx, ACT.Exp).then_inc(ly.pexp_ready, 1)

                def scores(n):
                    act.wait_ge(ly.pmax_ready, n + 2)
                    act.activation(ploc[:, n % 2, :], ploc[:, n % 2, :], ACT.Exp,
                                   bias=small[:, 8 + n:9 + n], accum_out=small[:, 16 + n:17 + n]
                                   ).then_inc(ly.pexp_ready, 1)

                def context_turn():
                    p = full_of("pTc")
                    drain("pTc", act.copy(pctx, p[:, :]))

                def turn_probs(n):
                    p = full_of(("pT", n))
                    drain(("pT", n), act.copy(pT[:, n % 2, :], p[:, 0:NT]))

                def values(n):
                    if n % 4 == 3:
                        p = full_of(("o", n // 4))
                        drain(("o", n // 4), act.copy(mixT[:, 2 + n // 4, :], p[:, 0:NT]))

                def decay(dh):
                    lane = (dh // 4) * 32 + dh % 4
                    tiles_of_s = (0, 1, 2, 1 if dh < 4 else 2)
                    p = full_of(("mu", dh))
                    if dh >= 2:
                        act.wait_ge(ly.score_ready, dh - 1)
                    for b in range(4):
                        ins = act.activation(W[:, dh % 2, b * P:(b + 1) * P], p[:, b * P:(b + 1) * P], ACT.Exp,
                                             bias=tokg[:, tiles_of_s[b], lane:lane + 1], scale=-1.0)
                    drain(("mu", dh), ins)
                    p = full_of(("int", dh))
                    if dh >= 2:
                        bk.wait_drained(act, ("num", dh - 2))
                    for t in (1, 2):
                        ins = act.activation(inter[:, dh % 2, t, :], p[:, (t - 1) * 129:t * 129], ACT.Copy,
                                             scale=tokg[:, 5 + t, lane:lane + 1])
                    drain(("int", dh), ins)

                def read(dh):
                    p = full_of(("C", dh))
                    drain(("C", dh), act.copy(cnew[:, dh, :], p[:, 0:129]))

                norm(0)
                steps = {"gates": gates, "by_token": by_token, "by_feature": by_feature,
                         "gate_columns": gate_columns, "old_keys": old_keys, "turn": turn,
                         "context_scores": context_scores, "scores": scores, "context_turn": context_turn,
                         "turn_probs": turn_probs, "values": values, "decay": decay, "read": read}
                for kind, *args in mixing_steps(ly.first):
                    if kind in steps:
                        steps[kind](*args)

                act.activation(sigo, sigo, ACT.Sigmoid).then_inc(ly.sigo_ready, 1)
                act.wait_ge(ly.msq_ready, 1)
                act.activation(head[:, 1, :], head[:, 0, :], ACT.Sqrt, bias=eps, scale=1.0 / P
                               ).then_inc(ly.hstd_ready, 1)
                for h in range(4):
                    p = full_of(("hT", h))
                    drain(("hT", h), act.copy(mixT[:, 4 + h, :], p[:, 0:NT]))
                norm(1)
                p = full_of("lgT")
                drain("lgT", act.copy(lgT, p[0:20, 0:NT]))
                for i in range(6):
                    p = full_of(("h2", i))
                    drain(("h2", i), act.copy(h2tok[:, i // 2, (i % 2) * 512:(i % 2 + 1) * 512], p[:, :]))
                act.wait_ge(ly.rexp_in, 1)
                act.activation(r_exp, r_exp, ACT.Exp).then_inc(ly.rexp_ready, 1)

                def half_gathered(name, job=None):
                    p = full_of(name, job)
                    drain(name, act.copy(xg[:, 0:4, :], p[:, :].rearrange("p (k n) -> p k n", k=4)))

                half_gathered(("xg0", 0))
                act.wait_ge(ly.jobs_ready, 1)
                count = act.value_load(jobs[0:1, 0:1], min_val=4, max_val=6)
                with act.Fori(0, count) as job:
                    def silu(e):
                        p = full_of(("G", e), job)
                        act.wait_ge(ly.gated_ready, job * 4 + (e - 1 if e > 1 else 0))
                        drain(("G", e), act.activation(sg[:, e % 2, :], p[:, :], ACT.Silu))

                    def turned(e):
                        p = full_of(("aT", e), job)
                        drain(("aT", e), act.copy(aT[:, e % 2, :], p[:, :]))

                    silu(0)
                    p = full_of("selT", job)
                    drain("selT", act.copy(selT, p[:, 0:NT]))
                    silu(1)
                    turned(0)
                    silu(2)
                    turned(1)
                    silu(3)
                    turned(2)
                    half_gathered(("xg", 0), job)
                    turned(3)
                    p = full_of(("y", 0), job)
                    drain(("y", 0), act.copy(ysb[:, 0:512], p[:, :]))
                act.wait_ge(ly.x_done, 1)

            act.activation(mixT[:], xT[:], ACT.Square).then_inc(fin_sq, 1)
            act.wait_ge(fin_sum, 1)
            act.activation(std[:], ps[0][:, 0:NT], ACT.Sqrt, bias=eps).then_inc(fin_root, 1)

        @block.vector
        def _(dve):
            chain = [0]

            def link(ins):
                chain[0] += 1
                ins.then_inc(dve_chain, 1)
                dve.wait_ge(dve_chain, chain[0])

            dve.memset(upad[:], 0.0).then_inc(set_once, 1)
            dve.memset(wgp[:], 0.0).then_inc(set_once, 1)
            dve.memset(vaug[:, :, :, 128:129], 1.0).then_inc(set_once, 1)
            dve.memset(m0[:], 0.0).then_inc(set_once, 1)
            dve.memset(gbias[:], 0.0).then_inc(set_once, 1)
            dve.memset(csil[:], 0.0).then_inc(set_once, 1)
            for k in range(KT):
                dve.wait_ge(x_turned, k + 1)
                dve.tensor_copy(xT[:, k, :], ps[k][:, 0:NT]).then_inc(x_copied, 1)
            for ly in layers:
                bk, L = ly.bk, ly.number

                def drain(name, ins):
                    ins.then_inc(bk.drained[bk.bank(name)], 1)

                def full_of(name, job=None):
                    bk.wait_full(dve, name, job)
                    return ps[bk.bank(name)]

                def wide(x, n):
                    return x[:, :, None].broadcast_to((P, x.shape[1], n))

                def mod(which, c):
                    if c % 4 < 3:
                        return
                    q = c // 4
                    p = full_of(("mod", which, q))
                    drain(("mod", which, q), dve.tensor_copy(modrow[:], p[:, :]))
                    p = full_of(("modT", which, q))
                    drain(("modT", which, q), dve.tensor_tensor(
                        modT[:, which, 16 * q:16 * q + 16, :], p[:, :].rearrange("p (m r) -> p m r", r=32)[:, :, 0:2],
                        wide(vT[:, which, V_BMOD + 16 * q:V_BMOD + 16 * q + 16], 2), ALU.add))
                    bk.wait_drained(dve, ("modT", which, q))
                    if q == 2:
                        for n, m_first, v0 in ((0, 8, V_LN1), (1, 32, V_LN2)):
                            dve.scalar_tensor_tensor(gains[:, which, n], modT[:, which, m_first:m_first + 8, :], 1.0,
                                                     wide(vT[:, which, v0:v0 + 8], 2), ALU.add, ALU.mult
                                                     ).then_inc(mod_ready, 1)

                def norm(n):
                    bk.wait_drained(dve, ("ss", n))
                    link(dve.reciprocal(std[:], std[:]))
                    cols = STREAMS[1][1]
                    for k in range(KT + 1):
                        if k < KT:
                            dve.tensor_tensor(hT[:, k, :], xT[:, k, :], std[:], ALU.mult).then_inc(ly.scaled_ready, 1)
                        if k > 0:
                            dve.wait_ge(ly.scaled_ready, n * KT + k)
                            dve.tensor_scalar(hT[:, k - 1, cols], hT[:, k - 1, cols], gains[:, L, n, k - 1, 1:2],
                                              modT[:, L, 24 * n + k - 1, 1:2], ALU.mult, ALU.add
                                              ).then_inc(ly.h_latent, 1)

                def gates():
                    p = full_of("gates")
                    dve.tensor_scalar(rows[:, 0, :], p[64:128, 0:NT], gbias[64:128, :], None, ALU.add)
                    drain("gates", dve.tensor_scalar(rows[:, 1, :], p[0:64, 0:NT], gbias[0:64, :], None, ALU.add))
                    bk.wait_drained(dve, "gates")
                    dve.scalar_tensor_tensor(rows[:, 2, :], rows[:, 0, :], -1.0, rows[:, 0, :], ALU.mult, ALU.min
                                             ).then_inc(ly.fabs_ready, 1)
                    dve.wait_ge(ly.fexp_ready, 1)
                    link(dve.scalar_tensor_tensor(rows[:, 0, :], rows[:, 0, :], 0.0, rows[:, 5, :], ALU.min, ALU.subtract))
                    F, B = slice(0, 32), slice(32, 64)
                    segments = ((F, slice(0, P)), (F, slice(P, NT)), (B, slice(P - 1, None, -1)),
                                (B, slice(NT - 1, P - 1, -1)))
                    for r, c in segments:
                        ins = dve.tensor_tensor_scan(rows[r, 2, c], rows[r, 0, c], rows[r, 0, c], 0.0, ALU.add, ALU.bypass)
                    link(ins)
                    link(dve.tensor_tensor(rows[:, 1, :], rows[:, 1, :], rows[:, 2, :], ALU.subtract))
                    for n, (r, c) in enumerate(segments):
                        init = m0[r, 0:1] if n % 2 else 0.0
                        ins = dve.tensor_tensor_scan(rows[r, 3, c], rows[r, 1, c], rows[r, 1, c], init, ALU.max, ALU.bypass)
                    link(ins)
                    if not ly.first:
                        dve.wait_ge(layers[L - 1].stored, 16 * 6)
                    for r, last in ((F, P - 1), (B, 0)):
                        dve.tensor_scalar(mend[r, 1:2], rows[r, 3, last:last + 1], -1.0, None, ALU.mult)
                        ins = dve.tensor_tensor(mend[r, 2:3], rows[r, 3, last:last + 1], rows[r, 2, last:last + 1], ALU.add)
                    link(ins)
                    dve.tensor_tensor(rows[:, 2, :], rows[:, 2, :], rows[:, 3, :], ALU.add).then_inc(ly.rowsin_ready, 1)

                def rope():
                    for t in range(TILES):
                        bk.wait_drained(dve, ("mk", t))
                        bk.wait_drained(dve, ("mq", t))
                    for t in (1, 2):
                        z = zqk[:, t, :].rearrange("p (h x y f) -> p h x y f", h=8, x=2, y=2)
                        for h0 in (0, 4):
                            x1, x2 = (z[:, h0:h0 + 4, :, y, :] for y in (0, 1))
                            table = cst[:, C_ROPE + (t - 1) * P:C_ROPE + t * P].rearrange("p (s x f) -> p s x f", s=2, x=2)
                            cos, sin = (table[:, None, s].broadcast_to((P, 4, 2, 32)) for s in (0, 1))
                            tmp = rope_tmp
                            dve.tensor_tensor(tmp[0], x1, sin, ALU.mult)
                            dve.tensor_tensor(tmp[1], x2, sin, ALU.mult)
                            link(dve.tensor_tensor(tmp[2], x1, cos, ALU.mult))
                            link(dve.tensor_tensor(x1, tmp[2], tmp[1], ALU.subtract))
                            link(dve.tensor_tensor(tmp[2], x2, cos, ALU.mult))
                            ins = dve.tensor_tensor(x2, tmp[2], tmp[0], ALU.add)
                            if (t, h0) == (2, 4):
                                ins.then_inc(ly.rope_ready, 1)
                            else:
                                link(ins)

                def by_feature(i):
                    if i not in (2, 3):
                        return
                    c = i - 2
                    bk.wait_drained(dve, ("fm", 4 + c))
                    p = full_of(("fm", i))
                    dve.tensor_tensor(upad[:, c, 1:129], upad[:, c, 1:129], p[:, 0:P], ALU.mult)
                    drain(("fm", i), dve.tensor_tensor(upad[:, c, 130:386], upad[:, c, 130:386], p[:, P:NT], ALU.mult))
                    bk.wait_drained(dve, ("fm", i))
                    taps = [vT[:, L, V_CONV + 2 * w + c:V_CONV + 2 * w + c + 1] for w in range(3)]
                    out = ((mixT[:, c, 0:P], 1, P), (mixT[:, c, P:NT], 130, 256))
                    for dst, c0, n in out:
                        ins = dve.tensor_scalar(dst, upad[:, c, c0:c0 + n], taps[1], None, ALU.mult)
                    link(ins)
                    for w, shift in ((0, -1), (2, 1)):
                        for dst, c0, n in out:
                            ins = dve.scalar_tensor_tensor(dst, upad[:, c, c0 + shift:c0 + shift + n], taps[w],
                                                           dst, ALU.mult, ALU.add)
                        link(ins)
                    bk.wait_drained(dve, ("fm", c))
                    dve.tensor_tensor(mixT[:, c, :], mixT[:, c, :], cb[:, c, :], ALU.mult).then_inc(ly.conv_ready, 1)

                pc4 = pctx.rearrange("p (h k) -> p h k", h=4)

                def context_scores():
                    for odd in range(2):
                        p = full_of(("sp", odd))
                        pair = p[:, 0:256].rearrange("p (h k) -> p h k", h=2)
                        most = small[:, 2 + 2 * odd:4 + 2 * odd]
                        link(dve.tensor_reduce(most, pair, AX.X, ALU.max))
                        drain(("sp", odd), dve.tensor_tensor(pc4[:, odd::2], pair, wide(most, P), ALU.subtract))
                    bk.wait_drained(dve, ("sp", 0))
                    bk.wait_drained(dve, ("sp", 1))
                    dve.sem_inc(ly.pmax_ready, 1)

                def scores(n):
                    h, q = NA[n]
                    p = full_of(("scores", n))
                    if n >= 2:
                        bk.wait_full(dve, ("pT", n - 2))
                    dve.tensor_tensor(ploc[:, n % 2, 0:256].rearrange("p (j w) -> p j w", j=4),
                                      p[:, 0:256].rearrange("p (j w) -> p j w", j=4),
                                      relb[:, h, 3 - 2 * q:7 - 2 * q, :], ALU.add)
                    drain(("scores", n), dve.tensor_copy(ploc[:, n % 2, 256:384], p[:, 256:384]))
                    bk.wait_drained(dve, ("scores", n))
                    dve.tensor_reduce(small[:, 8 + n:9 + n], ploc[:, n % 2, :], AX.X, ALU.max, negate=True
                                      ).then_inc(ly.pmax_ready, 1)

                def context_turn():
                    dve.wait_ge(ly.pexp_ready, 1)
                    link(dve.tensor_reduce(small[:, 2:6], pc4, AX.X, ALU.add))
                    link(dve.reciprocal(small[:, 2:6], small[:, 2:6]))
                    dve.tensor_tensor(pc4, pc4, wide(small[:, 2:6], P), ALU.mult).then_inc(ly.prob_ready, 1)

                def turn_probs(n):
                    dve.wait_ge(ly.pexp_ready, n + 2)
                    link(dve.reciprocal(small[:, 24 + n:25 + n], small[:, 16 + n:17 + n]))
                    dve.tensor_scalar(ploc[:, n % 2, :], ploc[:, n % 2, :], small[:, 24 + n:25 + n], None, ALU.mult
                                      ).then_inc(ly.prob_ready, 1)

                def decay(dh):
                    h, lane = dh % 4, (dh // 4) * 32 + dh % 4
                    bk.wait_drained(dve, ("mu", dh))
                    p = full_of(("kq", dh))
                    if dh >= 2:
                        bk.wait_full(dve, ("C", dh - 2))
                    dve.scalar_tensor_tensor(S[:, dh % 2, :], p[:, :], ISQ, W[:, dh % 2, :], ALU.mult, ALU.mult
                                             ).then_inc(ly.score_ready, 1)
                    dve.tensor_scalar(kw[:, dh % 2, :], kctx[:, h * P:(h + 1) * P],
                                      tokg[:, 8, lane:lane + 1], ISQ, ALU.mult, ALU.mult).then_inc(ly.kw_ready, 1)
                    dve.wait_ge(ly.score_ready, dh + 1)
                    dve.sem_inc(bk.drained[bk.bank(("kq", dh))], 1)

                def read(dh):
                    h, lane, b = dh % 4, (dh // 4) * 32 + dh % 4, dh % 2
                    p = full_of(("num", dh))
                    bk.wait_drained(dve, ("int", dh))
                    dve.tensor_copy(total[:, b, 0, :], p[:, 0:129])
                    drain(("num", dh), dve.tensor_tensor(total[:, b, 1:3, :], inter[:, b, 1:3, :],
                                                         p[:, 129:387].rearrange("p (t n) -> p t n", t=2), ALU.add))
                    bk.wait_drained(dve, ("num", dh))
                    den = total[:, b, :, 128]
                    link(dve.scalar_tensor_tensor(small[:, 32:35], den, -1.0, den, ALU.mult, ALU.max))
                    link(dve.tensor_tensor(small[:, 32:35], small[:, 32:35], tokg[:, 3:6, lane], ALU.max))
                    link(dve.reciprocal(small[:, 32:35], small[:, 32:35]))
                    for t in range(TILES):
                        dst = hsum[:, t, h * P:(h + 1) * P]
                        if dh < 4:
                            ins = dve.tensor_scalar(dst, total[:, b, t, 0:P], small[:, 32 + t:33 + t], None, ALU.mult)
                        else:
                            ins = dve.scalar_tensor_tensor(dst, total[:, b, t, 0:P], small[:, 32 + t:33 + t], dst,
                                                           ALU.mult, ALU.add)
                    if dh >= 3:
                        link(ins)

                if ly.first:
                    for d in range(DEPTH):
                        p = full_of(("vec", d))
                        drain(("vec", d), dve.tensor_copy(vT[:, d, :], p[:, 0:V_ROWS]))
                    bk.wait_drained(dve, ("vec", 0))
                    bk.wait_drained(dve, ("vec", 1))
                    dve.sem_inc(vT_ready, 1)
                    for c in range(12):
                        mod(0, c)
                dve.wait_ge(ly.smalls_loaded, 16 * SMALLS)
                dve.tensor_copy(wgp[:].rearrange("p k (g r) -> p k g r", g=4)[:, :, :, 0:4],
                                wgate[:].rearrange("p k (g r) -> p k g r", g=4)).then_inc(ly.wgp_ready, 1)
                dve.tensor_copy(caug[:, :, P], vT[:, L, V_N0:V_N0 + 8]).then_inc(ly.caug_ready, 1)
                rel3 = relb[:].rearrange("p h j w -> p (h j) w")
                na_mask = cst[:, C_NAMASK:C_NAMASK + GRID_W]
                link(dve.tensor_tensor(rel3, rel3, na_mask[:, None, :].broadcast_to((P, 4 * RELBIAS_DIFFS, GRID_W)), ALU.add))
                dve.wait_ge(mod_ready, 2 * (L + 1))
                norm(0)
                steps = {"gates": gates, "mod": mod, "rope": rope, "by_feature": by_feature,
                         "context_scores": context_scores, "scores": scores, "context_turn": context_turn,
                         "turn_probs": turn_probs, "decay": decay, "read": read}
                for kind, *args in mixing_steps(ly.first):
                    if kind == "decay" and args[0] == 0:
                        bk.wait_drained(dve, "rowsA")
                        bk.wait_drained(dve, "rowsB")
                    if kind in steps:
                        steps[kind](*args)

                hs3 = hsum.rearrange("p t (h d) -> p (t h) d", h=4)
                sq3 = zqk[:, 0:2, :].rearrange("p t n -> p (t n)")[:, 0:1536].rearrange("p (t d) -> p t d", t=12)
                bk.wait_full(dve, ("C", 7))
                link(dve.tensor_tensor(sq3, hs3, hs3, ALU.mult))
                dve.tensor_reduce(head[:, 0, :], sq3, AX.X, ALU.add).then_inc(ly.msq_ready, 1)
                dve.wait_ge(ly.sigo_ready, 1)
                link(dve.tensor_tensor(sigo, sigo, gbc[:, None, :].broadcast_to((P, 3, 512)), ALU.mult))
                dve.wait_ge(ly.hstd_ready, 1)
                link(dve.reciprocal(head[:, 2, :], head[:, 1, :]))
                link(dve.tensor_tensor(hs3, hs3, wide(head[:, 2, :], P), ALU.mult))
                dve.tensor_tensor(hsum, hsum, sigo, ALU.mult).then_inc(ly.hnorm_ready, 1)

                def residual(name, gate0, m, p):
                    for j, cols in STREAMS:
                        ins = dve.scalar_tensor_tensor(xT[:, m, cols], p[:, cols], modT[:, L, gate0 + m, j:j + 1],
                                                       xT[:, m, cols], ALU.mult, ALU.add)
                    drain(name, ins)

                for m in range(KT):
                    residual(("wo", m), 16, m, full_of(("wo", m)))
                for m in range(KT):
                    bk.wait_drained(dve, ("wo", m))
                norm(1)

                p = full_of("lg")
                drain("lg", dve.tensor_tensor(logits, p[:, 0:60].rearrange("p (t n) -> p t n", t=3),
                                              rbias[:, None, :].broadcast_to((P, 3, 20)), ALU.add))
                bk.wait_drained(dve, "lg")
                gl, el = logits[:, :, 0:4], logits[:, :, 4:20]

                def first_max(values, best, onehot, prio, n):
                    link(dve.tensor_reduce(best, values, AX.X, ALU.max))
                    link(dve.tensor_tensor(onehot, values, wide(best, n), ALU.is_equal))
                    link(dve.tensor_tensor(onehot, onehot, cst[:, None, prio:prio + n].broadcast_to((P, 3, n)), ALU.mult))
                    link(dve.tensor_reduce(r_tmp, onehot, AX.X, ALU.max))
                    return dve.tensor_tensor(onehot, onehot, wide(r_tmp, n), ALU.is_equal)

                first_max(gl, g_best, oh_group, C_PRIO4, 4).then_inc(ly.onehot_ready, 1)
                dve.wait_ge(ly.onehot_ready, 1)
                el4 = el.rearrange("p t (g e) -> p t g e", g=4)
                picked4 = picked.rearrange("p t (g e) -> p t g e", g=4)
                off4 = one1.rearrange("p t (g e) -> p t g e", g=4)
                ohb = oh_group[:, :, :, None].broadcast_to((P, 3, 4, 4))
                for t in range(TILES):
                    dve.tensor_tensor(picked4[:, t], el4[:, t], ohb[:, t], ALU.mult)
                    ins = dve.tensor_scalar(off4[:, t], ohb[:, t], -1.0, BIG, ALU.add, ALU.mult)
                link(ins)
                link(dve.tensor_tensor(picked, picked, one1, ALU.add))
                link(first_max(picked, e_best1, one1, C_PRIO16, 16))
                link(dve.scalar_tensor_tensor(picked, one1, -3.0 * BIG, picked, ALU.mult, ALU.add))
                link(first_max(picked, e_best2, one2, C_PRIO16, 16))
                link(dve.tensor_tensor(r_exp[:, :, 0:4], gl, wide(g_best, 4), ALU.subtract))
                dve.tensor_tensor(r_exp[:, :, 4], e_best2, e_best1, ALU.subtract).then_inc(ly.rexp_in, 1)
                p = full_of("rank")
                drain("rank", dve.tensor_copy(rank_s, p[:, 0:16]))
                bk.wait_drained(dve, "rank")
                ranks = rank_s[:, 0:12].rearrange("p (t g) -> p t g", t=3)
                sizes = rank_s[:, 12:16]
                base = cst[:, C_BASE:C_BASE + 4]
                link(dve.tensor_scalar(extra, sizes, 128.5, None, ALU.is_gt))
                link(dve.scalar_tensor_tensor(extra, sizes, 256.5, extra, ALU.is_gt, ALU.add))
                link(dve.tensor_tensor_scan(upto, extra, extra, 0.0, ALU.add, ALU.bypass))
                link(dve.tensor_tensor(before, upto, extra, ALU.subtract))
                link(dve.tensor_scalar(before, before, 128.0, 384.0, ALU.mult, ALU.add))
                dve.tensor_tensor(before, before, base, ALU.subtract)
                link(dve.tensor_tensor(ranks, ranks, oh_group, ALU.mult))
                link(dve.tensor_reduce(r_tmp, ranks, AX.X, ALU.add))
                link(dve.tensor_tensor(ranks, oh_group, before[:, None, :].broadcast_to((P, 3, 4)), ALU.mult))
                dve.tensor_reduce(r_tmp2, ranks, AX.X, ALU.add)
                link(dve.tensor_scalar(g_best, r_tmp, 127.5, None, ALU.is_gt))
                link(dve.tensor_tensor(r_tmp2, r_tmp2, g_best, ALU.mult))
                dve.tensor_tensor(r_tmp, r_tmp, r_tmp2, ALU.add)
                link(dve.tensor_tensor(ranks, oh_group, base[:, None, :].broadcast_to((P, 3, 4)), ALU.mult))
                link(dve.tensor_reduce(r_tmp2, ranks, AX.X, ALU.add))
                link(dve.tensor_tensor(slot_of, r_tmp, r_tmp2, ALU.add))

                def select():
                    for t in range(TILES):
                        ins = dve.tensor_scalar(sel[:, t, :], cst[:, C_IOTA:C_IOTA + P], slot_of[:, t:t + 1], None,
                                                ALU.is_equal)
                    return ins

                link(select())
                link(dve.tensor_scalar(slot_of, slot_of, -128.0, None, ALU.add))
                dve.wait_ge(ly.rexp_ready, 1)
                dve.tensor_reduce(r_tmp, r_exp[:, :, 0:4], AX.X, ALU.add)
                link(dve.tensor_scalar(r_tmp2, r_exp[:, :, 4], 1.0, None, ALU.add))
                link(dve.tensor_tensor(r_tmp, r_tmp, r_tmp2, ALU.mult))
                link(dve.reciprocal(r_tmp, r_tmp))
                link(dve.tensor_tensor(r_tmp2, r_tmp, r_exp[:, :, 4], ALU.mult))
                dve.tensor_tensor(one1, one1, wide(r_tmp, 16), ALU.mult)
                link(dve.tensor_tensor(one2, one2, wide(r_tmp2, 16), ALU.mult))
                link(dve.tensor_tensor(one1, one1, one2, ALU.add))
                dve.tensor_reduce(gates4, one1.rearrange("p t (g e) -> p t e g", g=4), AX.X, ALU.add
                                  ).then_inc(ly.sel_ready, 1)
                link(dve.tensor_scalar(jobs_f[:, 0:1], upto[:, 3:4], 4.0, None, ALU.add))
                for n in range(2):
                    link(dve.tensor_scalar(rank_s[:, 0:4], upto, n + 0.5, None, ALU.is_lt))
                    link(dve.tensor_reduce(jobs_f[:, 1 + n:2 + n], rank_s[:, 0:4], AX.X, ALU.add))
                link(dve.tensor_scalar(jobs_f[:, 1:3], jobs_f[:, 1:3], 3.0, None, ALU.min))
                dve.tensor_copy(jobs[:, 0:3], jobs_f[:, 0:3]).then_inc(ly.jobs_ready, 1)
                dve.wait_ge(ly.jobs_ready, 1)

                def gathered(names, job=None):
                    p = full_of(names[0], job)
                    drain(names[0], dve.tensor_copy(gslot[:], p[:, 0:4]))
                    p = full_of(names[1], job)
                    drain(names[1], dve.tensor_copy(xg[:, 4:8, :], p[:, :].rearrange("p (k n) -> p k n", k=4)))

                gathered(("gs0", ("xg0", 1)))
                bk.wait_drained(dve, "gs0")
                bk.wait_drained(dve, ("xg0", 1))
                count = dve.value_load(jobs[0:1, 0:1], min_val=4, max_val=6)
                with dve.Fori(0, count) as job:
                    dve.sem_clear(job_chain)
                    steps_in_job = [0]

                    def step(ins):
                        steps_in_job[0] += 1
                        ins.then_inc(job_chain, 1)
                        dve.wait_ge(job_chain, steps_in_job[0])

                    def gated(e):
                        p = full_of(("U", e), job)
                        bk.wait_drained(dve, ("G", e), job)
                        step(dve.scalar_tensor_tensor(act_in[:, e % 2, :], p[:, :], gslot[:, e:e + 1], sg[:, e % 2, :],
                                                      ALU.mult, ALU.mult))
                        dve.sem_inc(bk.drained[bk.bank(("U", e))], 1)
                        dve.sem_inc(ly.gated_ready, 1)

                    gated(0)
                    bk.wait_full(dve, "selT", job)
                    step(select())
                    step(dve.tensor_scalar(slot_of, slot_of, -128.0, None, ALU.add))
                    dve.sem_inc(ly.sel_ready, 1)
                    gated(1)
                    gated(2)
                    gated(3)
                    gathered(("gs", ("xg", 1)), job)
                    p = full_of(("y", 1), job)
                    drain(("y", 1), dve.tensor_copy(ysb[:, 512:1024], p[:, :]))
                    for m in range(KT):
                        residual(("back", m), 40, m, full_of(("back", m), job))
                    bk.wait_drained(dve, ("back", KT - 1), job)
                dve.sem_inc(ly.x_done, 1)

            dve.wait_ge(fin_root, 1)
            dve.reciprocal(std[:], std[:]).then_inc(fin_root, 1)
            dve.wait_ge(fin_root, 2)
            for k in range(KT):
                dve.scalar_tensor_tensor(hT[:, k, :], xT[:, k, :], vT[:, 0, V_FINAL + k:V_FINAL + k + 1], std[:],
                                         ALU.mult, ALU.mult).then_inc(fin_scaled, 1)
            for i in range(6):
                dve.wait_ge(fin_turned, i + 1)
                dve.tensor_copy(fin_rows[:, i // 2, (i % 2) * 512:(i % 2 + 1) * 512], ps[1 + i][:, :]
                                ).then_inc(fin_copied, 1)


_OUTS = {
    "y_prompt": (1, 128, 1024), "y_sample": (1, 256, 1024),
    "new_cache_k": (1, 2, 128, 4, 64), "new_cache_v": (1, 2, 128, 4, 64),
    "new_state_C": (1, 2, 2, 4, 128, 128), "new_state_n": (1, 2, 2, 4, 128), "new_state_m": (1, 2, 2, 4),
}


def kernel(**inputs):
    import concourse.bacc as bacc
    from concourse.bass_utils import run_bass_kernel_spmd as run

    nc = bacc.Bacc("TRN2", target_bir_lowering=False, num_devices=1)
    arrays, a, o = {}, {}, {}
    for name, value in {**inputs, "constants": constant_table()}.items():
        value = np.ascontiguousarray(value)
        arrays[f"in_{name}"] = value
        a[name] = nc.dram_tensor(f"in_{name}", value.shape, mybir.dt.from_np(value.dtype), kind="ExternalInput").ap()
    for name, shape in _OUTS.items():
        o[name] = nc.dram_tensor(f"out_{name}", shape, F32, kind="ExternalOutput").ap()
    build(nc, a, o)
    r = run(nc, [arrays], core_ids=[0])
    return tuple(r.results[0][f"out_{name}"] for name in _OUTS)
```

```python
from contextlib import ExitStack

import numpy as np
import concourse.bass as bass
from concourse import mybir

ALU = mybir.AluOpType
ACT = mybir.ActivationFunctionType
F32 = mybir.dt.float32
F32R = mybir.dt.float32r
I32 = mybir.dt.int32
AX = mybir.AxisListType

P = 128
BIG = 1.0e30
GRID_W = 64
WIN_COLS = 16
EPS = 1e-6
GATE_LOADS, SMALLS = 7, 8
RING = 4
HALF = 2048
RAW = 6
AHEAD = 3
BANKS = 8
LAYERS = 2
RELBIAS_DIFFS = 7

C_IDENT, C_MASKF, C_MASKB, C_TRI, C_IOTA, C_ONES, C_MEAN = (P * i for i in range(7))
C_SEL = 7 * P
C_ROPE = C_SEL + 8 * P
C_NAMASK = C_ROPE + 2 * P
C_PRIO4 = C_NAMASK + GRID_W
C_PRIO16 = C_PRIO4 + 4
C_BASE = C_PRIO16 + 16
C_EPS = C_BASE + 4
C_ONE = C_EPS + 1
C_WIDTH = C_ONE + 1

V_LN1, V_LN2, V_BMOD, V_CONV, V_N0, V_C, V_FINAL, V_ROWS = 0, 8, 16, 64, 70, 78, 94, 102

NA = [(h, q) for h in range(4) for q in range(2)]


def mixing_steps(layer):
    mods = [("mod", layer, c) for c in range(4, 12)]
    mods += [("mod", layer + 1, c) for c in range(4)] if layer + 1 < LAYERS else []
    fill = [("by_token", "mo", t) for t in range(3)] + [("by_feature", i) for i in range(4)]
    steps = [("gates",)]
    steps += [("by_token", "mq", t) for t in range(3)] + [("by_token", "mk", t) for t in range(3)]
    steps += mods[0:1] + [("rope",)] + [("by_feature", i) for i in (6, 7, 4, 5)] + mods[1:2]
    steps += [("by_feature", 8), ("by_feature", 9), ("by_token", "kvp", 0), ("by_token", "nv", 1), ("by_token", "nv", 2)]
    steps += mods[2:3] + [("gate_columns",), ("old_keys",)] + [("by_token", "mv", t) for t in range(3)] + mods[3:4]
    steps += [("context_scores",), ("turn", 0), ("turn", 1), ("turn", 2), ("turn", 3), ("scores", 0), ("turn", 4),
              ("turn", 5), ("turn", 6), ("turn", 7), ("scores", 1), ("context_turn",)]
    del mods[:4]
    for n in range(8):
        steps += [("turn_probs", n)] + ([("scores", n + 2)] if n < 6 else [])
        steps += fill[n:n + 1]
        steps += [("context_values",)] if n == 0 else []
        steps += [("values", n)] + (mods[:1] if n % 2 else [])
        if n % 2:
            del mods[:1]
    steps += [("decay", 0)]
    for dh in range(8):
        steps += ([("decay", dh + 1)] if dh < 7 else []) + mods[:1] + [("read", dh)]
        del mods[:1]
    assert not mods
    return steps


def constant_table():
    t = np.zeros((P, C_WIDTH), np.float32)
    i = np.arange(P)
    t[:, C_IDENT:C_IDENT + P] = np.eye(P)
    t[:, C_MASKF:C_MASKF + P] = np.where(i[:, None] > i[None, :], BIG, 0.0)
    t[:, C_MASKB:C_MASKB + P] = np.where(i[:, None] < i[None, :], BIG, 0.0)
    t[:, C_TRI:C_TRI + P] = i[:, None] < i[None, :]
    t[:, C_IOTA:C_IOTA + P] = i[None, :]
    t[:, C_ONES:C_ONES + P] = 1.0
    t[:, C_MEAN:C_MEAN + P] = 1.0 / 1024
    for dh in range(8):
        t[(dh // 4) * 32 + dh % 4, C_SEL + dh * P:C_SEL + (dh + 1) * P] = 1.0
    nf = 32
    inv = (np.float32(10000.0) ** (-np.arange(nf, dtype=np.float32) / nf)).astype(np.float32)
    for half in range(2):
        tok = half * P + i
        pos = np.stack([tok // GRID_W, tok % GRID_W], -1).astype(np.float32)
        ang = (pos[:, :, None] * inv).astype(np.float32).reshape(P, 2 * nf)
        t[:, C_ROPE + half * P:C_ROPE + half * P + 64] = np.cos(ang)
        t[:, C_ROPE + half * P + 64:C_ROPE + (half + 1) * P] = np.sin(ang)
    col = i % GRID_W
    start = np.clip(col - WIN_COLS // 2, 0, GRID_W - WIN_COLS)
    key = np.arange(GRID_W)
    inside = (key[None, :] >= start[:, None]) & (key[None, :] < start[:, None] + WIN_COLS)
    t[:, C_NAMASK:C_NAMASK + GRID_W] = np.where(inside, 0.0, -BIG)
    t[:, C_PRIO4:C_PRIO4 + 4] = np.arange(4, 0, -1)
    t[:, C_PRIO16:C_PRIO16 + 16] = np.arange(16, 0, -1)
    t[:, C_BASE:C_BASE + 4] = P * np.arange(4)
    t[:, C_EPS] = EPS
    t[:, C_ONE] = 1.0
    return t


class Banks:

    def __init__(self, full, drained):
        self.full, self.drained = full, drained
        self.at, self.used, self.per_job = {}, [0] * BANKS, [0] * BANKS
        self.in_job = False

    def place(self, name, bank):
        assert name not in self.at
        self.at[name] = (bank, self.used[bank], self.in_job)
        self.used[bank] += 1
        if self.in_job:
            self.per_job[bank] += 1

    def number(self, name, job):
        bank, n, in_job = self.at[name]
        return bank, (job * self.per_job[bank] + n if in_job else n)

    def wait_free(self, pe, name, job=None):
        bank, n = self.number(name, job)
        if self.at[name][1] > 0 or self.at[name][2]:
            pe.wait_ge(self.drained[bank], n)

    def wait_full(self, eng, name, job=None):
        bank, n = self.number(name, job)
        eng.wait_ge(self.full[bank], n + 1)

    def wait_drained(self, eng, name, job=None):
        bank, n = self.number(name, job)
        eng.wait_ge(self.drained[bank], n + 1)

    def bank(self, name):
        return self.at[name][0]


def place_products(bk, layer):
    turn = [0]

    def spread(*names, over=(0, 1, 2, 3, 4, 6, 7)):
        for name in names:
            bk.place(name, over[turn[0] % len(over)])
            turn[0] += 1

    def mod(which, c):
        if c % 4 == 0:
            bk.place(("mod", which, c // 4), 5)
        if c % 4 == 3:
            bk.place(("modT", which, c // 4), 5)

    if layer == 0:
        spread(("vec", 0), ("vec", 1))
        for c in range(4):
            mod(0, c)
    spread(("ss", 0))
    before_heads = (0, 1, 2, 3, 4)
    for kind, *args in mixing_steps(layer):
        if kind == "gates":
            spread("gates")
        elif kind == "by_token":
            spread(tuple(args), over=before_heads)
        elif kind == "by_feature":
            spread(("fm", *args), over=before_heads)
        elif kind == "mod":
            mod(*args)
        elif kind == "gate_columns":
            spread("rowsA", "rowsB", over=before_heads)
        elif kind == "old_keys":
            spread("old_keys", over=before_heads)
        elif kind == "turn":
            spread(("turn", *args), over=before_heads)
        elif kind == "context_scores":
            spread(("sp", 0), ("sp", 1), over=before_heads)
        elif kind == "scores":
            spread(("scores", *args), over=before_heads)
        elif kind == "context_turn":
            spread("pTc", over=before_heads)
        elif kind == "turn_probs":
            spread(("pT", *args), over=before_heads)
        elif kind == "context_values":
            bk.place(("o", 0), 6)
            bk.place(("o", 1), 7)
        elif kind == "decay":
            spread(("mu", *args), ("kq", *args), ("int", *args))
        elif kind == "read":
            spread(("num", *args), ("C", *args))
    spread(*[("hT", h) for h in range(4)], *[("wo", m) for m in range(8)], ("ss", 1))
    spread("lgT", "lg", *[("h2", i) for i in range(6)], "rank")
    bk.place("gs0", 6)
    bk.place(("xg0", 0), 2)
    bk.place(("xg0", 1), 3)
    bk.in_job = True
    for name, bank in ((("G", 0), 2), (("U", 0), 3), ("selT", 7), (("G", 1), 4), (("U", 1), 5), (("aT", 0), 6),
                       (("y", 0), 0), (("y", 1), 1), (("G", 2), 2), (("U", 2), 3), (("aT", 1), 7),
                       (("G", 3), 4), (("U", 3), 5), (("aT", 2), 6), ("gs", 7), (("xg", 0), 2), (("xg", 1), 3),
                       (("aT", 3), 6)):
        bk.place(name, bank)
    for m in range(8):
        bk.place(("back", m), (4, 5, 7, 6, 0, 1)[m % 6])
    bk.in_job = False


JOB_ORDER = (("G", 0), ("U", 0), ("G", 1), ("U", 1), ("G", 2), ("U", 2), ("D", 0),
             ("G", 3), ("U", 3), ("D", 1), ("D", 2), ("D", 3))
HALVES = 2 * len(JOB_ORDER)
assert HALVES % RAW == 0 and HALVES % AHEAD == 0


def stream_loads(layer):
    loads, mods_read = [], [0]

    def mod(which, c):
        if c % 4 == 3:
            loads.append((("mod", which, c), ("mod", which, c // 4)))
        else:
            mods_read[0] += 1
            loads.append((("mod", which, c), mods_read[0]))

    if layer == 0:
        for c in range(4):
            mod(0, c)
    for kind, *args in mixing_steps(layer):
        if kind == "mod":
            mod(*args)
        elif kind == "by_token" and args[1] == 0 and args[0] in ("mq", "mk", "mv", "mo"):
            loads.append((("in", args[0]), (args[0], 2)))
        elif kind == "by_feature" and args[0] in (6, 8, 0):
            loads.append((("in", {6: "hq", 8: "kv", 0: "bc"}[args[0]]),
                          {6: ("fm", 5), 8: ("nv", 2), 0: ("fm", 3)}[args[0]]))
    loads += [(("out", 0), ("wo", 3)), (("out", 1), ("wo", 7))]
    return loads


IN_COLUMN = {"bc": 0, "hq": 512, "kv": 1024, "mq": 1536, "mk": 2048, "mv": 2560, "mo": 3072}


class Layer:

    def __init__(self, sem, number):
        self.number = number
        self.first = number == 0

        def s(name):
            return sem(f"{name}_{number}")
        self.bk = Banks([s(f"full{b}") for b in range(BANKS)], [s(f"drained{b}") for b in range(BANKS)])
        place_products(self.bk, number)
        self.ring_loaded = [s(f"ring_loaded{r}") for r in range(RING)]
        self.loads = stream_loads(number)
        self.index = {name: i for i, (name, _) in enumerate(self.loads)}
        self.mod_read = s("mod_read")
        self.half_loaded = [s(f"half_loaded{r}") for r in range(RAW)]
        self.half_read = s("half_read")
        self.down_read = s("down_read")
        self.high_ready = s("high_ready")
        self.low_ready = s("low_ready")
        self.xg_high_ready = s("xg_high_ready")
        self.hidden_high_ready = s("hidden_high_ready")
        self.gates_loaded = s("gates_loaded")
        self.smalls_loaded = s("smalls_loaded")
        self.relb_loaded = s("relb_loaded")
        self.stored = s("stored")
        self.squares_ready = s("squares_ready")
        self.scaled_ready = s("scaled_ready")
        self.h_context = s("h_context")
        self.h_latent = s("h_latent")
        self.wgp_ready = s("wgp_ready")
        self.fabs_ready = s("fabs_ready")
        self.fexp_ready = s("fexp_ready")
        self.rowsin_ready = s("rowsin_ready")
        self.rowsout_ready = s("rowsout_ready")
        self.rope_ready = s("rope_ready")
        self.conv_ready = s("conv_ready")
        self.pmax_ready = s("pmax_ready")
        self.pexp_ready = s("pexp_ready")
        self.prob_ready = s("prob_ready")
        self.caug_ready = s("caug_ready")
        self.score_ready = s("score_ready")
        self.kw_ready = s("kw_ready")
        self.msq_ready = s("msq_ready")
        self.sigo_ready = s("sigo_ready")
        self.hstd_ready = s("hstd_ready")
        self.hnorm_ready = s("hnorm_ready")
        self.onehot_ready = s("onehot_ready")
        self.rexp_in = s("rexp_in")
        self.rexp_ready = s("rexp_ready")
        self.jobs_ready = s("jobs_ready")
        self.sel_ready = s("sel_ready")
        self.gated_ready = s("gated_ready")
        self.x_done = s("x_done")

    def wait_loaded(self, eng, name):
        i = self.index[name]
        eng.wait_ge(self.ring_loaded[i % RING], 16 * (i // RING + 1))

    def buffer(self, name):
        return self.index[name] % RING

    def wait_load_read(self, eng, i):
        last = self.loads[i][1]
        if isinstance(last, int):
            eng.wait_ge(self.mod_read, last)
        else:
            self.bk.wait_full(eng, last)

    def wait_half_read(self, eng, i, job):
        m = i // 2
        which, e = JOB_ORDER[m]
        if i % 2 == 0:
            eng.wait_ge(self.half_read, job * len(JOB_ORDER) + m + 1)
        elif which != "D":
            self.bk.wait_full(eng, (which, e), job)
        elif e < 3:
            eng.wait_ge(self.down_read, job * 3 + e + 1)
        else:
            self.bk.wait_full(eng, ("y", 1), job)


def build(nc, a, o):
    D, FF, NT, TILES, DEPTH = 1024, 512, 384, 3, 2
    KT = D // P
    IN_COLS = a["w_in"].shape[2]
    STREAMS = ((0, slice(0, P)), (1, slice(P, NT)))
    ISQ = 1.0 / float(np.sqrt(128.0))

    with ExitStack() as ctx:
        place = {}

        def sb(name, shape, dt=F32):
            place[name] = -(-nc.sbuf_base // 32) * 32
            return ctx.enter_context(nc.sbuf_tensor(name, shape, dt))

        def sem(name):
            return ctx.enter_context(nc.semaphore(name))

        layers = [Layer(sem, n) for n in range(DEPTH)]

        xT = sb("xT", [P, KT, NT])
        hT = sb("hT", [P, KT, NT])
        mixT = sb("mixT", [P, KT, NT])
        ring = sb("ring", [P, RING, 4096])
        zqk = sb("zqk", [P, 3, 1024])
        vaug = sb("vaug", [P, 3, 4, 129])
        arena = sb("arena", [P, 6668])
        upad = sb("upad", [P, 2, 388])
        kctx = sb("kctx", [P, 512])
        kvp = sb("kvp", [P, 512])
        nv = sb("nv", [P, 2, 256])
        modrow = sb("modrow", [P, 512])
        cb = sb("cb", [P, 2, NT])
        nqT = sb("nqT", [P, 2, NT])
        nkT = sb("nkT", [P, 2, NT])
        cst = sb("cst", [P, C_WIDTH])
        caug = sb("caug", [P, 8, 129])
        cnew = sb("cnew", [P, 8, 129])
        relb = sb("relb", [P, 4, RELBIAS_DIFFS, GRID_W])
        gbc = sb("gbc", [P, 512])
        vT = sb("vT", [P, DEPTH, V_ROWS])
        csil = sb("csil", [P, 8, 32])
        modT = sb("modT", [P, DEPTH, 48, 2])
        gains = sb("gains", [P, DEPTH, 2, 8, 2])
        std = sb("std", [P, NT])
        wgate = sb("wgate", [P, KT, 16])
        wgp = sb("wgp", [P, KT, P])
        wroute = sb("wroute", [P, KT, 20])
        gbias = sb("gbias", [P, 1])
        rbias = sb("rbias", [P, 20])
        m0 = sb("m0", [64, 1])
        rows = mixT[0:64, 2:8, :]
        mend = sb("mend", [64, 4])
        tokg = sb("tokg", [P, 9, 64])
        kct = sb("kct", [P, 2, P])
        cachek = sb("cachek", [P, 256])
        cachev = sb("cachev", [P, 256])
        small = sb("small", [P, 64])
        head = sb("head", [P, 3, 12])
        route = sb("route", [P, 320])
        jobs = sb("jobs", [P, 4], I32)
        gslot = sb("gslot", [P, 4])
        kw = sb("kw", [P, 2, P])

        ident = cst[:, C_IDENT:C_IDENT + P]
        ones = cst[:, C_ONES:C_ONES + P]
        mean = cst[:, C_MEAN:C_MEAN + P]
        eps = cst[:, C_EPS:C_EPS + 1]
        one = cst[:, C_ONE:C_ONE + 1]

        W = arena[:, 0:1024].rearrange("p (b n) -> p b n", b=2)
        S = arena[:, 1024:2048].rearrange("p (b n) -> p b n", b=2)
        inter = arena[:, 2048:2048 + 774].rearrange("p (b t n) -> p b t n", b=2, t=3)
        total = arena[:, 2822:2822 + 774].rearrange("p (b t n) -> p b t n", b=2, t=3)
        sigo = arena[:, 3596:5132].rearrange("p (t n) -> p t n", t=3)
        hsum = arena[:, 5132:6668].rearrange("p (t n) -> p t n", t=3)
        pctx = arena[:, 0:512]
        ploc = arena[:, 512:1280].rearrange("p (b n) -> p b n", b=2)
        pT = arena[:, 1280:2048].rearrange("p (b n) -> p b n", b=2)
        rope_tmp = [arena[:, 5132 + n * 256:5388 + n * 256].rearrange("p (h x f) -> p h x f", h=4, x=2) for n in range(3)]
        sg = arena[:, 1024:2048].rearrange("p (b n) -> p b n", b=2)
        act_in = arena[:, 2048:3072].rearrange("p (b n) -> p b n", b=2)
        ysb = arena[:, 4096:5120]
        selT = arena[:, 5120:5504]
        sel = arena[:, 5504:5888].rearrange("p (t n) -> p t n", t=3)
        lgT = arena[0:20, 5888:5888 + NT]
        h2tok = zqk
        squares = hT
        xrow = ring[:, RING - 1, 0:3072].rearrange("p (t d) -> p t d", t=3)
        vrow = hT[0:V_ROWS, 0:2, 0:P]
        fin_rows = zqk
        def over(name, tensor, at, shape, dt=F32R):
            return nc.alloc_sbuf_tensor_at(name, shape, dt, offset=place[tensor] + 4 * at)
        xg_high = over("xg_high", "arena", 0, [P, KT, P])
        aT_high = over("aT_high", "arena", 3072, [P, 2, 512])
        xg_low = over("xg_low", "mixT", HALF, [P, KT, P])
        aT_low = over("aT_low", "hT", HALF, [P, 2, 512])
        assert all(len(ly.loads) % RING == 1 for ly in layers)
        raw = [ring[:, 1 + r // 2, (r % 2) * HALF:(r % 2 + 1) * HALF] for r in range(4)]
        assert place["cb"] - place["kctx"] == 4 * HALF and place["cst"] - place["cb"] >= 4 * HALF
        raw += [over("raw4", "kctx", 0, [P, HALF], F32)[:], over("raw5", "cb", 0, [P, HALF], F32)[:]]
        high = [over("high0", "ring", 0, [P, HALF]), over("high1", "ring", HALF, [P, HALF]),
                over("high2", "mixT", 0, [P, HALF])]
        low = [over("low0", "ring", 6 * HALF, [P, HALF]), over("low1", "ring", 7 * HALF, [P, HALF]),
               over("low2", "hT", 0, [P, HALF])]
        cuts = [0]

        def piece(n, pattern=None, **sizes):
            cuts[0] += n
            v = route[:, cuts[0] - n:cuts[0]]
            return v.rearrange(pattern, **sizes) if pattern else v
        logits = piece(60, "p (t n) -> p t n", t=3)
        oh_group = piece(12, "p (t n) -> p t n", t=3)
        gates4 = piece(12, "p (t n) -> p t n", t=3)
        picked = piece(48, "p (t n) -> p t n", t=3)
        one1 = piece(48, "p (t n) -> p t n", t=3)
        one2 = piece(48, "p (t n) -> p t n", t=3)
        r_exp = piece(15, "p (t n) -> p t n", t=3)
        g_best, e_best1, e_best2, r_tmp, r_tmp2, slot_of = (piece(3) for _ in range(6))
        rank_s = piece(16)
        extra, upto, before, jobs_f = (piece(4) for _ in range(4))

        ps = [ctx.enter_context(nc.psum_tensor(f"ps{b}", [P, 512], F32)) for b in range(BANKS)]

        const_loaded, x_loaded, x_turned, x_copied, vecs_loaded = (
            sem(n) for n in ("const_loaded", "x_loaded", "x_turned", "x_copied", "vecs_loaded"))
        set_once, windows_written, csil_ready, vT_ready, mod_ready = (
            sem(n) for n in ("set_once", "windows_written", "csil_ready", "vT_ready", "mod_ready"))
        dve_chain, act_chain, job_chain = (sem(n) for n in ("dve_chain", "act_chain", "job_chain"))
        fin_sq, fin_sum, fin_root, fin_scaled = (sem(n) for n in ("fin_sq", "fin_sum", "fin_root", "fin_scaled"))
        fin_turned, fin_copied, fin_copied_upper, fin_stored = (
            sem(n) for n in ("fin_turned", "fin_copied", "fin_copied_upper", "fin_stored"))
        bias_windows = nc.dram_tensor("bias_windows", (DEPTH, P, 4, RELBIAS_DIFFS, GRID_W), F32).ap()

        TRI_BLOCKS = [(0, 0), (1, 1), (2, 2)]

        def blocks(dh):
            return TRI_BLOCKS + [(1, 2) if dh < 4 else (2, 1)]

        def half(h):
            return slice(64 * (h % 2), 64 * (h % 2) + 64)

        block = ctx.enter_context(nc.Block())

        @block.sync
        def _(sp):
            sp.dma_start(cst[:], a["constants"]).then_inc(const_loaded, 16)
            for first, n, src in (
                    (V_LN1, 8, a["ln1_g"].rearrange("l (r n) -> r l n", n=P)),
                    (V_LN2, 8, a["ln2_g"].rearrange("l (r n) -> r l n", n=P)),
                    (V_BMOD, 48, a["b_mod"].rearrange("l (r n) -> r l n", n=P)),
                    (V_N0, 8, a["state_n"][0].rearrange("l r h d -> (r h) l d"))):
                sp.dma_start(vrow[first:first + n], src).then_inc(vecs_loaded, 16)
            for d in range(DEPTH):
                sp.dma_start(vrow[V_CONV:V_CONV + 6, d, :], a["conv_w"][d].rearrange("w (r n) -> (w r) n", n=P)
                             ).then_inc(vecs_loaded, 16)
            for first, src in ((V_C, a["c_ctx"]), (V_C + 8, a["c"][0]), (V_FINAL, a["final_g"])):
                sp.dma_start(vrow[first:first + 8, 0, :], src.rearrange("(r n) -> r n", n=P)).then_inc(vecs_loaded, 16)
            sp.dma_start(xrow[:, 0, :], a["x_prompt"][0]).then_inc(x_loaded, 16)
            sp.dma_start(xrow[:, 1:3, :], a["x_sample"][0].rearrange("(t p) d -> p t d", p=P)).then_inc(x_loaded, 16)
            jobs_before = None
            for ly in layers:
                bk, n_loads = ly.bk, len(ly.loads)
                w_mod = a["w_mod"].rearrange("l (k p) n -> l p k n", p=P)
                w_in = a["w_in"][ly.number].rearrange("(k p) n -> p k n", p=P)
                w_out = a["w_out"][ly.number].rearrange("(k p) n -> p k n", p=P)

                def buffer_free(i):
                    if i >= RING:
                        ly.wait_load_read(sp, i - RING)
                    elif ly.first:
                        if i % RING == RING - 1:
                            sp.wait_ge(x_turned, KT)
                    elif i in (0, 3):
                        sp.wait_ge(layers[ly.number - 1].half_read, jobs_before * len(JOB_ORDER))
                    else:
                        sp.wait_ge(layers[ly.number - 1].low_ready, jobs_before * HALVES)

                for i, (name, _) in enumerate(ly.loads):
                    buffer_free(i)
                    kind, *which = name
                    if kind == "mod":
                        src = w_mod[which[0], :, :, which[1] * 512:(which[1] + 1) * 512]
                    elif kind == "out":
                        src = w_out[:, :, which[0] * 512:(which[0] + 1) * 512]
                    else:
                        c0 = IN_COLUMN[which[0]]
                        src = w_in[:, :, c0:c0 + 512]
                    sp.dma_start(ring[:, i % RING, :].rearrange("p (k n) -> p k n", k=KT), src
                                 ).then_inc(ly.ring_loaded[i % RING], 16)

                def job_loads(job, group, before=None):
                    for i in range(HALVES):
                        which, e = JOB_ORDER[i // 2]
                        if i >= RAW:
                            sp.wait_ge(ly.low_ready, job * HALVES + i - RAW + 1)
                        elif before is None:
                            ly.wait_load_read(sp, n_loads - RING + min(i // 2, RING - 1))
                            if i == 4:
                                sp.wait_ge(ly.stored, 16 * 6)
                        else:
                            sp.wait_ge(ly.low_ready, before * HALVES + HALVES + i - RAW + 1)
                        w = a[{"G": "w_gate", "U": "w_up", "D": "w_down"}[which]][ly.number]
                        kt = (FF // P if which == "D" else KT) // 2
                        rows_of_half = slice(i % 2 * kt * P, (i % 2 + 1) * kt * P)
                        sp.dma_start(raw[i % RAW].rearrange("p (k n) -> p k n", k=kt),
                                     w[bass.ds(group * 4 + e, 1), rows_of_half].rearrange("e (k p) n -> p (e k) n", p=P)
                                     ).then_inc(ly.half_loaded[i % RAW], 16)

                job_loads(0, 0)
                with sp.Fori(0, 3) as before:
                    job_loads(before + 1, before + 1, before)
                sp.wait_ge(ly.jobs_ready, 1)
                jobs_before = sp.value_load(jobs[0:1, 0:1], min_val=4, max_val=6)
                with sp.If(jobs_before > 4):
                    with sp.Fori(3, jobs_before - 1) as before:
                        group = sp.value_load(jobs[0:1, bass.ds(before - 2, 1)], min_val=0, max_val=3)
                        job_loads(before + 1, group, before)

            for t in range(TILES):
                sp.wait_ge(fin_copied, t + 1)
                sp.wait_ge(fin_copied_upper, t + 1)
                rows_out = o["y_prompt"][0] if t == 0 else o["y_sample"][0][(t - 1) * P:t * P, :]
                sp.dma_start(rows_out, fin_rows[:, t, :]).then_inc(fin_stored, 16)
            sp.wait_ge(fin_stored, 16 * TILES)

        @block.gpsimd
        def _(pool):
            def small_loads(ly):
                d = ly.number

                def load(dst, src):
                    pool.dma_start(dst, src, allow_slow_non_contiguous=True).then_inc(ly.smalls_loaded, 16)

                def load_for_gates(dst, src):
                    pool.dma_start(dst, src, allow_slow_non_contiguous=True).then_inc(ly.gates_loaded, 16)
                load_for_gates(wgate[:], a["w_in"][d].rearrange("(k p) n -> p k n", p=P)[:, :, IN_COLS - 16:IN_COLS])
                for r in range(2):
                    for way in range(2):
                        row = 64 * r + 32 * way
                        load_for_gates(gbias[row:row + 4, :], a["ml_gate_b"][d, r, way:way + 1].rearrange("a h -> h a"))
                for way in range(2):
                    load_for_gates(m0[32 * way:32 * way + 4, :], a["state_m"][0, d, way:way + 1].rearrange("a h -> h a"))
                if ly.first:
                    ly.bk.wait_full(pool, ("mod", 0, 0))
                load(cachek[:], a["cache_k"][0, d].rearrange("t h d -> t (h d)"))
                load(cachev[:], a["cache_v"][0, d].rearrange("t h d -> t (h d)"))
                load(caug[:, :, 0:P], a["state_C"][0, d].rearrange("r h d e -> d (r h) e"))
                load(gbc[:], a["ml_norm_g"][d:d + 1].broadcast_to((P, 512)))
                load(wroute[:, :, 0:4], a["w_rg"][d].rearrange("(k p) n -> p k n", p=P))
                load(wroute[:, :, 4:20], a["w_re"][d].rearrange("(k p) n -> p k n", p=P))
                load(rbias[:, 0:4], a["b_rg"][d:d + 1].broadcast_to((P, 4)))
                load(rbias[:, 4:20], a["b_re"][d:d + 1].broadcast_to((P, 16)))

            pool.wait_ge(set_once, 6)
            small_loads(layers[0])
            for d in range(DEPTH):
                for parity in range(2):
                    for h in range(4):
                        base = ((d * 4 + h) * 15 + 4 - parity) * 31 + 15
                        pool.dma_start(bias_windows[d, 64 * parity:64 * parity + 64, h].rearrange("p j w -> j p w"),
                                       bass.AP(a["na_rpb"].tensor, base,
                                               [[31, RELBIAS_DIFFS], [-1, GRID_W], [1, GRID_W]])
                                       ).then_inc(windows_written, 16)
            pool.wait_ge(windows_written, 16 * 8 * DEPTH)
            pool.dma_start(relb[:], bias_windows[0]).then_inc(layers[0].relb_loaded, 16)
            for ly in layers:
                bk, d = ly.bk, ly.number

                def store(dst, src):
                    pool.dma_start(dst, src, allow_slow_non_contiguous=True).then_inc(ly.stored, 16)
                bk.wait_drained(pool, ("kvp", 0))
                store(o["new_cache_k"][0, d].rearrange("t h d -> t (h d)"), kvp[:, 0:256])
                store(o["new_cache_v"][0, d].rearrange("t h d -> t (h d)"), kvp[:, 256:512])
                pool.wait_ge(ly.rowsin_ready, 1)
                for way in range(2):
                    store(o["new_state_m"][0, d, way:way + 1].rearrange("a h -> h a"), mend[32 * way:32 * way + 4, 2:3])
                for dh in range(8):
                    bk.wait_drained(pool, ("C", dh))
                store(o["new_state_C"][0, d].rearrange("r h d e -> d (r h) e"), cnew[:, :, 0:P])
                store(o["new_state_n"][0, d].rearrange("r h d -> d (r h)"), cnew[:, :, P])
                pool.wait_ge(ly.stored, 16 * 6)
                if d + 1 < DEPTH:
                    pool.wait_ge(ly.jobs_ready, 1)
                    small_loads(layers[d + 1])
                    pool.dma_start(relb[:], bias_windows[d + 1]).then_inc(layers[d + 1].relb_loaded, 16)

        @block.tensor
        def _(pe):
            pe.wait_ge(const_loaded, 16)
            pe.wait_ge(x_loaded, 32)
            for k in range(KT):
                for t in range(TILES):
                    mm = pe.transpose(ps[k][:, t * P:(t + 1) * P], xrow[:, t, k * P:(k + 1) * P], ident)
                mm.then_inc(x_turned, 1)

            for ly in layers:
                bk = ly.bk

                def begin(name, job=None):
                    bk.wait_free(pe, name, job)
                    return ps[bk.bank(name)]

                def done(mm, name):
                    mm.then_inc(bk.full[bk.bank(name)], 1)

                def mod(which, c):
                    ly.wait_loaded(pe, ("mod", which, c))
                    w = ring[:, ly.buffer(("mod", which, c)), :].rearrange("p (k n) -> p k n", k=KT)
                    name = ("mod", which, c // 4)
                    p = begin(name) if c % 4 == 0 else ps[bk.bank(name)]
                    for k in range(KT):
                        for g in range(4):
                            mm = pe.matmul(p[32 * g:32 * g + 32, (c % 4) * P:(c % 4 + 1) * P], csil[:, k, :],
                                           w[:, k, g * P:(g + 1) * P], start=(k == 0), stop=(k == KT - 1))
                    if c % 4 == 3:
                        done(mm, name)
                        bk.wait_drained(pe, name)
                        turned = ("modT", which, c // 4)
                        p = begin(turned)
                        for i in range(4):
                            mm = pe.transpose(p[:, i * P:(i + 1) * P], modrow[:, i * P:(i + 1) * P], ident)
                        done(mm, turned)
                    else:
                        mm.then_inc(ly.mod_read, 1)

                def sum_squares(n):
                    p = begin(("ss", n))
                    for k in range(KT):
                        pe.wait_ge(ly.squares_ready, n * KT + k + 1)
                        mm = pe.matmul(p[:, 0:NT], mean, squares[:, k, :], start=(k == 0), stop=(k == KT - 1))
                    done(mm, ("ss", n))

                def wait_normed(n, k):
                    pe.wait_ge(ly.h_context, n * KT + k + 1)
                    pe.wait_ge(ly.h_latent, n * KT + k + 1)

                def gates():
                    pe.wait_ge(ly.wgp_ready, 1)
                    p = begin("gates")
                    for k in range(KT):
                        wait_normed(0, k)
                        mm = pe.matmul(p[:, 0:NT], wgp[:, k, :], hT[:, k, :], start=(k == 0), stop=(k == KT - 1))
                    done(mm, "gates")

                def by_token(what, t):
                    load = ("in", "kv" if what in ("kvp", "nv") else what)
                    c0, n = (256, 256) if what == "nv" else (0, 512)
                    ly.wait_loaded(pe, load)
                    w = ring[:, ly.buffer(load), :].rearrange("p (k n) -> p k n", k=KT)
                    p = begin((what, t))
                    for k in range(KT):
                        mm = pe.matmul(p[:, 0:n], hT[:, k, t * P:(t + 1) * P], w[:, k, c0:c0 + n],
                                       start=(k == 0), stop=(k == KT - 1))
                    done(mm, (what, t))

                def by_feature(i):
                    load = ("in", ("bc", "hq", "kv")[i // 4])
                    ly.wait_loaded(pe, load)
                    w = ring[:, ly.buffer(load), :].rearrange("p (k n) -> p k n", k=KT)
                    p = begin(("fm", i))
                    for k in range(KT):
                        mm = pe.matmul(p[:, 0:NT], w[:, k, (i % 4) * P:(i % 4 + 1) * P], hT[:, k, :],
                                       start=(k == 0), stop=(k == KT - 1))
                    done(mm, ("fm", i))

                def gate_columns():
                    pe.wait_ge(ly.rowsout_ready, 3)
                    p = begin("rowsA")
                    for n, r in enumerate((1, 5)):
                        for t in range(TILES):
                            mm = pe.transpose(p[:, (3 * n + t) * 64:(3 * n + t + 1) * 64],
                                              rows[:, r, t * P:(t + 1) * P], ident[0:64, 0:64])
                    done(mm, "rowsA")
                    p = begin("rowsB")
                    for n, t in enumerate((1, 2, 0)):
                        mm = pe.transpose(p[:, n * 64:(n + 1) * 64], rows[:, 4, t * P:(t + 1) * P],
                                          ident[0:64, 0:64])
                    done(mm, "rowsB")

                def old_keys():
                    pe.wait_ge(ly.smalls_loaded, 16 * SMALLS)
                    p = begin("old_keys")
                    for i in range(2):
                        mm = pe.transpose(p[:, i * P:(i + 1) * P], cachek[:, i * P:(i + 1) * P], ident)
                    done(mm, "old_keys")

                def turn(i):
                    pe.wait_ge(ly.rope_ready, 1)
                    p = begin(("turn", i))
                    for t in range(TILES):
                        mm = pe.transpose(p[:, t * P:(t + 1) * P], zqk[:, t, i * P:(i + 1) * P], ident)
                    done(mm, ("turn", i))

                def context_scores():
                    bk.wait_drained(pe, ("fm", 7))
                    bk.wait_drained(pe, ("fm", 8))
                    bk.wait_drained(pe, ("fm", 9))
                    bk.wait_drained(pe, "old_keys")
                    for odd in range(2):
                        p = begin(("sp", odd))
                        for i in range(2):
                            mm = pe.matmul(p[:, i * P:(i + 1) * P], nqT[half(odd), i, 0:P],
                                           nkT[half(odd), i, 0:P], start=True, stop=True)
                        done(mm, ("sp", odd))

                def scores(n):
                    h, q = NA[n]
                    p = begin(("scores", n))
                    qs = nqT[half(h), h // 2, (1 + q) * P:(2 + q) * P]
                    pe.matmul(p[:, 0:256], qs, nkT[half(h), h // 2, P:NT], start=True, stop=True)
                    done(pe.matmul(p[:, 256:384], qs, kct[half(h), h // 2, :], start=True, stop=True), ("scores", n))

                def context_turn():
                    pe.wait_ge(ly.prob_ready, 1)
                    p = begin("pTc")
                    for h in range(4):
                        mm = pe.transpose(p[:, h * P:(h + 1) * P], pctx[:, h * P:(h + 1) * P], ident)
                    done(mm, "pTc")

                def turn_probs(n):
                    pe.wait_ge(ly.prob_ready, n + 2)
                    p = begin(("pT", n))
                    for i in range(3):
                        mm = pe.transpose(p[:, i * P:(i + 1) * P], ploc[:, n % 2, i * P:(i + 1) * P], ident)
                    done(mm, ("pT", n))

                def context_values():
                    bk.wait_drained(pe, "pTc")
                    for i in range(2):
                        begin(("o", i))
                    for h in range(4):
                        pe.matmul(ps[bk.bank(("o", h // 2))][half(h), 0:P], kvp[:, 256 + h * 64:256 + (h + 1) * 64],
                                  pctx[:, h * P:(h + 1) * P], start=True, stop=True)

                def values(n):
                    h, q = NA[n]
                    bk.wait_drained(pe, ("pT", n))
                    for i in range(3):
                        v = nv[:, i] if i < 2 else cachev[:]
                        mm = pe.matmul(ps[bk.bank(("o", h // 2))][half(h), (1 + q) * P:(2 + q) * P],
                                       v[:, h * 64:(h + 1) * 64], pT[:, n % 2, i * P:(i + 1) * P],
                                       start=(i == 0), stop=(i == 2))
                    if n % 4 == 3:
                        done(mm, ("o", n // 4))

                def decay(dh):
                    h = dh % 4
                    if dh == 0:
                        bk.wait_drained(pe, ("turn", 7))
                        bk.wait_drained(pe, ("turn", 6))
                        pe.wait_ge(ly.caug_ready, 1)
                    p = begin(("mu", dh))
                    sel_row = cst[0:64, C_SEL + dh * P:C_SEL + (dh + 1) * P]
                    mask = C_MASKF if dh < 4 else C_MASKB
                    off = blocks(dh)[3][1]
                    pe.matmul(p[:, 0:NT], sel_row, rows[:, 3, :], start=True, stop=False, skip_group_check=True)
                    for b in range(3):
                        pe.matmul(p[:, b * P:(b + 1) * P], ident, cst[:, mask:mask + P], start=False,
                                  stop=True, skip_group_check=True)
                    done(pe.matmul(p[:, NT:512], sel_row, rows[:, 3, off * P:(off + 1) * P], start=True,
                                   stop=True, skip_group_check=True), ("mu", dh))
                    p = begin(("kq", dh))
                    for b, (s, t) in enumerate(blocks(dh)):
                        mm = pe.matmul(p[:, b * P:(b + 1) * P], zqk[:, s, (4 + h) * P:(5 + h) * P],
                                       zqk[:, t, h * P:(h + 1) * P], start=True, stop=True)
                    done(mm, ("kq", dh))
                    p = begin(("int", dh))
                    for t in (1, 2):
                        mm = pe.matmul(p[:, (t - 1) * 129:t * 129], zqk[:, t, h * P:(h + 1) * P],
                                       caug[:, dh, :], start=True, stop=True)
                    done(mm, ("int", dh))

                def read(dh):
                    h = dh % 4
                    pe.wait_ge(ly.score_ready, dh + 1)
                    p = begin(("num", dh))
                    for t in range(TILES):
                        own = [b for b, (_, to) in enumerate(blocks(dh)) if to == t]
                        for n, b in enumerate(own):
                            mm = pe.matmul(p[:, t * 129:(t + 1) * 129], S[:, dh % 2, b * P:(b + 1) * P],
                                           vaug[:, blocks(dh)[b][0], h, :], start=(n == 0), stop=(n == len(own) - 1))
                    done(mm, ("num", dh))
                    pe.wait_ge(ly.kw_ready, dh + 1)
                    p = begin(("C", dh))
                    done(pe.matmul(p[:, 0:129], kw[:, dh % 2, :], vaug[:, 0, h, :], start=True, stop=True), ("C", dh))

                if ly.first:
                    pe.wait_ge(vecs_loaded, 16 * 9)
                    pe.wait_ge(x_copied, KT)
                    for d in range(DEPTH):
                        p = begin(("vec", d))
                        n = V_ROWS if d == 0 else V_C
                        done(pe.transpose(p[:, 0:n], vrow[0:n, d, :], ident[0:n, 0:n]), ("vec", d))
                    pe.wait_ge(csil_ready, 1)
                    for c in range(4):
                        mod(0, c)
                sum_squares(0)
                steps = {"gates": gates, "by_token": by_token, "by_feature": by_feature, "mod": mod,
                         "gate_columns": gate_columns, "old_keys": old_keys, "turn": turn,
                         "context_scores": context_scores, "scores": scores, "context_turn": context_turn,
                         "turn_probs": turn_probs, "context_values": context_values, "values": values,
                         "decay": decay, "read": read}
                for kind, *args in mixing_steps(ly.number):
                    if kind in steps:
                        steps[kind](*args)

                for h in range(4):
                    pe.wait_ge(ly.hnorm_ready, h + 1)
                    p = begin(("hT", h))
                    for t in range(TILES):
                        mm = pe.transpose(p[:, t * P:(t + 1) * P], hsum[:, t, h * P:(h + 1) * P], ident)
                    done(mm, ("hT", h))

                pe.wait_ge(ly.conv_ready, 1)
                for i in range(2):
                    bk.wait_drained(pe, ("o", i))
                for h in range(4):
                    bk.wait_drained(pe, ("hT", h))
                for m in range(KT):
                    ly.wait_loaded(pe, ("out", m // 4))
                    w = ring[:, ly.buffer(("out", m // 4)), :].rearrange("p (k n) -> p k n", k=KT)
                    p = begin(("wo", m))
                    for k in range(KT):
                        mm = pe.matmul(p[:, 0:NT], w[:, k, (m % 4) * P:(m % 4 + 1) * P], mixT[:, k, :],
                                       start=(k == 0), stop=(k == KT - 1))
                    done(mm, ("wo", m))

                sum_squares(1)

                p = begin("lgT")
                for k in range(KT):
                    wait_normed(1, k)
                    mm = pe.matmul(p[0:20, 0:NT], wroute[:, k, :], hT[:, k, :], start=(k == 0), stop=(k == KT - 1))
                done(mm, "lgT")
                bk.wait_drained(pe, "lgT")
                p = begin("lg")
                for t in range(TILES):
                    mm = pe.transpose(p[:, t * 20:(t + 1) * 20], lgT[:, t * P:(t + 1) * P], ident[0:20, 0:20])
                done(mm, "lg")
                for i in range(6):
                    t, upper = i // 2, i % 2
                    p = begin(("h2", i))
                    for n in range(4):
                        mm = pe.transpose(p[:, n * P:(n + 1) * P], hT[:, upper * 4 + n, t * P:(t + 1) * P], ident)
                    done(mm, ("h2", i))
                pe.wait_ge(ly.onehot_ready, 1)
                p = begin("rank")
                tri = cst[:, C_TRI:C_TRI + P]
                for t in range(TILES):
                    for s in range(t):
                        pe.matmul(p[:, t * 4:(t + 1) * 4], ones, oh_group[:, s, :], start=(s == 0), stop=False)
                    pe.matmul(p[:, t * 4:(t + 1) * 4], tri, oh_group[:, t, :], start=(t == 0), stop=True)
                for s in range(TILES):
                    mm = pe.matmul(p[:, 12:16], ones, oh_group[:, s, :], start=(s == 0), stop=(s == 2))
                done(mm, "rank")

                def gather(names, job=None):
                    p = begin(names[0], job)
                    for t in range(TILES):
                        mm = pe.matmul(p[:, 0:4], sel[:, t, :], gates4[:, t, :], start=(t == 0), stop=(t == 2))
                    done(mm, names[0])
                    for x in range(2):
                        p = begin(names[1 + x], job)
                        for n in range(4):
                            k = 4 * x + n
                            for t in range(TILES):
                                mm = pe.matmul(p[:, n * P:(n + 1) * P], h2tok[:, t, k * P:(k + 1) * P],
                                               sel[:, t, :], start=(t == 0), stop=(t == 2))
                        done(mm, names[1 + x])

                for i in range(6):
                    bk.wait_drained(pe, ("h2", i))
                pe.wait_ge(ly.sel_ready, 1)
                gather(("gs0", ("xg0", 0), ("xg0", 1)))
                for x in range(2):
                    bk.wait_drained(pe, ("xg0", x))
                pe.wait_ge(ly.jobs_ready, 1)
                count = pe.value_load(jobs[0:1, 0:1], min_val=4, max_val=6)
                with pe.Fori(0, count) as job:
                    def half_parts(name, upper, kt):
                        i = 2 * JOB_ORDER.index(name) + upper
                        pe.wait_ge(ly.low_ready, job * HALVES + i + 1)
                        return (part[i % AHEAD][:].rearrange("p (k n) -> p k n", k=kt) for part in (high, low))

                    def three_passes(p, x_high, x_low, w_high, w_low, start, stop):
                        pe.matmul(p, x_high, w_high, start=start, stop=False)
                        pe.matmul(p, x_high, w_low, start=False, stop=False)
                        return pe.matmul(p, x_low, w_high, start=False, stop=stop)

                    def gate_up(e):
                        for which in "GU":
                            name = (which, e)
                            p = begin(name, job)
                            for upper in range(2):
                                w_high, w_low = half_parts(name, upper, 4)
                                for n in range(4):
                                    k = 4 * upper + n
                                    mm = three_passes(p[:, :], xg_high[:, k, :], xg_low[:, k, :], w_high[:, n, :],
                                                      w_low[:, n, :], k == 0, k == KT - 1)
                                if upper == 0:
                                    mm.then_inc(ly.half_read, 1)
                            done(mm, name)

                    def turn_hidden(e):
                        pe.wait_ge(ly.gated_ready, job * 4 + e + 1)
                        p = begin(("aT", e), job)
                        for f in range(4):
                            mm = pe.transpose(p[:, f * P:(f + 1) * P], act_in[:, e % 2, f * P:(f + 1) * P], ident)
                        done(mm, ("aT", e))

                    def down(e):
                        bk.wait_drained(pe, ("aT", e), job)
                        if e == 0:
                            begin(("y", 0), job)
                            begin(("y", 1), job)
                        for upper in range(2):
                            w_high, w_low = half_parts(("D", e), upper, 2)
                            for y in range(2):
                                cols = slice(y * 512, (y + 1) * 512)
                                for n in range(2):
                                    f = 2 * upper + n
                                    mm = three_passes(ps[bk.bank(("y", y))][:, :], aT_high[:, e % 2, f * P:(f + 1) * P],
                                                      aT_low[:, e % 2, f * P:(f + 1) * P], w_high[:, n, cols],
                                                      w_low[:, n, cols], e == 0 and f == 0, e == 3 and f == 3)
                                if e == 3 and upper == 1:
                                    done(mm, ("y", y))
                            if upper == 0:
                                mm.then_inc(ly.half_read, 1)
                        if e < 3:
                            mm.then_inc(ly.down_read, 1)

                    bk.wait_free(pe, ("G", 0), job)
                    bk.wait_free(pe, ("U", 0), job)
                    gate_up(0)
                    p = begin("selT", job)
                    for t in range(TILES):
                        mm = pe.transpose(p[:, t * P:(t + 1) * P], sel[:, t, :], ident)
                    done(mm, "selT")
                    gate_up(1)
                    turn_hidden(0)
                    gate_up(2)
                    down(0)
                    turn_hidden(1)
                    gate_up(3)
                    down(1)
                    turn_hidden(2)
                    pe.wait_ge(ly.sel_ready, job + 2)
                    gather(("gs", ("xg", 0), ("xg", 1)), job)
                    turn_hidden(3)
                    down(2)
                    down(3)
                    bk.wait_drained(pe, "selT", job)
                    for y in range(2):
                        bk.wait_drained(pe, ("y", y), job)
                    for m in range(KT):
                        p = begin(("back", m), job)
                        done(pe.matmul(p[:, 0:NT], ysb[:, m * P:(m + 1) * P], selT, start=True, stop=True), ("back", m))

            for k in range(KT):
                pe.wait_ge(fin_sq, k + 1)
                mm = pe.matmul(ps[0][:, 0:NT], mean, mixT[:, k, :], start=(k == 0), stop=(k == KT - 1))
            mm.then_inc(fin_sum, 1)
            for i in range(6):
                pe.wait_ge(fin_scaled, 4 * (i % 2) + 4)
                for n in range(4):
                    mm = pe.transpose(ps[1 + i][:, n * P:(n + 1) * P],
                                      hT[:, (i % 2) * 4 + n, (i // 2) * P:(i // 2 + 1) * P], ident)
                mm.then_inc(fin_turned, 1)

        @block.scalar
        def _(act):
            chain = [0]

            def link(ins):
                chain[0] += 1
                ins.then_inc(act_chain, 1)
                act.wait_ge(act_chain, chain[0])

            act.wait_ge(set_once, 6)
            act.wait_ge(vT_ready, 1)
            act.activation(csil[:, :, 0:2].rearrange("p k s -> p s k"),
                           vT[:, 0, V_C:V_C + 16].rearrange("p (s k) -> p s k", s=2), ACT.Silu
                           ).then_inc(csil_ready, 1)
            act.wait_ge(x_copied, KT)
            for ly in layers:
                bk, L = ly.bk, ly.number

                def drain(name, ins):
                    ins.then_inc(bk.drained[bk.bank(name)], 1)

                def full_of(name, job=None):
                    bk.wait_full(act, name, job)
                    return ps[bk.bank(name)]

                def split_high(i, job=None):
                    round_of = i // RAW + 1
                    act.wait_ge(ly.half_loaded[i % RAW],
                                16 * round_of if job is None else job * (16 * HALVES // RAW) + 16 * round_of)
                    if job is not None:
                        ly.wait_half_read(act, i - AHEAD, job)
                    if job is None and i == 0:
                        ly.wait_load_read(act, len(ly.loads) - 1)
                    act.copy(high[i % AHEAD][:], raw[i % RAW]).then_inc(ly.high_ready, 1)

                def norm(n):
                    for k in range(KT):
                        if n == 1:
                            bk.wait_drained(act, ("wo", k))
                        act.activation(squares[:, k, :], xT[:, k, :], ACT.Square).then_inc(ly.squares_ready, 1)
                    p = full_of(("ss", n))
                    drain(("ss", n), act.activation(std[:], p[:, 0:NT], ACT.Sqrt, bias=eps))
                    if n == 1:
                        split_high(0)
                    cols = STREAMS[0][1]
                    for k in range(KT):
                        act.wait_ge(ly.scaled_ready, n * KT + k + 1)
                        act.activation(hT[:, k, cols], hT[:, k, cols], ACT.Identity,
                                       scale=gains[:, L, n, k, 0:1], bias=modT[:, L, 24 * n + k, 0:1]
                                       ).then_inc(ly.h_context, 1)

                def gates():
                    act.wait_ge(ly.fabs_ready, 1)
                    link(act.activation(rows[:, 4, :], rows[:, 2, :], ACT.Exp))
                    act.activation(rows[:, 5, :], rows[:, 4, :], ACT.Ln, bias=one[0:64, :]).then_inc(ly.fexp_ready, 1)

                def gates_end():
                    act.wait_ge(ly.rowsin_ready, 1)
                    act.activation(rows[:, 4, P:NT], rows[:, 3, P:NT], ACT.Exp, bias=m0[:, :], scale=-1.0
                                   ).then_inc(ly.rowsout_ready, 1)
                    act.activation(rows[:, 4, 0:P], rows[:, 1, 0:P], ACT.Exp, bias=mend[:, 1:2]
                                   ).then_inc(ly.rowsout_ready, 1)
                    act.activation(rows[:, 5, :], rows[:, 2, :], ACT.Exp, scale=-1.0).then_inc(ly.rowsout_ready, 1)

                def by_token(what, t):
                    p = full_of((what, t))
                    if what == "kvp" and not ly.first:
                        act.wait_ge(layers[L - 1].stored, 16 * 6)
                    if what == "mq":
                        ins = act.copy(zqk[:, t, 0:512], p[:, :])
                    elif what == "mk":
                        if t == 0:
                            act.copy(kctx[:], p[:, :])
                        ins = act.copy(zqk[:, t, 512:1024], p[:, :])
                    elif what == "mv":
                        ins = act.copy(vaug[:, t, :, 0:P], p[:, :].rearrange("p (h d) -> p h d", h=4))
                    elif what == "mo":
                        ins = act.copy(sigo[:, t, :], p[:, :])
                    elif what == "kvp":
                        ins = act.copy(kvp[:], p[:, :])
                    else:
                        ins = act.copy(nv[:, t - 1], p[:, 0:256])
                    drain((what, t), ins)
                    if (what, t) == ("mk", 0):
                        gates_end()

                def by_feature(i):
                    if i in (2, 3):
                        return
                    p = full_of(("fm", i))
                    if i < 2:
                        ins = act.copy(cb[:, i, :], p[:, 0:NT])
                    elif i < 6:
                        act.copy(upad[:, i - 4, 1:129], p[:, 0:P])
                        ins = act.copy(upad[:, i - 4, 130:386], p[:, P:NT])
                    elif i < 8:
                        ins = act.mul(nqT[:, i - 6, :], p[:, 0:NT], 0.125)
                    else:
                        ins = act.copy(nkT[:, i - 8, :], p[:, 0:NT])
                    drain(("fm", i), ins)

                def gate_columns():
                    p = full_of("rowsA")
                    drain("rowsA", act.copy(tokg[:, 0:6, :], p[:, 0:384].rearrange("p (n r) -> p n r", n=6)))
                    p = full_of("rowsB")
                    drain("rowsB", act.copy(tokg[:, 6:9, :], p[:, 0:192].rearrange("p (n r) -> p n r", n=3)))

                def old_keys():
                    p = full_of("old_keys")
                    drain("old_keys", act.copy(kct[:], p[:, 0:256].rearrange("p (n r) -> p n r", n=2)))

                def turn(i):
                    p = full_of(("turn", i))
                    drain(("turn", i), act.copy(zqk[:, :, i * P:(i + 1) * P], p[:, 0:NT].rearrange("p (t n) -> p t n", t=3)))

                def context_scores():
                    act.wait_ge(ly.pmax_ready, 1)
                    act.activation(pctx, pctx, ACT.Exp).then_inc(ly.pexp_ready, 1)

                def scores(n):
                    act.wait_ge(ly.pmax_ready, n + 2)
                    act.activation(ploc[:, n % 2, :], ploc[:, n % 2, :], ACT.Exp,
                                   bias=small[:, 8 + n:9 + n], accum_out=small[:, 16 + n:17 + n]
                                   ).then_inc(ly.pexp_ready, 1)

                def context_turn():
                    p = full_of("pTc")
                    drain("pTc", act.copy(pctx, p[:, :]))

                def turn_probs(n):
                    p = full_of(("pT", n))
                    drain(("pT", n), act.copy(pT[:, n % 2, :], p[:, 0:NT]))

                def values(n):
                    if n % 4 == 3:
                        p = full_of(("o", n // 4))
                        drain(("o", n // 4), act.copy(mixT[:, 2 + n // 4, :], p[:, 0:NT]))

                def decay(dh):
                    lane = (dh // 4) * 32 + dh % 4
                    tiles_of_s = (0, 1, 2, 1 if dh < 4 else 2)
                    p = full_of(("mu", dh))
                    if dh >= 2:
                        act.wait_ge(ly.score_ready, dh - 1)
                    for b in range(4):
                        ins = act.activation(W[:, dh % 2, b * P:(b + 1) * P], p[:, b * P:(b + 1) * P], ACT.Exp,
                                             bias=tokg[:, tiles_of_s[b], lane:lane + 1], scale=-1.0)
                    drain(("mu", dh), ins)
                    p = full_of(("int", dh))
                    if dh >= 2:
                        bk.wait_drained(act, ("num", dh - 2))
                    for t in (1, 2):
                        ins = act.activation(inter[:, dh % 2, t, :], p[:, (t - 1) * 129:t * 129], ACT.Copy,
                                             scale=tokg[:, 5 + t, lane:lane + 1])
                    drain(("int", dh), ins)

                def read(dh):
                    p = full_of(("C", dh))
                    drain(("C", dh), act.copy(cnew[:, dh, :], p[:, 0:129]))

                norm(0)
                steps = {"gates": gates, "by_token": by_token, "by_feature": by_feature,
                         "gate_columns": gate_columns, "old_keys": old_keys, "turn": turn,
                         "context_scores": context_scores, "scores": scores, "context_turn": context_turn,
                         "turn_probs": turn_probs, "values": values, "decay": decay, "read": read}
                for kind, *args in mixing_steps(ly.number):
                    if (kind, *args) == ("decay", 0):
                        for t in range(TILES):
                            bk.wait_drained(act, ("mo", t))
                        act.activation(sigo, sigo, ACT.Sigmoid).then_inc(ly.sigo_ready, 1)
                    if kind in steps:
                        steps[kind](*args)

                act.wait_ge(ly.msq_ready, 1)
                act.activation(head[:, 1, :], head[:, 0, :], ACT.Sqrt, bias=eps, scale=1.0 / P
                               ).then_inc(ly.hstd_ready, 1)
                for h in range(4):
                    p = full_of(("hT", h))
                    drain(("hT", h), act.copy(mixT[:, 4 + h, :], p[:, 0:NT]))
                norm(1)

                p = full_of("lgT")
                drain("lgT", act.copy(lgT, p[0:20, 0:NT]))
                split_high(1)
                for i in range(6):
                    p = full_of(("h2", i))
                    drain(("h2", i), act.copy(h2tok[:, i // 2, (i % 2) * 512:(i % 2 + 1) * 512], p[:, :]))
                split_high(2)
                act.wait_ge(ly.rexp_in, 1)
                act.activation(r_exp, r_exp, ACT.Exp).then_inc(ly.rexp_ready, 1)

                def half_gathered(name, job=None):
                    p = full_of(name, job)
                    act.copy(xg_high[:, 4 * name[1]:4 * name[1] + 4, :],
                             p[:, :].rearrange("p (k n) -> p k n", k=4)).then_inc(ly.xg_high_ready, 1)

                half_gathered(("xg0", 0))
                half_gathered(("xg0", 1))
                act.wait_ge(ly.jobs_ready, 1)
                count = act.value_load(jobs[0:1, 0:1], min_val=4, max_val=6)
                with act.Fori(0, count) as job:
                    def silu(e):
                        p = full_of(("G", e), job)
                        act.wait_ge(ly.gated_ready, job * 4 + (e - 1 if e > 1 else 0))
                        drain(("G", e), act.activation(sg[:, e % 2, :], p[:, :], ACT.Silu))

                    def hidden_high(e):
                        p = full_of(("aT", e), job)
                        act.copy(aT_high[:, e % 2, :], p[:, :]).then_inc(ly.hidden_high_ready, 1)

                    for i in range(HALVES):
                        if i + AHEAD < HALVES:
                            split_high(i + AHEAD, job)
                        if i in (1, 5, 9, 15):
                            silu((1, 5, 9, 15).index(i))
                        if i == 3:
                            p = full_of("selT", job)
                            drain("selT", act.copy(selT, p[:, 0:NT]))
                        if i in (7, 13, 19):
                            hidden_high((7, 13, 19).index(i))
                        if i == 19:
                            half_gathered(("xg", 0), job)
                            half_gathered(("xg", 1), job)
                            hidden_high(3)
                    with act.If(count > job + 1):
                        split_high(HALVES, job)
                    p = full_of(("y", 0), job)
                    drain(("y", 0), act.copy(ysb[:, 0:512], p[:, :]))
                    with act.If(count > job + 1):
                        split_high(HALVES + 1, job)
                        split_high(HALVES + 2, job)
                act.wait_ge(ly.x_done, 1)

            for k in range(KT):
                act.activation(mixT[:, k, :], xT[:, k, :], ACT.Square).then_inc(fin_sq, 1)
            act.wait_ge(fin_sum, 1)
            act.activation(std[:], ps[0][:, 0:NT], ACT.Sqrt, bias=eps).then_inc(fin_root, 1)
            for t in range(TILES):
                act.wait_ge(fin_turned, 2 * t + 2)
                act.copy(fin_rows[:, t, 512:1024], ps[2 + 2 * t][:, :]).then_inc(fin_copied_upper, 1)

        @block.vector
        def _(dve):
            chain = [0]

            def link(ins):
                chain[0] += 1
                ins.then_inc(dve_chain, 1)
                dve.wait_ge(dve_chain, chain[0])

            dve.memset(upad[:], 0.0).then_inc(set_once, 1)
            dve.memset(wgp[:], 0.0).then_inc(set_once, 1)
            dve.memset(vaug[:, :, :, 128:129], 1.0).then_inc(set_once, 1)
            dve.memset(m0[:], 0.0).then_inc(set_once, 1)
            dve.memset(gbias[:], 0.0).then_inc(set_once, 1)
            dve.memset(csil[:], 0.0).then_inc(set_once, 1)
            for k in range(KT):
                dve.wait_ge(x_turned, k + 1)
                dve.tensor_copy(xT[:, k, :], ps[k][:, 0:NT]).then_inc(x_copied, 1)
            for ly in layers:
                bk, L = ly.bk, ly.number

                def drain(name, ins):
                    ins.then_inc(bk.drained[bk.bank(name)], 1)

                def full_of(name, job=None):
                    bk.wait_full(dve, name, job)
                    return ps[bk.bank(name)]

                def wide(x, n):
                    return x[:, :, None].broadcast_to((P, x.shape[1], n))

                def mod(which, c):
                    if c % 4 < 3:
                        return
                    q = c // 4
                    p = full_of(("mod", which, q))
                    drain(("mod", which, q), dve.tensor_copy(modrow[:], p[:, :]))
                    p = full_of(("modT", which, q))
                    drain(("modT", which, q), dve.tensor_tensor(
                        modT[:, which, 16 * q:16 * q + 16, :], p[:, :].rearrange("p (m r) -> p m r", r=32)[:, :, 0:2],
                        wide(vT[:, which, V_BMOD + 16 * q:V_BMOD + 16 * q + 16], 2), ALU.add))
                    bk.wait_drained(dve, ("modT", which, q))
                    if q != 1:
                        n, m_first, v0 = (0, 8, V_LN1) if q == 0 else (1, 32, V_LN2)
                        dve.scalar_tensor_tensor(gains[:, which, n], modT[:, which, m_first:m_first + 8, :], 1.0,
                                                 wide(vT[:, which, v0:v0 + 8], 2), ALU.add, ALU.mult
                                                 ).then_inc(mod_ready, 1)

                def norm(n):
                    bk.wait_drained(dve, ("ss", n))
                    dve.wait_ge(mod_ready, 2 * L + n + 1)
                    link(dve.reciprocal(std[:], std[:]))
                    cols = STREAMS[1][1]
                    for k in range(KT + 1):
                        if k < KT:
                            dve.tensor_tensor(hT[:, k, :], xT[:, k, :], std[:], ALU.mult).then_inc(ly.scaled_ready, 1)
                        if k > 0:
                            dve.wait_ge(ly.scaled_ready, n * KT + k)
                            dve.tensor_scalar(hT[:, k - 1, cols], hT[:, k - 1, cols], gains[:, L, n, k - 1, 1:2],
                                              modT[:, L, 24 * n + k - 1, 1:2], ALU.mult, ALU.add
                                              ).then_inc(ly.h_latent, 1)

                def gates():
                    p = full_of("gates")
                    dve.tensor_scalar(rows[:, 0, :], p[64:128, 0:NT], gbias[64:128, :], None, ALU.add)
                    drain("gates", dve.tensor_scalar(rows[:, 1, :], p[0:64, 0:NT], gbias[0:64, :], None, ALU.add))
                    bk.wait_drained(dve, "gates")
                    dve.scalar_tensor_tensor(rows[:, 2, :], rows[:, 0, :], -1.0, rows[:, 0, :], ALU.mult, ALU.min
                                             ).then_inc(ly.fabs_ready, 1)
                    dve.wait_ge(ly.fexp_ready, 1)
                    link(dve.scalar_tensor_tensor(rows[:, 0, :], rows[:, 0, :], 0.0, rows[:, 5, :], ALU.min, ALU.subtract))
                    F, B = slice(0, 32), slice(32, 64)
                    segments = ((F, slice(0, P)), (F, slice(P, NT)), (B, slice(P - 1, None, -1)),
                                (B, slice(NT - 1, P - 1, -1)))
                    for r, c in segments:
                        ins = dve.tensor_tensor_scan(rows[r, 2, c], rows[r, 0, c], rows[r, 0, c], 0.0, ALU.add, ALU.bypass)
                    link(ins)
                    link(dve.tensor_tensor(rows[:, 1, :], rows[:, 1, :], rows[:, 2, :], ALU.subtract))
                    for n, (r, c) in enumerate(segments):
                        init = m0[r, 0:1] if n % 2 else 0.0
                        ins = dve.tensor_tensor_scan(rows[r, 3, c], rows[r, 1, c], rows[r, 1, c], init, ALU.max, ALU.bypass)
                    link(ins)
                    if not ly.first:
                        dve.wait_ge(layers[L - 1].stored, 16 * 6)
                    for r, last in ((F, P - 1), (B, 0)):
                        dve.tensor_scalar(mend[r, 1:2], rows[r, 3, last:last + 1], -1.0, None, ALU.mult)
                        ins = dve.tensor_tensor(mend[r, 2:3], rows[r, 3, last:last + 1], rows[r, 2, last:last + 1], ALU.add)
                    link(ins)
                    dve.tensor_tensor(rows[:, 2, :], rows[:, 2, :], rows[:, 3, :], ALU.add).then_inc(ly.rowsin_ready, 1)

                def rope():
                    for t in range(TILES):
                        bk.wait_drained(dve, ("mk", t))
                        bk.wait_drained(dve, ("mq", t))
                    for t in (1, 2):
                        z = zqk[:, t, :].rearrange("p (h x y f) -> p h x y f", h=8, x=2, y=2)
                        for h0 in (0, 4):
                            x1, x2 = (z[:, h0:h0 + 4, :, y, :] for y in (0, 1))
                            table = cst[:, C_ROPE + (t - 1) * P:C_ROPE + t * P].rearrange("p (s x f) -> p s x f", s=2, x=2)
                            cos, sin = (table[:, None, s].broadcast_to((P, 4, 2, 32)) for s in (0, 1))
                            tmp = rope_tmp
                            dve.tensor_tensor(tmp[0], x1, sin, ALU.mult)
                            dve.tensor_tensor(tmp[1], x2, sin, ALU.mult)
                            link(dve.tensor_tensor(tmp[2], x1, cos, ALU.mult))
                            link(dve.tensor_tensor(x1, tmp[2], tmp[1], ALU.subtract))
                            link(dve.tensor_tensor(tmp[2], x2, cos, ALU.mult))
                            ins = dve.tensor_tensor(x2, tmp[2], tmp[0], ALU.add)
                            if (t, h0) == (2, 4):
                                ins.then_inc(ly.rope_ready, 1)
                            else:
                                link(ins)

                def by_feature(i):
                    if i not in (2, 3):
                        return
                    c = i - 2
                    bk.wait_drained(dve, ("fm", 4 + c))
                    p = full_of(("fm", i))
                    dve.tensor_tensor(upad[:, c, 1:129], upad[:, c, 1:129], p[:, 0:P], ALU.mult)
                    drain(("fm", i), dve.tensor_tensor(upad[:, c, 130:386], upad[:, c, 130:386], p[:, P:NT], ALU.mult))
                    bk.wait_drained(dve, ("fm", i))
                    taps = [vT[:, L, V_CONV + 2 * w + c:V_CONV + 2 * w + c + 1] for w in range(3)]
                    out = ((mixT[:, c, 0:P], 1, P), (mixT[:, c, P:NT], 130, 256))
                    for dst, c0, n in out:
                        ins = dve.tensor_scalar(dst, upad[:, c, c0:c0 + n], taps[1], None, ALU.mult)
                    link(ins)
                    for w, shift in ((0, -1), (2, 1)):
                        for dst, c0, n in out:
                            ins = dve.scalar_tensor_tensor(dst, upad[:, c, c0 + shift:c0 + shift + n], taps[w],
                                                           dst, ALU.mult, ALU.add)
                        link(ins)
                    bk.wait_drained(dve, ("fm", c))
                    dve.tensor_tensor(mixT[:, c, :], mixT[:, c, :], cb[:, c, :], ALU.mult).then_inc(ly.conv_ready, 1)

                pc4 = pctx.rearrange("p (h k) -> p h k", h=4)

                def context_scores():
                    for odd in range(2):
                        p = full_of(("sp", odd))
                        pair = p[:, 0:256].rearrange("p (h k) -> p h k", h=2)
                        most = small[:, 2 + 2 * odd:4 + 2 * odd]
                        link(dve.tensor_reduce(most, pair, AX.X, ALU.max))
                        drain(("sp", odd), dve.tensor_tensor(pc4[:, odd::2], pair, wide(most, P), ALU.subtract))
                    bk.wait_drained(dve, ("sp", 0))
                    bk.wait_drained(dve, ("sp", 1))
                    dve.sem_inc(ly.pmax_ready, 1)

                def scores(n):
                    h, q = NA[n]
                    p = full_of(("scores", n))
                    if n >= 2:
                        bk.wait_full(dve, ("pT", n - 2))
                    dve.tensor_tensor(ploc[:, n % 2, 0:256].rearrange("p (j w) -> p j w", j=4),
                                      p[:, 0:256].rearrange("p (j w) -> p j w", j=4),
                                      relb[:, h, 3 - 2 * q:7 - 2 * q, :], ALU.add)
                    drain(("scores", n), dve.tensor_copy(ploc[:, n % 2, 256:384], p[:, 256:384]))
                    bk.wait_drained(dve, ("scores", n))
                    dve.tensor_reduce(small[:, 8 + n:9 + n], ploc[:, n % 2, :], AX.X, ALU.max, negate=True
                                      ).then_inc(ly.pmax_ready, 1)

                def context_turn():
                    dve.wait_ge(ly.pexp_ready, 1)
                    link(dve.tensor_reduce(small[:, 2:6], pc4, AX.X, ALU.add))
                    link(dve.reciprocal(small[:, 2:6], small[:, 2:6]))
                    dve.tensor_tensor(pc4, pc4, wide(small[:, 2:6], P), ALU.mult).then_inc(ly.prob_ready, 1)

                def turn_probs(n):
                    dve.wait_ge(ly.pexp_ready, n + 2)
                    link(dve.reciprocal(small[:, 24 + n:25 + n], small[:, 16 + n:17 + n]))
                    dve.tensor_scalar(ploc[:, n % 2, :], ploc[:, n % 2, :], small[:, 24 + n:25 + n], None, ALU.mult
                                      ).then_inc(ly.prob_ready, 1)

                def decay(dh):
                    h, lane = dh % 4, (dh // 4) * 32 + dh % 4
                    bk.wait_drained(dve, ("mu", dh))
                    p = full_of(("kq", dh))
                    if dh >= 2:
                        bk.wait_full(dve, ("C", dh - 2))
                    dve.scalar_tensor_tensor(S[:, dh % 2, :], p[:, :], ISQ, W[:, dh % 2, :], ALU.mult, ALU.mult
                                             ).then_inc(ly.score_ready, 1)
                    dve.tensor_scalar(kw[:, dh % 2, :], kctx[:, h * P:(h + 1) * P],
                                      tokg[:, 8, lane:lane + 1], ISQ, ALU.mult, ALU.mult).then_inc(ly.kw_ready, 1)
                    dve.wait_ge(ly.score_ready, dh + 1)
                    dve.sem_inc(bk.drained[bk.bank(("kq", dh))], 1)

                def read(dh):
                    h, lane, b = dh % 4, (dh // 4) * 32 + dh % 4, dh % 2
                    p = full_of(("num", dh))
                    bk.wait_drained(dve, ("int", dh))
                    dve.tensor_copy(total[:, b, 0, :], p[:, 0:129])
                    drain(("num", dh), dve.tensor_tensor(total[:, b, 1:3, :], inter[:, b, 1:3, :],
                                                         p[:, 129:387].rearrange("p (t n) -> p t n", t=2), ALU.add))
                    bk.wait_drained(dve, ("num", dh))
                    den = total[:, b, :, 128]
                    link(dve.scalar_tensor_tensor(small[:, 32:35], den, -1.0, den, ALU.mult, ALU.max))
                    link(dve.tensor_tensor(small[:, 32:35], small[:, 32:35], tokg[:, 3:6, lane], ALU.max))
                    link(dve.reciprocal(small[:, 32:35], small[:, 32:35]))
                    for t in range(TILES):
                        dst = hsum[:, t, h * P:(h + 1) * P]
                        if dh < 4:
                            ins = dve.tensor_scalar(dst, total[:, b, t, 0:P], small[:, 32 + t:33 + t], None, ALU.mult)
                        else:
                            ins = dve.scalar_tensor_tensor(dst, total[:, b, t, 0:P], small[:, 32 + t:33 + t], dst,
                                                           ALU.mult, ALU.add)
                    if dh >= 3:
                        link(ins)
                    if dh >= 4:
                        heads = hsum[:, :, h * P:(h + 1) * P]
                        link(dve.tensor_tensor(total[:, b, :, 0:P], heads, heads, ALU.mult))
                        ins = dve.tensor_reduce(head[:, 0, 3 * h:3 * h + 3], total[:, b, :, 0:P], AX.X, ALU.add)
                    if dh == 7:
                        ins.then_inc(ly.msq_ready, 1)

                if ly.first:
                    for d in range(DEPTH):
                        p = full_of(("vec", d))
                        n = V_ROWS if d == 0 else V_C
                        drain(("vec", d), dve.tensor_copy(vT[:, d, 0:n], p[:, 0:n]))
                    bk.wait_drained(dve, ("vec", 0))
                    bk.wait_drained(dve, ("vec", 1))
                    dve.sem_inc(vT_ready, 1)
                    for c in range(4):
                        mod(0, c)
                dve.wait_ge(ly.gates_loaded, 16 * GATE_LOADS)
                dve.tensor_copy(wgp[:].rearrange("p k (g r) -> p k g r", g=4)[:, :, :, 0:4],
                                wgate[:].rearrange("p k (g r) -> p k g r", g=4)).then_inc(ly.wgp_ready, 1)
                dve.tensor_copy(caug[:, :, P], vT[:, L, V_N0:V_N0 + 8]).then_inc(ly.caug_ready, 1)
                norm(0)
                steps = {"gates": gates, "mod": mod, "rope": rope, "by_feature": by_feature,
                         "context_scores": context_scores, "scores": scores, "context_turn": context_turn,
                         "turn_probs": turn_probs, "decay": decay, "read": read}
                for kind, *args in mixing_steps(ly.number):
                    if kind == "context_scores":
                        dve.wait_ge(ly.smalls_loaded, 16 * SMALLS)
                        dve.wait_ge(ly.relb_loaded, 16)
                        rel3 = relb[:].rearrange("p h j w -> p (h j) w")
                        na_mask = cst[:, C_NAMASK:C_NAMASK + GRID_W]
                        link(dve.tensor_tensor(rel3, rel3, na_mask[:, None, :].broadcast_to((P, 4 * RELBIAS_DIFFS, GRID_W)),
                                              ALU.add))
                    if kind == "decay" and args[0] == 0:
                        bk.wait_drained(dve, "rowsA")
                        bk.wait_drained(dve, "rowsB")
                        dve.wait_ge(ly.sigo_ready, 1)
                        link(dve.tensor_tensor(sigo, sigo, gbc[:, None, :].broadcast_to((P, 3, 512)), ALU.mult))
                    if kind in steps:
                        steps[kind](*args)

                dve.wait_ge(ly.hstd_ready, 1)
                link(dve.reciprocal(head[:, 2, :], head[:, 1, :]))
                for h in range(4):
                    for t in range(TILES):
                        of_head = slice(h * P, (h + 1) * P)
                        ins = dve.scalar_tensor_tensor(hsum[:, t, of_head], hsum[:, t, of_head],
                                                       head[:, 2, 3 * h + t:3 * h + t + 1], sigo[:, t, of_head],
                                                       ALU.mult, ALU.mult)
                    ins.then_inc(ly.hnorm_ready, 1)

                def residual(name, gate0, m, p):
                    for j, cols in STREAMS:
                        ins = dve.scalar_tensor_tensor(xT[:, m, cols], p[:, cols], modT[:, L, gate0 + m, j:j + 1],
                                                       xT[:, m, cols], ALU.mult, ALU.add)
                    drain(name, ins)

                for m in range(KT):
                    residual(("wo", m), 16, m, full_of(("wo", m)))
                for m in range(KT):
                    bk.wait_drained(dve, ("wo", m))
                norm(1)

                def split_low(i, job=None):
                    dve.wait_ge(ly.high_ready, i + 1 if job is None else job * HALVES + i + 1)
                    dve.tensor_tensor(low[i % AHEAD][:], raw[i % RAW], high[i % AHEAD][:].bitcast(F32), ALU.subtract
                                      ).then_inc(ly.low_ready, 1)

                split_low(0)

                p = full_of("lg")
                drain("lg", dve.tensor_tensor(logits, p[:, 0:60].rearrange("p (t n) -> p t n", t=3),
                                              rbias[:, None, :].broadcast_to((P, 3, 20)), ALU.add))
                bk.wait_drained(dve, "lg")
                gl, el = logits[:, :, 0:4], logits[:, :, 4:20]

                def first_max(values, best, onehot, prio, n):
                    link(dve.tensor_reduce(best, values, AX.X, ALU.max))
                    link(dve.tensor_tensor(onehot, values, wide(best, n), ALU.is_equal))
                    link(dve.tensor_tensor(onehot, onehot, cst[:, None, prio:prio + n].broadcast_to((P, 3, n)), ALU.mult))
                    link(dve.tensor_reduce(r_tmp, onehot, AX.X, ALU.max))
                    return dve.tensor_tensor(onehot, onehot, wide(r_tmp, n), ALU.is_equal)

                first_max(gl, g_best, oh_group, C_PRIO4, 4).then_inc(ly.onehot_ready, 1)
                dve.wait_ge(ly.onehot_ready, 1)
                el4 = el.rearrange("p t (g e) -> p t g e", g=4)
                picked4 = picked.rearrange("p t (g e) -> p t g e", g=4)
                off4 = one1.rearrange("p t (g e) -> p t g e", g=4)
                ohb = oh_group[:, :, :, None].broadcast_to((P, 3, 4, 4))
                for t in range(TILES):
                    dve.tensor_tensor(picked4[:, t], el4[:, t], ohb[:, t], ALU.mult)
                    ins = dve.tensor_scalar(off4[:, t], ohb[:, t], -1.0, BIG, ALU.add, ALU.mult)
                link(ins)
                link(dve.tensor_tensor(picked, picked, one1, ALU.add))
                link(first_max(picked, e_best1, one1, C_PRIO16, 16))
                link(dve.scalar_tensor_tensor(picked, one1, -3.0 * BIG, picked, ALU.mult, ALU.add))
                link(first_max(picked, e_best2, one2, C_PRIO16, 16))
                link(dve.tensor_tensor(r_exp[:, :, 0:4], gl, wide(g_best, 4), ALU.subtract))
                dve.tensor_tensor(r_exp[:, :, 4], e_best2, e_best1, ALU.subtract).then_inc(ly.rexp_in, 1)
                p = full_of("rank")
                drain("rank", dve.tensor_copy(rank_s, p[:, 0:16]))
                bk.wait_drained(dve, "rank")
                ranks = rank_s[:, 0:12].rearrange("p (t g) -> p t g", t=3)
                sizes = rank_s[:, 12:16]
                base = cst[:, C_BASE:C_BASE + 4]
                link(dve.tensor_scalar(extra, sizes, 128.5, None, ALU.is_gt))
                link(dve.scalar_tensor_tensor(extra, sizes, 256.5, extra, ALU.is_gt, ALU.add))
                link(dve.tensor_tensor_scan(upto, extra, extra, 0.0, ALU.add, ALU.bypass))
                link(dve.tensor_tensor(before, upto, extra, ALU.subtract))
                link(dve.tensor_scalar(before, before, 128.0, 384.0, ALU.mult, ALU.add))
                dve.tensor_tensor(before, before, base, ALU.subtract)
                link(dve.tensor_tensor(ranks, ranks, oh_group, ALU.mult))
                link(dve.tensor_reduce(r_tmp, ranks, AX.X, ALU.add))
                link(dve.tensor_tensor(ranks, oh_group, before[:, None, :].broadcast_to((P, 3, 4)), ALU.mult))
                dve.tensor_reduce(r_tmp2, ranks, AX.X, ALU.add)
                link(dve.tensor_scalar(g_best, r_tmp, 127.5, None, ALU.is_gt))
                link(dve.tensor_tensor(r_tmp2, r_tmp2, g_best, ALU.mult))
                dve.tensor_tensor(r_tmp, r_tmp, r_tmp2, ALU.add)
                link(dve.tensor_tensor(ranks, oh_group, base[:, None, :].broadcast_to((P, 3, 4)), ALU.mult))
                link(dve.tensor_reduce(r_tmp2, ranks, AX.X, ALU.add))
                link(dve.tensor_tensor(slot_of, r_tmp, r_tmp2, ALU.add))

                def select():
                    for t in range(TILES):
                        ins = dve.tensor_scalar(sel[:, t, :], cst[:, C_IOTA:C_IOTA + P], slot_of[:, t:t + 1], None,
                                                ALU.is_equal)
                    return ins

                link(select())
                link(dve.tensor_scalar(slot_of, slot_of, -128.0, None, ALU.add))
                dve.wait_ge(ly.rexp_ready, 1)
                dve.tensor_reduce(r_tmp, r_exp[:, :, 0:4], AX.X, ALU.add)
                link(dve.tensor_scalar(r_tmp2, r_exp[:, :, 4], 1.0, None, ALU.add))
                link(dve.tensor_tensor(r_tmp, r_tmp, r_tmp2, ALU.mult))
                link(dve.reciprocal(r_tmp, r_tmp))
                link(dve.tensor_tensor(r_tmp2, r_tmp, r_exp[:, :, 4], ALU.mult))
                dve.tensor_tensor(one1, one1, wide(r_tmp, 16), ALU.mult)
                link(dve.tensor_tensor(one2, one2, wide(r_tmp2, 16), ALU.mult))
                link(dve.tensor_tensor(one1, one1, one2, ALU.add))
                dve.tensor_reduce(gates4, one1.rearrange("p t (g e) -> p t e g", g=4), AX.X, ALU.add
                                  ).then_inc(ly.sel_ready, 1)
                split_low(1)
                link(dve.tensor_scalar(jobs_f[:, 0:1], upto[:, 3:4], 4.0, None, ALU.add))
                for n in range(2):
                    link(dve.tensor_scalar(rank_s[:, 0:4], upto, n + 0.5, None, ALU.is_lt))
                    link(dve.tensor_reduce(jobs_f[:, 1 + n:2 + n], rank_s[:, 0:4], AX.X, ALU.add))
                link(dve.tensor_scalar(jobs_f[:, 1:3], jobs_f[:, 1:3], 3.0, None, ALU.min))
                dve.tensor_copy(jobs[:, 0:3], jobs_f[:, 0:3]).then_inc(ly.jobs_ready, 1)
                dve.wait_ge(ly.jobs_ready, 1)

                def gathered(names, job=None):
                    p = full_of(names[0], job)
                    drain(names[0], dve.tensor_copy(gslot[:], p[:, 0:4]))
                    for x in range(2):
                        dve.wait_ge(ly.xg_high_ready, x + 1 if job is None else job * 2 + x + 3)
                        p = full_of(names[1 + x], job)
                        of_half = slice(4 * x, 4 * x + 4)
                        drain(names[1 + x], dve.tensor_tensor(
                            xg_low[:, of_half, :], p[:, :].rearrange("p (k n) -> p k n", k=4),
                            xg_high[:, of_half, :].bitcast(F32), ALU.subtract))

                gathered(("gs0", ("xg0", 0), ("xg0", 1)))
                bk.wait_drained(dve, "gs0")
                split_low(2)
                count = dve.value_load(jobs[0:1, 0:1], min_val=4, max_val=6)
                with dve.Fori(0, count) as job:
                    dve.sem_clear(job_chain)
                    steps_in_job = [0]

                    def step(ins):
                        steps_in_job[0] += 1
                        ins.then_inc(job_chain, 1)
                        dve.wait_ge(job_chain, steps_in_job[0])

                    def gated(e):
                        p = full_of(("U", e), job)
                        bk.wait_drained(dve, ("G", e), job)
                        step(dve.scalar_tensor_tensor(act_in[:, e % 2, :], p[:, :], gslot[:, e:e + 1], sg[:, e % 2, :],
                                                      ALU.mult, ALU.mult))
                        dve.sem_inc(bk.drained[bk.bank(("U", e))], 1)
                        dve.sem_inc(ly.gated_ready, 1)

                    def hidden_low(e):
                        dve.wait_ge(ly.hidden_high_ready, job * 4 + e + 1)
                        p = full_of(("aT", e), job)
                        drain(("aT", e), dve.tensor_tensor(aT_low[:, e % 2, :], p[:, :],
                                                           aT_high[:, e % 2, :].bitcast(F32), ALU.subtract))

                    for i in range(HALVES):
                        if i + AHEAD < HALVES:
                            split_low(i + AHEAD, job)
                        if i in (3, 7, 11, 17):
                            gated((3, 7, 11, 17).index(i))
                        if i == 4:
                            bk.wait_full(dve, "selT", job)
                            step(select())
                            step(dve.tensor_scalar(slot_of, slot_of, -128.0, None, ALU.add))
                            dve.sem_inc(ly.sel_ready, 1)
                        if i in (8, 14, 19):
                            hidden_low((8, 14, 19).index(i))
                        if i == 19:
                            gathered(("gs", ("xg", 0), ("xg", 1)), job)
                            hidden_low(3)
                    with dve.If(count > job + 1):
                        split_low(HALVES, job)
                    p = full_of(("y", 1), job)
                    drain(("y", 1), dve.tensor_copy(ysb[:, 512:1024], p[:, :]))
                    for m in range(3):
                        residual(("back", m), 40, m, full_of(("back", m), job))
                    with dve.If(count > job + 1):
                        split_low(HALVES + 1, job)
                    for m in range(3, KT):
                        residual(("back", m), 40, m, full_of(("back", m), job))
                    with dve.If(count > job + 1):
                        split_low(HALVES + 2, job)
                    bk.wait_drained(dve, ("back", KT - 1), job)
                dve.sem_inc(ly.x_done, 1)

            dve.wait_ge(fin_root, 1)
            dve.reciprocal(std[:], std[:]).then_inc(fin_root, 1)
            dve.wait_ge(fin_root, 2)
            for k in range(KT):
                dve.scalar_tensor_tensor(hT[:, k, :], xT[:, k, :], vT[:, 0, V_FINAL + k:V_FINAL + k + 1], std[:],
                                         ALU.mult, ALU.mult).then_inc(fin_scaled, 1)
            for t in range(TILES):
                dve.wait_ge(fin_turned, 2 * t + 1)
                dve.tensor_copy(fin_rows[:, t, 0:512], ps[1 + 2 * t][:, :]).then_inc(fin_copied, 1)


_OUTS = {
    "y_prompt": (1, 128, 1024), "y_sample": (1, 256, 1024),
    "new_cache_k": (1, 2, 128, 4, 64), "new_cache_v": (1, 2, 128, 4, 64),
    "new_state_C": (1, 2, 2, 4, 128, 128), "new_state_n": (1, 2, 2, 4, 128), "new_state_m": (1, 2, 2, 4),
}


def kernel(**inputs):
    import concourse.bacc as bacc
    from concourse.bass_utils import run_bass_kernel_spmd as run

    nc = bacc.Bacc("TRN2", target_bir_lowering=False, num_devices=1)
    arrays, a, o = {}, {}, {}
    for name, value in {**inputs, "constants": constant_table()}.items():
        value = np.ascontiguousarray(value)
        arrays[f"in_{name}"] = value
        a[name] = nc.dram_tensor(f"in_{name}", value.shape, mybir.dt.from_np(value.dtype), kind="ExternalInput").ap()
    for name, shape in _OUTS.items():
        o[name] = nc.dram_tensor(f"out_{name}", shape, F32, kind="ExternalOutput").ap()
    build(nc, a, o)
    r = run(nc, [arrays], core_ids=[0])
    return tuple(r.results[0][f"out_{name}"] for name in _OUTS)
```
